# Optimizing a Trainium2 kernel written in Bass

```python
import jax, jax.numpy as jnp
from jax import lax
import numpy as np

D_MODEL = 1024
BATCH = 1
SEQ = 512
DEPTH = 1

MEM_LEN = 256
FOX_HEADS = 8
FOX_HEAD_DIM = 64
DSA_HEADS = 8
DSA_HEAD_DIM = 64
IDX_HEADS = 8
IDX_DIM = 64
MEM_HEADS = 4
MEM_HEAD_DIM = 128
BRANCH_WIDTH = 512
N_BRANCHES = 3
D_FF = 2816
ROPE_THETA = 10000.0
Q_BLOCK = 128
TOPK_MAX = 256
EPS = 1e-6

SPLIT_SIZES = (
    BRANCH_WIDTH, BRANCH_WIDTH, BRANCH_WIDTH,
    FOX_HEADS,
    BRANCH_WIDTH, DSA_HEAD_DIM, DSA_HEAD_DIM,
    IDX_HEADS * IDX_DIM, IDX_DIM, IDX_HEADS,
    BRANCH_WIDTH,
    N_BRANCHES * D_MODEL,
)
SPLIT_POINTS = tuple(int(v) for v in np.cumsum(SPLIT_SIZES)[:-1])
D_IN = int(sum(SPLIT_SIZES))


def rmsnorm(x, g):
    xf = x.astype(jnp.float32)
    y = xf * lax.rsqrt(jnp.mean(xf * xf, axis=-1, keepdims=True) + EPS)
    return (y * g.astype(jnp.float32)).astype(x.dtype)

def swiglu(x, w_gate, w_up, w_down):
    return (jax.nn.silu(x @ w_gate) * (x @ w_up)) @ w_down

def rope_tables(positions, dim, dtype):
    inv_freq = ROPE_THETA ** (-jnp.arange(0, dim, 2, dtype=jnp.float32) / dim)
    ang = positions.astype(jnp.float32)[..., None] * inv_freq
    return jnp.cos(ang)[:, :, None, :].astype(dtype), jnp.sin(ang)[:, :, None, :].astype(dtype)

def rope(x, cos, sin):
    x1, x2 = jnp.split(x, 2, axis=-1)
    return jnp.concatenate([x1 * cos - x2 * sin, x2 * cos + x1 * sin], axis=-1)

def to_blocks(a):
    B, S = a.shape[:2]
    return a.reshape((B, S // Q_BLOCK, Q_BLOCK) + a.shape[2:]).swapaxes(0, 1)

def from_blocks(a):
    nb, B, Q = a.shape[:3]
    return a.swapaxes(0, 1).reshape((B, nb * Q) + a.shape[3:])

def fox_attention(q, k, v, logf):
    B, S, H, hd = q.shape
    c = jnp.cumsum(logf, axis=1)
    c_keys = c.transpose(0, 2, 1)
    key_pos = jnp.arange(S)
    scale = hd ** -0.5

    def block(args):
        qi, ci, bi = args
        qpos = bi * Q_BLOCK + jnp.arange(Q_BLOCK)
        s = jnp.einsum('bqhd,bkhd->bhqk', qi, k).astype(jnp.float32) * scale
        s = s + ci.transpose(0, 2, 1)[..., None] - c_keys[:, :, None, :]
        s = jnp.where(key_pos[None, :] <= qpos[:, None], s, -jnp.inf)
        p = jax.nn.softmax(s, axis=-1)
        return jnp.einsum('bhqk,bkhd->bqhd', p.astype(v.dtype), v)

    out = lax.map(block, (to_blocks(q), to_blocks(c), jnp.arange(S // Q_BLOCK)))
    return from_blocks(out).reshape(B, S, H * hd)

def dsa_attention(q, k, v, iq, ik, iw, k_sel):
    B, S, H, hd = q.shape
    key_pos = jnp.arange(S)
    scale = hd ** -0.5
    gather = jax.vmap(lambda a, i: a[i])

    def block(args):
        qi, iqi, iwi, bi = args
        qpos = bi * Q_BLOCK + jnp.arange(Q_BLOCK)
        sc = jnp.einsum('bqhd,bkd->bqhk', iqi, ik).astype(jnp.float32)
        score = jnp.einsum('bqh,bqhk->bqk', iwi.astype(jnp.float32), jax.nn.relu(sc))
        score = jnp.where((key_pos[None, :] <= qpos[:, None])[None], score, -jnp.inf)
        _, idx = lax.top_k(score, k_sel)
        valid = idx <= qpos[None, :, None]
        ks = gather(k, idx)
        vs = gather(v, idx)
        s = jnp.einsum('bqhd,bqkd->bqhk', qi, ks).astype(jnp.float32) * scale
        s = jnp.where(valid[:, :, None, :], s, -jnp.inf)
        p = jax.nn.softmax(s, axis=-1)
        return jnp.einsum('bqhk,bqkd->bqhd', p.astype(vs.dtype), vs)

    out = lax.map(block, (to_blocks(q), to_blocks(iq), to_blocks(iw), jnp.arange(S // Q_BLOCK)))
    return from_blocks(out).reshape(B, S, H * hd)

def memory_attention(q, km, vm):
    B, S, H, hd = q.shape
    s = jnp.einsum('bshd,bmhd->bhsm', q, km).astype(jnp.float32) * hd ** -0.5
    p = jax.nn.softmax(s, axis=-1)
    return jnp.einsum('bhsm,bmhd->bshd', p.astype(vm.dtype), vm).reshape(B, S, H * hd)

def first_inputs(seed: int = 0) -> dict:
    key = jax.random.key(seed)
    ks = jax.random.split(key, 24)
    f32 = jnp.float32

    def w(k, shape, fan_in):
        return jax.random.normal(k, shape, f32) * fan_in ** -0.5

    def gain(k, shape):
        return 1.0 + 0.02 * jax.random.normal(k, shape, f32)

    L = DEPTH
    return {
        "x": jax.random.normal(ks[0], (BATCH, SEQ, D_MODEL), f32),
        "mem": jax.random.normal(ks[1], (BATCH, MEM_LEN, D_MODEL), f32),
        "positions": jnp.broadcast_to(jnp.arange(SEQ, dtype=jnp.int32), (BATCH, SEQ)),
        "ffn1_norm": gain(ks[2], (L, D_MODEL)),
        "ffn1_w_gate": w(ks[3], (L, D_MODEL, D_FF), D_MODEL),
        "ffn1_w_up": w(ks[4], (L, D_MODEL, D_FF), D_MODEL),
        "ffn1_w_down": w(ks[5], (L, D_FF, D_MODEL), D_FF),
        "mix_norm": gain(ks[6], (L, D_MODEL)),
        "mem_norm": gain(ks[7], (L, D_MODEL)),
        "w_in": w(ks[8], (L, D_MODEL, D_IN), D_MODEL),
        "b_forget": 3.0 + 0.5 * jax.random.normal(ks[9], (L, FOX_HEADS), f32),
        "fox_q_norm": gain(ks[10], (L, FOX_HEAD_DIM)),
        "fox_k_norm": gain(ks[11], (L, FOX_HEAD_DIM)),
        "dsa_q_norm": gain(ks[12], (L, DSA_HEAD_DIM)),
        "dsa_k_norm": gain(ks[13], (L, DSA_HEAD_DIM)),
        "mem_q_norm": gain(ks[14], (L, MEM_HEAD_DIM)),
        "mem_k_norm": gain(ks[15], (L, MEM_HEAD_DIM)),
        "w_mem_kv": w(ks[16], (L, D_MODEL, 2 * BRANCH_WIDTH), D_MODEL),
        "w_branch": w(ks[17], (L, N_BRANCHES, BRANCH_WIDTH, D_MODEL), BRANCH_WIDTH),
        "w_out": w(ks[18], (L, D_MODEL, D_MODEL), D_MODEL),
        "ffn2_norm": gain(ks[19], (L, D_MODEL)),
        "ffn2_w_gate": w(ks[20], (L, D_MODEL, D_FF), D_MODEL),
        "ffn2_w_up": w(ks[21], (L, D_MODEL, D_FF), D_MODEL),
        "ffn2_w_down": w(ks[22], (L, D_FF, D_MODEL), D_FF),
    }

def first_block(x, mem, positions, ffn1_norm, ffn1_w_gate, ffn1_w_up, ffn1_w_down, mix_norm,
              mem_norm, w_in, b_forget, fox_q_norm, fox_k_norm, dsa_q_norm, dsa_k_norm,
              mem_q_norm, mem_k_norm, w_mem_kv, w_branch, w_out, ffn2_norm, ffn2_w_gate,
              ffn2_w_up, ffn2_w_down):
    B, S, D = x.shape
    M = mem.shape[1]
    k_sel = min(TOPK_MAX, S // 4)
    cos, sin = rope_tables(positions, DSA_HEAD_DIM, x.dtype)
    cos_i, sin_i = rope_tables(positions, IDX_DIM, x.dtype)
    h = x
    for l in range(DEPTH):
        h = h + 0.5 * swiglu(rmsnorm(h, ffn1_norm[l]), ffn1_w_gate[l], ffn1_w_up[l], ffn1_w_down[l])

        u = rmsnorm(h, mix_norm[l])
        (fq, fk, fv, ff, dq, dk, dv, iq, ik, iw, mq, g) = jnp.split(u @ w_in[l], SPLIT_POINTS, axis=-1)

        fq = rmsnorm(fq.reshape(B, S, FOX_HEADS, FOX_HEAD_DIM), fox_q_norm[l])
        fk = rmsnorm(fk.reshape(B, S, FOX_HEADS, FOX_HEAD_DIM), fox_k_norm[l])
        fv = fv.reshape(B, S, FOX_HEADS, FOX_HEAD_DIM)
        logf = jax.nn.log_sigmoid(ff.astype(jnp.float32) + b_forget[l].astype(jnp.float32))
        o_a = fox_attention(fq, fk, fv, logf)

        dq = rope(rmsnorm(dq.reshape(B, S, DSA_HEADS, DSA_HEAD_DIM), dsa_q_norm[l]), cos, sin)
        dk = rope(rmsnorm(dk[:, :, None, :], dsa_k_norm[l]), cos, sin)[:, :, 0, :]
        iq = rope(iq.reshape(B, S, IDX_HEADS, IDX_DIM), cos_i, sin_i)
        ik = rope(ik[:, :, None, :], cos_i, sin_i)[:, :, 0, :]
        iw = iw * (IDX_HEADS ** -0.5 * IDX_DIM ** -0.5)
        o_b = dsa_attention(dq, dk, dv, iq, ik, iw, k_sel)

        km, vm = jnp.split(rmsnorm(mem, mem_norm[l]) @ w_mem_kv[l], 2, axis=-1)
        km = rmsnorm(km.reshape(B, M, MEM_HEADS, MEM_HEAD_DIM), mem_k_norm[l])
        vm = vm.reshape(B, M, MEM_HEADS, MEM_HEAD_DIM)
        mq = rmsnorm(mq.reshape(B, S, MEM_HEADS, MEM_HEAD_DIM), mem_q_norm[l])
        o_c = memory_attention(mq, km, vm)

        branches = jnp.stack([o_a, o_b, o_c], axis=2)
        proj = jnp.einsum('bsnw,nwd->bsnd', branches, w_branch[l])
        gates = jax.nn.sigmoid(g.reshape(B, S, N_BRANCHES, D))
        h = h + jnp.sum(gates * proj, axis=2) @ w_out[l]

        h = h + 0.5 * swiglu(rmsnorm(h, ffn2_norm[l]), ffn2_w_gate[l], ffn2_w_up[l], ffn2_w_down[l])
    return h


D_MIX = D_MODEL
C_CONV = D_MIX // 2
C_POOL = D_MIX - C_CONV
CONV_HEADS = 8
CONV_WIDTH = 31
POOL_WINDOWS = (2, 4, 8, 16)
N_POOL_GROUPS = len(POOL_WINDOWS)
POOL_GROUP = C_POOL // N_POOL_GROUPS
D_IN_2 = 2 * C_CONV + C_POOL
D_FF_2 = ((8 * D_MODEL // 3 + 255) // 256) * 256
RMS_EPS = 1e-6
LN_EPS = 1e-5


def rmsnorm_2(x, g):
    xf = x.astype(jnp.float32)
    y = xf * lax.rsqrt(jnp.mean(xf * xf, axis=-1, keepdims=True) + RMS_EPS)
    return (y * g.astype(jnp.float32)).astype(x.dtype)

def layernorm(x, g, b):
    xf = x.astype(jnp.float32)
    mu = jnp.mean(xf, axis=-1, keepdims=True)
    var = jnp.mean(jnp.square(xf - mu), axis=-1, keepdims=True)
    y = (xf - mu) * lax.rsqrt(var + LN_EPS)
    return (y * g.astype(jnp.float32) + b.astype(jnp.float32)).astype(x.dtype)

def conformer_conv_group(a, gate, w_dw, b_dw, ln_g, ln_b):
    u = a * jax.nn.sigmoid(gate)
    k = w_dw.astype(u.dtype)[:, None, :]
    v = lax.conv_general_dilated(
        u, k, window_strides=(1,), padding=[(CONV_WIDTH - 1, 0)],
        dimension_numbers=("NWC", "WIO", "NWC"),
        feature_group_count=C_CONV) + b_dw.astype(u.dtype)
    v = layernorm(v, ln_g, ln_b)
    return jax.nn.silu(v)

def multiscale_pool_group(p, w_pool, s_pool):
    seq = p.shape[1]
    pos = jnp.arange(seq)
    outs = []
    for i, w in enumerate(POOL_WINDOWS):
        seg = p[..., i * POOL_GROUP:(i + 1) * POOL_GROUP].astype(jnp.float32)
        cs = jnp.cumsum(seg, axis=1)
        lag = jnp.pad(cs, ((0, 0), (w, 0), (0, 0)))[:, :seq]
        cnt = jnp.minimum(pos + 1, w).astype(jnp.float32)[None, :, None]
        y = ((cs - lag) / cnt - seg).astype(p.dtype)
        outs.append(jnp.einsum("bsg,gh->bsh", y, w_pool[i]))
    return jnp.concatenate(outs, axis=-1) * s_pool

def swiglu_2(x, w_gate, w_up, w_down):
    return (jax.nn.silu(x @ w_gate) * (x @ w_up)) @ w_down

def second_inputs(seed: int = 0) -> dict:
    key = jax.random.key(seed)
    ks = jax.random.split(key, 20)
    f = jnp.float32
    n = lambda k, s, sc: jax.random.normal(k, s, f) * sc
    return {
        "x": jax.random.normal(ks[0], (BATCH, SEQ, D_MODEL), f),
        "g_mix": 1.0 + n(ks[1], (DEPTH, D_MODEL), 0.05),
        "w_in": n(ks[2], (DEPTH, D_MODEL, D_IN_2), D_MODEL ** -0.5),
        "b_in": n(ks[3], (DEPTH, D_IN_2), 0.02),
        "w_dw": n(ks[4], (DEPTH, CONV_WIDTH, C_CONV), CONV_WIDTH ** -0.5),
        "b_dw": n(ks[5], (DEPTH, C_CONV), 0.02),
        "ln_g": 1.0 + n(ks[6], (DEPTH, C_CONV), 0.05),
        "ln_b": n(ks[7], (DEPTH, C_CONV), 0.02),
        "w_pool": n(ks[8], (DEPTH, N_POOL_GROUPS, POOL_GROUP, POOL_GROUP), POOL_GROUP ** -0.5),
        "s_pool": 1.0 + n(ks[9], (DEPTH, C_POOL), 0.1),
        "w_out": n(ks[10], (DEPTH, D_MIX, D_MODEL), D_MIX ** -0.5),
        "g_ffn": 1.0 + n(ks[11], (DEPTH, D_MODEL), 0.05),
        "w_gate": n(ks[12], (DEPTH, D_MODEL, D_FF_2), D_MODEL ** -0.5),
        "w_up": n(ks[13], (DEPTH, D_MODEL, D_FF_2), D_MODEL ** -0.5),
        "w_down": n(ks[14], (DEPTH, D_FF_2, D_MODEL), D_FF_2 ** -0.5),
        "g_final": 1.0 + n(ks[15], (D_MODEL,), 0.05),
    }

def second_block(x, g_mix, w_in, b_in, w_dw, b_dw, ln_g, ln_b, w_pool, s_pool,
              w_out, g_ffn, w_gate, w_up, w_down, g_final):
    h = x
    for l in range(DEPTH):
        xn = rmsnorm_2(h, g_mix[l])
        z = xn @ w_in[l] + b_in[l]
        a = z[..., :C_CONV]
        gate = z[..., C_CONV:2 * C_CONV]
        p = z[..., 2 * C_CONV:]
        y_conv = conformer_conv_group(a, gate, w_dw[l], b_dw[l], ln_g[l], ln_b[l])
        y_pool = multiscale_pool_group(p, w_pool[l], s_pool[l])
        y = jnp.concatenate([y_conv, y_pool], axis=-1)
        h = h + y @ w_out[l]
        h = h + swiglu_2(rmsnorm_2(h, g_ffn[l]), w_gate[l], w_up[l], w_down[l])
    return rmsnorm_2(h, g_final)


def setup_inputs(seed=0):
    out = dict(first_inputs(seed))
    for name, value in second_inputs(seed + 1).items():
        if name != "x":
            out[name + "_2"] = value
    return out


def reference(
    x, mem, positions, ffn1_norm, ffn1_w_gate, ffn1_w_up, ffn1_w_down, mix_norm, mem_norm, w_in,
    b_forget, fox_q_norm, fox_k_norm, dsa_q_norm, dsa_k_norm, mem_q_norm, mem_k_norm, w_mem_kv,
    w_branch, w_out, ffn2_norm, ffn2_w_gate, ffn2_w_up, ffn2_w_down, g_mix_2, w_in_2, b_in_2,
    w_dw_2, b_dw_2, ln_g_2, ln_b_2, w_pool_2, s_pool_2, w_out_2, g_ffn_2, w_gate_2, w_up_2,
    w_down_2, g_final_2,
):
    x = first_block(
        x, mem, positions, ffn1_norm, ffn1_w_gate, ffn1_w_up, ffn1_w_down, mix_norm, mem_norm,
        w_in, b_forget, fox_q_norm, fox_k_norm, dsa_q_norm, dsa_k_norm, mem_q_norm, mem_k_norm,
        w_mem_kv, w_branch, w_out, ffn2_norm, ffn2_w_gate, ffn2_w_up, ffn2_w_down,
    )
    return second_block(
        x, g_mix_2, w_in_2, b_in_2, w_dw_2, b_dw_2, ln_g_2, ln_b_2, w_pool_2, s_pool_2, w_out_2,
        g_ffn_2, w_gate_2, w_up_2, w_down_2, g_final_2,
    )


_drawn_inputs = setup_inputs


def setup_inputs(seed=0):
    import zlib

    import numpy as np

    out = dict(_drawn_inputs(seed))
    spreads = {}
    factors = {'ffn1_norm': 4.72,
     'mix_norm': 4.511,
     'mem_norm': 8.0,
     'fox_q_norm': 8.0,
     'fox_k_norm': 8.0,
     'dsa_q_norm': 8.0,
     'dsa_k_norm': 8.0,
     'mem_q_norm': 8.0,
     'mem_k_norm': 8.0,
     'ffn2_norm': 6.614,
     'b_in_2': 38.186,
     'b_dw_2': 20.163,
     'ln_g_2': 84.683,
     'ln_b_2': 200.0,
     'g_mix_2': 8.0,
     's_pool_2': 8.0,
     'g_ffn_2': 8.0}
    for name, (base, spread) in spreads.items():
        noise = np.random.default_rng([zlib.crc32(name.encode()), seed]).standard_normal(out[name].shape)
        drawn = base * np.exp(spread * noise) if base else spread * noise
        out[name] = __import__('jax').numpy.asarray(drawn.astype(out[name].dtype))
    for name, factor in factors.items():
        out[name] = (out[name] * factor).astype(out[name].dtype)
    return out
```

```python
from contextlib import ExitStack

import numpy as np

import concourse.bass as bass
from concourse import mybir

ALU = mybir.AluOpType
ACT = mybir.ActivationFunctionType
F32 = mybir.dt.float32
F32R = mybir.dt.float32r
I32 = mybir.dt.int32

P = 128
D = 1024
S = 512
MEM = 256
DK = D // P
BW = 512
BK = BW // P
HEADS = 8
HD = 64
MHEADS = 4
FF = 2816
FC = FF // P
QB = S // P
TOPK = min(256, S // 4)
TAPS = 31
WINDOWS = (2, 4, 8, 16)
PADW = WINDOWS[-1]
EPS = 1e-6
LN_EPS = 1e-5
MASKED = -1.0e30
TAKEN = -3.0e38
TURN_RAD = float(2 * np.pi)
TURN_PARTS = (6.28125, 0.0019378662109375, -2.562999725341797e-06, 3.968374517882012e-09)
ROUNDER = 1.5 * 2.0 ** 23
PI_BELOW = 3.1415925
RAW = 4
SPL = 2

N_MEM, N_GU, N_DN, N_IN, N_BR, N_WO, N_IN2, N_WO2 = 8, 2 * FC, FC, 50, 12, 8, 12, 8
U_MEM = 0
U_GU1 = U_MEM + N_MEM
U_DN1 = U_GU1 + N_GU
U_IN = U_DN1 + N_DN
U_BR = U_IN + N_IN
U_WO = U_BR + N_BR
U_GU2 = U_WO + N_WO
U_DN2 = U_GU2 + N_GU
U_IN2 = U_DN2 + N_DN
U_WO2 = U_IN2 + N_IN2
U_GU3 = U_WO2 + N_WO2
U_DN3 = U_GU3 + N_GU
UNITS = U_DN3 + N_DN

VEC_COLS = {}
for _name, _n in (("ffn1_norm", 8), ("mix_norm", 8), ("mem_norm", 8), ("ffn2_norm", 8), ("g_mix_2", 8),
                  ("g_ffn_2", 8), ("g_final_2", 8), ("fox_q_norm", 1), ("fox_k_norm", 1), ("dsa_q_norm", 1),
                  ("dsa_k_norm", 1), ("mem_q_norm", 1), ("mem_k_norm", 1), ("b_forget", HEADS), ("b_in_2", 12),
                  ("w_dw_2", 4 * TAPS), ("b_dw_2", 4), ("ln_g_2", 4), ("ln_b_2", 4), ("s_pool_2", 4),
                  ("inv_freq", 1), ("pool_inv", len(WINDOWS) * PADW)):
    VEC_COLS[_name] = (sum(n for _, n in VEC_COLS.values()), _n)
NV = sum(n for _, n in VEC_COLS.values())

IN_KINDS = (["ik"] + ["iq"] * 4 + ["fq"] * 4 + ["fk"] * 4 + ["fv"] * 4 + ["dk"] + ["dq"] * 4 + ["mq"] * 4)
GATES = 3 * DK
IN_STEPS = IN_KINDS
MEM_STEPS = ["km"] * 4 + ["vm"] * 4
IN2_STEPS = ["a", "s"] * 4 + ["p"] * 4

ITEMS = ([("idx", h, q, (q + 1) * P) for q in range(1, QB) for h in range(HEADS)]
         + [("fox", h, q, (q + 1) * P) for h in range(HEADS) for q in range(QB)]
         + [("dsa", h, q, (q + 1) * P) for h in range(HEADS) for q in range(QB)]
         + [("mem", h, q, MEM) for h in range(MHEADS) for q in range(QB)])
N_IDX = sum(it[0] == "idx" for it in ITEMS)
FILL = 6
ROUNDS = TOPK // 8


def build(nc, T):
    ctx = ExitStack()
    with ctx:
        base = [16512]

        def at(name, shape, dt, offset=None):
            size = int(np.prod(shape[1:])) * 4
            if offset is None:
                offset = base[0]
                base[0] += size + (-size) % 32
            return nc.alloc_sbuf_tensor_at(name, shape, dt, offset=offset)

        raw = at("raw_weights", [P, RAW, DK * P], F32)
        wh = at("weights_high", [P, SPL, DK * P], F32R)
        wl = at("weights_low", [P, SPL, DK * P], F32R)
        h = at("residual", [P, DK, S], F32)
        x_at = base[0]
        xh = at("input_high", [P, DK, S], F32R)
        xl = at("input_low", [P, DK, S], F32R)
        big = base[0]
        base[0] += 2 * FC * S * 4
        hh = at("hidden_high", [P, FC, S], F32R, big)
        hl = at("hidden_low", [P, FC, S], F32R, big + FC * S * 4)
        K2 = S * 4
        fq = at("fox_q", [P, 4, S], F32, big)
        kd = at("dsa_k", [P, S], F32, big + 4 * K2)
        fv = at("fox_v", [P, QB, BW], F32, big + 5 * K2)
        fk = at("fox_k", [P, 4, S], F32, big + 9 * K2)
        iq = at("idx_q", [P, 4, S], F32, big + 13 * K2)
        ki = at("idx_k", [P, S], F32, big + 17 * K2)
        dq = at("dsa_q", [P, 4, S], F32, big + 18 * K2)
        mq = at("mem_q", [P, 4, S], F32, big + 22 * K2)
        dv = at("dsa_v", [P, QB, HD], F32, big + 26 * K2)
        sel = at("top_keys", [P, 9 * P], F32, big + 26 * K2 + 1024)
        tri = at("triangle", [P, S], F32, big + 26 * K2 + 1024)
        gates_own = at("gates", [P, 15, S], F32, big + 29 * K2)
        gates_late = at("gates_late", [P, 4, S], F32, big + 13 * K2)
        gates_last = at("gates_last", [P, 4, S], F32, big + 9 * K2)
        gates_end = at("gates_end", [P, 1, S], F32, big + 8 * K2)
        och = at("mem_out_high", [P, 4, S], F32R, big)
        ocl = at("mem_out_low", [P, 4, S], F32R, big + 4 * K2)
        mgh = at("merged_high", [P, DK, S], F32R, big + 18 * K2)
        mgl = at("merged_low", [P, DK, S], F32R, big + 29 * K2)
        glu = at("glu_padded", [P, 4, TAPS - 1 + S], F32, big)
        conv = at("conv_out", [P, 4, S], F32, big + 5 * K2)
        pool_in = at("pool_in", [P, 4, PADW + S], F32, big + 9 * K2)
        psum_a = at("pool_sum_a", [P, PADW + S], F32, big + 14 * K2)
        psum_b = at("pool_sum_b", [P, PADW + S], F32, big + 16 * K2)
        pooled = at("pooled", [P, 4, S], F32, big + 18 * K2)
        ymix = at("mixed", [P, DK, S], F32, big + 22 * K2)
        sig = at("glu_gate", [P, 2, S], F32, big + 30 * K2)
        wpool = at("pool_weights", [P, 4, P], F32, big + 32 * K2)

        vec = at("vectors", [P, NV], F32)
        ident = at("identity", [P, P], F32)
        ones = at("ones", [P, P], F32)
        bd = at("ones_by_head", [P, P], F32)
        rot = at("rotate_halves", [P, P], F32)
        cmask = at("causal_mask", [P, S], F32)
        rstd = at("token_factor", [P, S], F32)
        cos = at("rope_cos", [P, S], F32)
        sin = at("rope_sin", [P, S], F32)
        km = at("mem_k", [P, 4, MEM], F32)
        vm = at("mem_v", [P, MEM // P, BW], F32)
        iw = at("idx_weights", [P, QB, HEADS], F32)
        eps = at("epsilons", [P, 4], F32)
        forget = at("log_forget", [P, 2, QB, HEADS], F32)
        mx8 = at("top8", [P, 8], F32)
        stat = at("softmax_stats", [P, 3, 4], F32)
        t_at = base[0]
        tiles = [at(f"tile{i}", [P, S], F32) for i in range(9)]
        assert base[0] <= 229368, base[0]

        def v(name, c=0):
            o = VEC_COLS[name][0] + c
            return vec[:, o:o + 1]

        def gate_slot(g):
            if g < 15:
                return gates_own[:, g, :]
            if g < 19:
                return gates_late[:, g - 15, :]
            return gates_last[:, g - 19, :] if g < 23 else gates_end[:, 0, :]

        mem_in = at("mem_in", [P, DK, MEM], F32, big)
        mem_h = at("mem_high", [P, DK, MEM], F32R, big + 4 * K2)
        mem_l = at("mem_low", [P, DK, MEM], F32R, big + 8 * K2)
        mem_rt = [at(f"mem_root{i}", [P, MEM], F32, big + (12 + i) * K2) for i in range(2)]
        mem_rstd = at("mem_token_factor", [P, MEM], F32, big + 14 * K2)
        pos = at("positions_in", [P, S], I32, big + 15 * K2)
        ang, turns, turns_raw = (at(f"angle{i}", [P, S], F32, big + (16 + i) * K2) for i in range(3))
        out_t = at("out_t", [P, DK, S], F32, x_at)

        sel_at = [None, 0, 2 * P, 5 * P]

        bank = [ctx.enter_context(nc.psum_tensor(f"bank{i}", [P, S], F32)) for i in range(8)]

        sems = {}

        def sem(name):
            if name not in sems:
                sems[name] = ctx.enter_context(nc.semaphore(name))
            return sems[name]

        raw_loaded = [sem(f"raw_loaded{i}") for i in range(RAW)]
        high_done, low_done, unit_done = sem("high_done"), sem("low_done"), sem("unit_done")

        sq_feed, rt_feed = tiles[6:8], tiles[8]
        soft, probs_t, fbias, gate_t, cum = tiles[3:5], tiles[5:7], tiles[0:2], tiles[7], tiles[8]

        NORM = ("fq", "fk", "dk", "dq", "mq", "km")
        ROPE = ("iq", "ik", "dq", "dk")
        TURN = ("fv", "vm", "ik", "dk")

        def upto_step(steps, kinds, j):
            return sum(k in kinds for k in steps[:j + 1])

        def chunk_of(steps, j):
            return steps[:j].count(steps[j])

        mem_cfg = ("mem", MEM_STEPS, U_MEM, MEM, mem_h, mem_l, mem_rstd, [t[:, 0:MEM] for t in tiles[3:5]],
                   [t[:, :] for t in mem_rt])
        in_cfg = ("in", IN_STEPS, U_IN, S, xh, xl, rstd, [t[:, :] for t in tiles[3:5]],
                  [t[:, :] for t in tiles[5:7]])

        def chunk_id(n):
            kind, hd = ITEMS[n][:2]
            return {"fox": hd // 2, "dsa": 4 + hd // 2, "mem": 8 + hd}[kind]

        def ends_chunk(n):
            return N_IDX <= n < len(ITEMS) and (n == len(ITEMS) - 1 or chunk_id(n) != chunk_id(n + 1))

        def chunk_home(c):
            return (fq, dq, mq)[c // 4][:, c % 4, :]

        def chunk_parts(c):
            return (och[:, c - 8, :], ocl[:, c - 8, :]) if c >= 8 else (xh[:, c, :], xl[:, c, :])

        SPLITS = {97: (0, 1), 98: (2, 3), 99: (4, 5), 100: (6, 7), 101: (8,), 102: (9,), 103: (10,), 107: (11,)}
        LAST = len(ITEMS) + 5
        SEARCH0 = HEADS

        def gate_unit(g):
            return U_IN + len(IN_STEPS) + g

        block = ctx.enter_context(nc.Block())

        @block.sync
        def _(sp):
            sp.dma_start(mem_in[:, :, :], T["mem_t"]).then_inc(sem("mem_loaded"), 16)
            sp.dma_start(vec[:, :], T["vectors"]).then_inc(sem("vectors_loaded"), 16)
            sp.dma_start(pos[:, :], T["positions"]).then_inc(sem("positions_loaded"), 16)
            for dst, src in ((ident, "identity"), (ones, "ones"), (bd, "ones_by_head"),
                             (rot, "rotate_halves"), (cmask, "causal_mask")):
                sp.dma_start(dst[:, :], T[src]).then_inc(sem("constants_loaded"), 16)
            for u in range(RAW):
                sp.dma_start(raw[:, u, :], T["weights"][u]).then_inc(raw_loaded[u], 16)
                if u == 1:
                    sp.dma_start(h[:, :, :], T["x_t"]).then_inc(sem("x_loaded"), 16)
            with sp.Fori(1, UNITS // RAW) as i:
                for s in range(RAW):
                    sp.wait_ge(low_done, i * RAW + (s - RAW + 1))
                    sp.dma_start(raw[:, s, :], T["weights"][bass.ds(i * RAW + s, 1)].rearrange("a p n -> p (a n)")
                                 ).then_inc(raw_loaded[s], 16)
            for m in range(DK):
                sp.wait_ge(sem("out_ready"), m + 1)
                sp.dma_start(T["out_t"][:, m, :], out_t[:, m, :]).then_inc(sem("out_stored"), 16)
            sp.wait_ge(sem("out_stored"), 16 * DK)

        @block.gpsimd
        def _(pool):
            with pool.Fori(0, UNITS // RAW) as i:
                for s in range(RAW):
                    pool.wait_ge(high_done, i * RAW + (s + 1))
                    pool.tensor_tensor(wl[:, s % SPL, :], raw[:, s, :], wh[:, s % SPL, :].bitcast(F32),
                                       ALU.subtract).then_inc(low_done, 1)

        @block.tensor
        def _(pe):
            def products(out, u, k, rh, rl, start, stop):
                w = slice(k * P, (k + 1) * P)
                pe.matmul(out, wh[:, u % SPL, w], rh, start=start, stop=False)
                pe.matmul(out, wl[:, u % SPL, w], rh, start=False, stop=False)
                return pe.matmul(out, wh[:, u % SPL, w], rl, start=False, stop=stop)

            def project(u, out, rh, rl, low_at, n=S):
                pe.wait_ge(low_done, low_at)
                for k in range(DK):
                    mm = products(out, u, k, rh[:, k, 0:n], rl[:, k, 0:n], k == 0, k == DK - 1)
                mm.then_inc(unit_done, 1)

            def spread_unit(name, u, rh, rl, low_at, first=False, last=False):
                pe.wait_ge(low_done, low_at)
                for m in range(DK):
                    mm = products(bank[(m + 4) % 8][:, :], u, m, rh, rl, first, last)
                    if last and m < DK - 1:
                        mm.then_inc(sem(f"{name}_gathered"), 1)
                mm.then_inc(unit_done, 1)

            def square_sum(name, m, out, n=S):
                pe.wait_ge(sem(f"{name}_square"), m + 1)
                pe.matmul(out, ones[:, :], sq_feed[m % 2][:, 0:n], start=(m == 0), stop=(m == DK - 1)
                          ).then_inc(sem(f"{name}_sum"), 1)

            def phase_start(name):
                for m in range(DK):
                    square_sum(name, m, bank[4][:, :])
                pe.wait_ge(sem(f"{name}_low"), DK)

            def gate_up(name, u0):
                with pe.Fori(0, FC // 2) as i:
                    for c in range(2):
                        pe.wait_ge(sem(f"{name}_banks"), i * 2 + (c + 1))
                        for g in range(2):
                            project(u0 + 2 * c + g, bank[2 * c + g][:, :], xh, xl, i * 4 + (u0 + 2 * c + g + 1))

            def down(name, feed, u0):
                pe.wait_ge(sem(f"{feed}_root"), 1)
                pe.wait_ge(sem(f"{name}_banks"), FC + 2)
                pe.wait_ge(sem(f"{name}_split"), FC)
                for f in range(2):
                    spread_unit(name, u0 + f, hh[:, f, :], hl[:, f, :], u0 + f + 1, first=(f == 0))
                with pe.Fori(0, (FC - 6) // 4) as i:
                    for c in range(4):
                        f = bass.ds(i * 4 + (c + 2), 1)
                        spread_unit(name, u0 + 2 + c, hh[:, f, :].rearrange("p a n -> p (a n)"),
                                    hl[:, f, :].rearrange("p a n -> p (a n)"), i * 4 + (u0 + c + 3))
                pe.wait_ge(sem(f"{name}_split"), FC + 1)
                for f in range(FC - 4, FC):
                    spread_unit(name, u0 + f, hh[:, f, :], hl[:, f, :], u0 + f + 1, last=(f == FC - 1))

            def stepped(cfg, extra=None):
                tag, steps, u0, n, rh, rl, _, sq, _ = cfg
                for j in range(len(steps) + 2):
                    if j < len(steps):
                        if j >= 2:
                            pe.wait_ge(sem(f"{tag}_taken"), j - 1)
                        project(u0 + j, bank[j % 2][:, 0:n], rh, rl, u0 + j + 1, n)
                    i = j - 1
                    if 0 <= i < len(steps) and steps[i] in NORM:
                        k = upto_step(steps, NORM, i)
                        pe.wait_ge(sem(f"{tag}_squared"), k)
                        if k > 1:
                            pe.wait_ge(sem(f"{tag}_rooted"), k - 1)
                        pe.matmul(bank[2][:, 0:n], (ones if steps[i] in ("mq", "km") else bd)[:, :],
                                  sq[(k - 1) % 2], start=True, stop=True).then_inc(sem(f"{tag}_summed"), 1)
                    if 0 <= i < len(steps) and steps[i] in TURN:
                        k = upto_step(steps, TURN, i)
                        pe.wait_ge(sem(f"{tag}_taken"), i + 1)
                        if k > 2:
                            pe.wait_ge(sem(f"{tag}_turned_out"), k - 2)
                        lo = HD if steps[i] in ("ik", "dk") else 0
                        for b in range(n // P):
                            mm = pe.transpose(bank[4 + k % 2][:, b * P:b * P + P - lo],
                                              tiles[i % 3][lo:P, b * P:(b + 1) * P], ident[lo:P, lo:P])
                        mm.then_inc(sem(f"{tag}_turned"), 1)
                    i = j - 2
                    if 0 <= i < len(steps) and steps[i] in ROPE:
                        k = upto_step(steps, ROPE, i)
                        pe.wait_ge(sem(f"{tag}_taken"), i + 1)
                        if steps[i] in NORM:
                            pe.wait_ge(sem(f"{tag}_normed"), upto_step(steps, NORM, i))
                        if k > 1:
                            pe.wait_ge(sem(f"{tag}_roped"), k - 1)
                        m = HD if steps[i] in ("dk", "ik") else P
                        pe.matmul(bank[3][0:m, 0:n], rot[0:m, 0:m], tiles[i % 3][0:m, :], start=True, stop=True
                                  ).then_inc(sem(f"{tag}_rotated"), 1)
                    if extra and j < len(steps):
                        extra(j)
                    if tag == "in" and j == 4:
                        pe.wait_ge(sem("forget_logs"), 1)
                        pe.wait_ge(sem("triangle_loaded"), 16)
                        for b in range(QB):
                            mm = pe.matmul(bank[6][0:HEADS, b * P:S], forget[:, 0, b, :], tri[:, 0:S - b * P],
                                           start=(b == 0), stop=(b == QB - 1))
                        mm.then_inc(sem("forget_summed"), 1)

            pe.wait_ge(sem("constants_loaded"), 16 * 5)
            for m in range(DK):
                square_sum("mem", m, bank[6][:, 0:MEM], MEM)
            pe.wait_ge(sem("mem_low"), DK)
            stepped(mem_cfg, lambda j: square_sum("ffn1", j, bank[7][:, :]))

            pe.wait_ge(sem("ffn1_low"), DK)
            gate_up("g1", U_GU1)
            pe.wait_ge(sem("mem_turned_out"), 4)
            down("g1", "ffn1", U_DN1)

            phase_start("mix")
            pe.wait_ge(sem("mix_root"), 1)
            stepped(in_cfg)

            def gate_products():
                for g in range(GATES):
                    u = gate_unit(g)
                    for k in range(DK):
                        for part in range(3):
                            if k == 0 and part == 0:
                                pe.wait_ge(low_done, u + 1)
                                if g >= 2:
                                    pe.wait_ge(sem("gates_taken"), g - 1)
                            w = slice(k * P, (k + 1) * P)
                            mm = pe.matmul(bank[g % 2][:, :], (wl if part == 1 else wh)[:, u % SPL, w],
                                           (xl if part == 2 else xh)[:, k, :],
                                           start=(k == 0 and part == 0), stop=(k == DK - 1 and part == 2))
                            if k == DK - 1 and part == 2:
                                mm.then_inc(unit_done, 1)
                            yield

            filler = gate_products()

            def fill(n):
                for _ in range(n):
                    next(filler, None)

            def scores(n):
                kind, hd, q, ext = ITEMS[n]
                lo = HD * (hd % 2)
                if kind == "mem":
                    left, right = mq[:, hd, q * P:(q + 1) * P], km[:, hd, 0:MEM]
                else:
                    a = {"idx": iq, "fox": fq, "dsa": dq}[kind]
                    left = a[lo:lo + HD, hd // 2, q * P:(q + 1) * P]
                    right = (fk[lo:lo + HD, hd // 2, 0:ext] if kind == "fox"
                             else (ki if kind == "idx" else kd)[lo:lo + HD, 0:ext])
                if 2 <= n < N_IDX + 2:
                    pe.wait_ge(sem("relu_done"), n - 1)
                elif n >= N_IDX + 2:
                    pe.wait_ge(sem("shifted"), n - 1 - N_IDX)
                mm = pe.matmul(bank[3 + n % 2][:, 0:ext], left, right, start=True, stop=(kind != "fox"))
                if kind == "fox":
                    mm = pe.matmul(bank[3 + n % 2][:, ext - P:ext], ident[:, :], cmask[:, S - P:S],
                                   start=False, stop=True)
                mm.then_inc(sem("scores"), 1)

            def fox_bias(hd):
                if hd:
                    pe.wait_ge(sem("bias_out"), hd)
                pe.matmul(bank[2][:, :], ident[0:HEADS, hd:hd + 1].to_broadcast([HEADS, P]), cum[0:HEADS, :],
                          start=True, stop=True).then_inc(sem("bias"), 1)

            def turn(n):
                s = n - N_IDX
                pe.wait_ge(sem("probs"), s + 1)
                if s >= 2:
                    pe.wait_ge(sem("turned_out"), s - 1)
                for b in range(ITEMS[n][3] // P):
                    mm = pe.transpose(bank[5 + s % 2][:, b * P:(b + 1) * P], soft[n % 2][:, b * P:(b + 1) * P],
                                      ident[:, :])
                mm.then_inc(sem("turned"), 1)

            def weigh(n):
                kind, hd, q, ext = ITEMS[n]
                s = n - N_IDX
                pe.wait_ge(sem("turned_out"), s + 1)
                if chunk_id(n):
                    pe.wait_ge(sem("heads_out"), chunk_id(n))
                lo, hi = (0, P) if kind == "mem" else (HD * (hd % 2), HD * (hd % 2) + HD)
                for b in range(ext // P):
                    val = {"fox": lambda: fv[:, b, hd * HD:(hd + 1) * HD], "dsa": lambda: dv[:, b, :],
                           "mem": lambda: vm[:, b, hd * P:(hd + 1) * P]}[kind]()
                    mm = pe.matmul(bank[7][lo:hi, q * P:(q + 1) * P], val, probs_t[s % 2][:, b * P:(b + 1) * P],
                                   start=(b == 0), stop=(b == ext // P - 1))
                mm.then_inc(sem("weighed"), 1)

            pe.wait_ge(sem("in_taken"), len(IN_STEPS))
            pe.wait_ge(sem("in_normed"), upto_step(IN_STEPS, NORM, 99))
            pe.wait_ge(sem("in_roped"), upto_step(IN_STEPS, ROPE, 99))
            pe.wait_ge(sem("in_turned_out"), upto_step(IN_STEPS, TURN, 99))
            pe.wait_ge(sem("shared_keys"), 32)
            for n in range(len(ITEMS) + 2):
                if n < len(ITEMS):
                    kind, hd, q, _ = ITEMS[n]
                    if n == N_IDX:
                        pe.wait_ge(sem("forget_out"), 1)
                        fox_bias(0)
                    if kind == "fox" and q == 2 and hd < HEADS - 1:
                        fox_bias(hd + 1)
                    scores(n)
                fill(FILL // 2)
                if N_IDX <= n - 1 < len(ITEMS):
                    turn(n - 1)
                fill(FILL // 2)
                if n - 2 >= N_IDX:
                    weigh(n - 2)
            for _ in filler:
                pass

            pe.wait_ge(sem("shifted"), len(ITEMS) - N_IDX)
            pe.wait_ge(sem("turned_out"), len(ITEMS) - N_IDX)
            pe.wait_ge(sem("gates_taken"), GATES)
            for m in range(DK):
                for n in range(3):
                    if n == 0 and m >= 2:
                        pe.wait_ge(sem("branches_read"), m - 1)
                    for k in range(BK):
                        b = (m * 3 + n) * BK + k
                        if b % DK == 0:
                            pe.wait_ge(low_done, U_BR + b // DK + 1)
                        if m == 0:
                            pe.wait_ge(sem("out_split"), n * BK + k + 1)
                        rh, rl, o = ((xh, xl, 0), (xh, xl, 4), (och, ocl, 0))[n]
                        mm = products(bank[3 * (m % 2) + n][:, :], U_BR + b // DK, b % DK,
                                      rh[:, o + k, :], rl[:, o + k, :], k == 0, k == BK - 1)
                        if b % DK == DK - 1:
                            mm.then_inc(unit_done, 1)
                        elif n == 2 and k == BK - 1:
                            mm.then_inc(sem("branches_even"), 1)
            pe.wait_ge(sem("branches_read"), DK)
            for f in range(N_WO):
                pe.wait_ge(sem("merged_low"), f + 1)
                spread_unit("wo", U_WO + f, mgh[:, f, :], mgl[:, f, :], U_WO + f + 1, first=(f == 0),
                            last=(f == N_WO - 1))

            phase_start("ffn2")
            gate_up("g2", U_GU2)
            down("g2", "ffn2", U_DN2)

            phase_start("mix2")
            pe.wait_ge(sem("mix2_root"), 1)
            for j in range(len(IN2_STEPS)):
                if j >= 2:
                    pe.wait_ge(sem("in2_taken"), j - 1)
                project(U_IN2 + j, bank[j % 2][:, :], xh, xl, U_IN2 + j + 1)
            pe.wait_ge(sem("in2_taken"), len(IN2_STEPS))
            pe.wait_ge(sem("pool_weights_loaded"), 16)
            for g in range(len(WINDOWS)):
                pe.wait_ge(sem("pooled"), g + 1)
                pe.matmul(bank[2 + g][:, :], wpool[:, g, :], pooled[:, g, :], start=True, stop=True
                          ).then_inc(sem("pool_mapped"), 1)
            for c in range(4):
                pe.wait_ge(sem("conv_done"), c + 1)
                mm = pe.matmul(bank[6][:, :], ones[:, :], conv[:, c, :], start=(c == 0), stop=(c == 3))
            mm.then_inc(sem("ln_summed"), 1)
            for c in range(4):
                pe.wait_ge(sem("ln_square"), c + 1)
                pe.matmul(bank[7][:, :], ones[:, :], sq_feed[c % 2][:, :], start=(c == 0), stop=(c == 3)
                          ).then_inc(sem("ln_square_sum"), 1)
            pe.wait_ge(sem("pool_out"), 4)
            pe.wait_ge(sem("ln_root"), 1)
            for f in range(N_WO2):
                pe.wait_ge(sem("mixed_low"), f + 1)
                f_in = (f + 4) % 8
                spread_unit("wo2", U_WO2 + f, xh[:, f_in, :], xl[:, f_in, :], U_WO2 + f + 1, first=(f == 0),
                            last=(f == N_WO2 - 1))

            phase_start("ffn3")
            gate_up("g3", U_GU3)
            down("g3", "ffn3", U_DN3)
            for m in range(DK):
                square_sum("final", m, bank[4][:, :])

        @block.scalar
        def _(act):
            def high(u, i=None):
                wait, trip = (lambda c: c) if i is None else (lambda c: i * 4 + c), u // RAW + 1
                act.wait_ge(raw_loaded[u % RAW], 16 * trip if i is None else i * 16 + 16 * trip)
                if u >= SPL or i is not None:
                    act.wait_ge(unit_done, wait(u - SPL + 1))
                act.copy(wh[:, u % SPL, :], raw[:, u % RAW, :]).then_inc(high_done, 1)

            def after(u, i=None):
                if u + SPL < UNITS:
                    high(u + SPL, i=i)

            def feed_chunk(name, gain, m, src, dst, n=S, parts=True):
                if parts:
                    act.activation(dst[:, m, 0:n], src[:, m, 0:n], ACT.Copy, scale=v(gain, m)
                                   ).then_inc(sem(f"{name}_high"), 1)
                if m >= 2:
                    act.wait_ge(sem(f"{name}_sum"), m - 1)
                act.activation(sq_feed[m % 2][:, 0:n], src[:, m, 0:n], ACT.Square).then_inc(sem(f"{name}_square"), 1)

            def feed_root(name, out, src, count=D, bias=0):
                act.wait_ge(sem(f"{name}_sum"), DK)
                act.activation(out, src, ACT.Sqrt, bias=eps[:, bias:bias + 1], scale=1.0 / count
                               ).then_inc(sem(f"{name}_root"), 1)

            def feed(name, gain, parts=True):
                for m in range(DK):
                    act.wait_ge(sem(f"{name}_residual"), m + 1)
                    feed_chunk(name, gain, m, h, xh, parts=parts)
                feed_root(name, rt_feed[:, :], bank[4][:, :])

            def stepped(cfg, extra=None):
                tag, steps, u0, n, _, _, _, sq, rt = cfg
                for j in range(len(steps) + 1):
                    if j < len(steps):
                        after(u0 + j)
                        if steps[j] in NORM:
                            k = upto_step(steps, NORM, j)
                            act.wait_ge(sem(f"{tag}_taken"), j + 1)
                            if k > 2:
                                act.wait_ge(sem(f"{tag}_summed"), k - 2)
                            act.activation(sq[(k - 1) % 2], tiles[j % 3][:, 0:n], ACT.Square
                                           ).then_inc(sem(f"{tag}_squared"), 1)
                    i = j - 1
                    if i >= 0 and steps[i] in NORM:
                        k = upto_step(steps, NORM, i)
                        act.wait_ge(sem(f"{tag}_summed"), k)
                        if k > 2:
                            act.wait_ge(sem(f"{tag}_normed"), k - 2)
                        act.activation(rt[(k - 1) % 2], bank[2][:, 0:n], ACT.Sqrt, bias=eps[:, 0:1],
                                       scale=1.0 / (P if steps[i] in ("mq", "km") else HD)
                                       ).then_inc(sem(f"{tag}_rooted"), 1)
                    if extra:
                        extra(j)

            def gate_up(name, u0):
                with act.Fori(0, FC // 2) as i:
                    for c in range(2):
                        after(u0 + 2 * c, i)
                        act.wait_ge(sem(f"{name}_gate"), i * 2 + (c + 1))
                        act.activation(tiles[c][:, :], tiles[c][:, :], ACT.Silu).then_inc(sem(f"{name}_silu"), 1)
                        after(u0 + 2 * c + 1, i)
                        act.wait_ge(sem(f"{name}_act"), i * 2 + (c + 1))
                        act.copy(hh[:, bass.ds(i * 2 + c, 1), :].rearrange("p a n -> p (a n)"), tiles[2 + c][:, :]
                                 ).then_inc(sem(f"{name}_high"), 1)

            def down(u0):
                with act.Fori(0, FC // 4) as i:
                    for c in range(4):
                        after(u0 + c, i)
                for f in range(FC // 4 * 4, FC):
                    after(u0 + f)

            act.wait_ge(sem("vectors_loaded"), 16)
            act.wait_ge(sem("mem_loaded"), 16)
            for m in range(DK):
                feed_chunk("mem", "mem_norm", m, mem_in, mem_h, MEM)
                if m == 1:
                    high(0)
                if m == 3:
                    high(1)
            act.wait_ge(sem("eps_set"), 4)
            feed_root("mem", rt_feed[:, 0:MEM], bank[6][:, 0:MEM])
            act.wait_ge(sem("x_loaded"), 16)
            stepped(mem_cfg, lambda j: j < DK and feed_chunk("ffn1", "ffn1_norm", j, h, xh))
            act.wait_ge(sem("mem_factor"), 1)
            feed_root("ffn1", rt_feed[:, :], bank[7][:, :])
            act.wait_ge(sem("angles"), 1)
            act.activation(sin[:, :], ang[:, :], ACT.Sin).then_inc(sem("sine"), 1)
            act.activation(turns[:, :], ang[:, :], ACT.Abs).then_inc(sem("act_own"), 1)
            act.wait_ge(sem("act_own"), 1)
            act.activation(cos[:, :], turns[:, :], ACT.Sin, bias=eps[:, 2:3], scale=-1.0).then_inc(sem("sine"), 1)
            gate_up("g1", U_GU1)
            down(U_DN1)
            act.wait_ge(unit_done, U_IN)
            act.dma_start(tri[:, :], T["triangle"]).then_inc(sem("triangle_loaded"), 16)
            feed("mix", "mix_norm")

            def in_extra(j):
                if j == 1:
                    act.wait_ge(sem("forget_in"), 1)
                    act.activation(forget[:, 1], forget[:, 0], ACT.Abs).then_inc(sem("act_own"), 1)
                    act.wait_ge(sem("act_own"), 2)
                    act.activation(forget[:, 1], forget[:, 1], ACT.Exp, scale=-1.0).then_inc(sem("act_own"), 1)
                    act.wait_ge(sem("act_own"), 3)
                    act.activation(forget[:, 1], forget[:, 1], ACT.Ln, bias=eps[:, 3:4]
                                   ).then_inc(sem("forget_ln"), 1)
                for t, step in ((ki, 0), (kd, IN_STEPS.index("dk"))):
                    if j == step + 3:
                        act.wait_ge(sem("in_roped"), upto_step(IN_STEPS, ROPE, step))
                        act.dma_start(t[HD:P, :], t[0:HD, :]).then_inc(sem("shared_keys"), 16)

            stepped(in_cfg, in_extra)

            for n in range(LAST):
                if n % 4 == 0 and 4 <= n <= 4 * GATES:
                    after(gate_unit(n // 4 - 1))
                if n < N_IDX:
                    ext = ITEMS[n][3]
                    act.wait_ge(sem("scores"), n + 1)
                    if n >= 2:
                        act.wait_ge(sem("idx_added"), n - 1)
                    act.activation(soft[n % 2][:, 0:ext], bank[3 + n % 2][:, 0:ext], ACT.Relu
                                   ).then_inc(sem("relu_done"), 1)
                elif n < len(ITEMS):
                    ext, c = ITEMS[n][3], n % 4
                    act.wait_ge(sem("shifted"), n - N_IDX + 1)
                    act.activation(soft[n % 2][:, 0:ext], soft[n % 2][:, 0:ext], ACT.Exp, scale=-1.0,
                                   bias=stat[:, 0, c:c + 1], accum_out=stat[:, 1, c:c + 1]).then_inc(sem("exped"), 1)
                s = n - 1 - N_IDX
                if 0 <= s < len(ITEMS) - N_IDX:
                    ext = ITEMS[n - 1][3]
                    act.wait_ge(sem("turned"), s + 1)
                    if s >= 2:
                        act.wait_ge(sem("weighed"), s - 1)
                    act.copy(probs_t[s % 2][:, 0:ext], bank[5 + s % 2][:, 0:ext]).then_inc(sem("turned_out"), 1)
                if n % 4 == 0 and 4 <= n <= 4 * GATES:
                    act.wait_ge(sem("gates_taken"), n // 4)
                    act.activation(gate_t[:, :], gate_t[:, :], ACT.Exp, scale=-1.0).then_inc(sem("gate_exp"), 1)
                for c in SPLITS.get(n, ()):
                    act.wait_ge(sem("heads_out"), c + 1)
                    act.wait_ge(unit_done, U_BR)
                    if c >= 8:
                        act.wait_ge(sem("out_split"), 8)
                    act.copy(chunk_parts(c)[0], chunk_home(c)).then_inc(sem("out_high"), 1)

            for u in range(U_BR, U_BR + N_BR):
                after(u)
                for m in range(DK):
                    if U_BR + (12 * m + 11) // DK == u:
                        act.wait_ge(sem("merge_summed"), m + 1)
                        act.copy(mgh[:, m, :], tiles[3 + m % 2][:, :]).then_inc(sem("merged_high"), 1)
            for u in range(U_WO, U_WO + N_WO):
                after(u)
            feed("ffn2", "ffn2_norm")
            gate_up("g2", U_GU2)
            down(U_DN2)
            act.wait_ge(unit_done, U_IN2)
            act.dma_start(wpool[:, :, :], T["pool_weights"]).then_inc(sem("pool_weights_loaded"), 16)
            feed("mix2", "g_mix_2")
            for j, kind in enumerate(IN2_STEPS):
                after(U_IN2 + j)
                c = chunk_of(IN2_STEPS, j)
                if kind == "s":
                    act.wait_ge(sem("in2_taken"), j + 1)
                    act.activation(sig[:, c % 2, :], sig[:, c % 2, :], ACT.Sigmoid, bias=v("b_in_2", 4 + c)
                                   ).then_inc(sem("glu_sigmoid"), 1)
                if kind == "p":
                    act.wait_ge(sem("in2_taken"), j + 1)
                    act.activation(pool_in[:, c, PADW:], pool_in[:, c, PADW:], ACT.Identity, bias=v("b_in_2", 8 + c)
                                   ).then_inc(sem("pool_biased"), 1)
            for g in range(4):
                act.wait_ge(sem("pool_mapped"), g + 1)
                act.activation(ymix[:, 4 + g, :], bank[2 + g][:, :], ACT.Copy, scale=v("s_pool_2", g)
                               ).then_inc(sem("pool_out"), 1)
                act.wait_ge(sem("pool_out"), g + 1)
                act.copy(xh[:, 4 + g, :], ymix[:, 4 + g, :]).then_inc(sem("mixed_high"), 1)
            for c in range(4):
                act.wait_ge(sem("centred"), c + 1)
                if c >= 2:
                    act.wait_ge(sem("ln_square_sum"), c - 1)
                act.activation(sq_feed[c % 2][:, :], conv[:, c, :], ACT.Square).then_inc(sem("ln_square"), 1)
            act.wait_ge(sem("ln_square_sum"), 4)
            act.activation(rt_feed[:, :], bank[7][:, :], ACT.Sqrt, bias=eps[:, 1:2], scale=1.0 / (4 * P)
                           ).then_inc(sem("ln_root"), 1)
            for c in range(4):
                act.wait_ge(sem("ln_scaled"), c + 1)
                act.activation(ymix[:, c, :], ymix[:, c, :], ACT.Silu, bias=v("ln_b_2", c)).then_inc(sem("ln_out"), 1)
                act.wait_ge(sem("ln_out"), c + 1)
                act.copy(xh[:, c, :], ymix[:, c, :]).then_inc(sem("mixed_high"), 1)
            for u in range(U_WO2, U_WO2 + N_WO2):
                after(u)
            feed("ffn3", "g_ffn_2")
            gate_up("g3", U_GU3)
            down(U_DN3)
            feed("final", None, parts=False)

        @block.vector
        def _(dve):
            owned = [0]

            def own(ins):
                owned[0] += 1
                ins.then_inc(sem("dve_own"), 1)
                dve.wait_ge(sem("dve_own"), owned[0])

            def low(name, gain, m, src, hi, lo_, n=S):
                dve.wait_ge(sem(f"{name}_high"), m + 1)
                dve.scalar_tensor_tensor(out=lo_[:, m, 0:n], in0=src[:, m, 0:n], scalar=v(gain, m),
                                         in1=hi[:, m, 0:n].bitcast(F32), op0=ALU.mult, op1=ALU.subtract
                                         ).then_inc(sem(f"{name}_low"), 1)

            def factor(name, out, root):
                dve.wait_ge(sem(f"{name}_root"), 1)
                dve.reciprocal(out, root).then_inc(sem(f"{name}_factor"), 1)
                dve.wait_ge(sem(f"{name}_factor"), 1)

            def feed(name, gain, gathered, u_last, share, parts=True):
                for m in range(DK):
                    if m < DK - 1:
                        dve.wait_ge(sem(f"{gathered}_gathered"), m + 1)
                    else:
                        dve.wait_ge(unit_done, u_last + 1)
                    dve.scalar_tensor_tensor(out=h[:, m, :], in0=bank[(m + 4) % 8][:, :], scalar=share,
                                             in1=h[:, m, :], op0=ALU.mult, op1=ALU.add
                                             ).then_inc(sem(f"{name}_residual"), 1)
                    if parts and m:
                        low(name, gain, m - 1, h, xh, xl)
                if parts:
                    dve.wait_ge(sem(f"{name}_residual"), DK)
                    low(name, gain, DK - 1, h, xh, xl)

            def gate_up(name, u0):
                dve.sem_inc(sem(f"{name}_banks"), 2)
                dve.sem_inc(sem(f"{name}_split"), 1)
                with dve.Fori(0, FC // 2) as i:
                    for c in range(2):
                        one = i * 2 + (c + 1)
                        dve.wait_ge(unit_done, i * 4 + (u0 + 2 * c + 1))
                        dve.tensor_tensor(tiles[c][:, :], bank[2 * c][:, :], rstd[:, :], ALU.mult
                                          ).then_inc(sem(f"{name}_gate"), 1)
                        dve.wait_ge(unit_done, i * 4 + (u0 + 2 * c + 2))
                        dve.wait_ge(sem(f"{name}_split"), one)
                        dve.tensor_tensor(tiles[2 + c][:, :], bank[2 * c + 1][:, :], rstd[:, :], ALU.mult
                                          ).then_inc(sem(f"{name}_banks"), 1)
                        dve.wait_ge(sem(f"{name}_silu"), one)
                        dve.wait_ge(sem(f"{name}_banks"), i * 2 + (c + 3))
                        dve.tensor_tensor(tiles[2 + c][:, :], tiles[2 + c][:, :], tiles[c][:, :], ALU.mult
                                          ).then_inc(sem(f"{name}_act"), 1)
                        dve.wait_ge(sem(f"{name}_high"), one)
                        f = bass.ds(i * 2 + c, 1)
                        dve.tensor_tensor(hl[:, f, :].rearrange("p a n -> p (a n)"), tiles[2 + c][:, :],
                                          hh[:, f, :].rearrange("p a n -> p (a n)").bitcast(F32), ALU.subtract
                                          ).then_inc(sem(f"{name}_split"), 1)

            def stepped(cfg, extra=None):
                tag, steps, u0, n, _, _, tok, _, rt = cfg
                for j in range(len(steps) + 2):
                    if j < len(steps):
                        if j >= 3 and steps[j - 3] in TURN:
                            dve.wait_ge(sem(f"{tag}_turned"), upto_step(steps, TURN, j - 3))
                        if j >= 3 and steps[j - 3] in NORM:
                            dve.wait_ge(sem(f"{tag}_normed"), upto_step(steps, NORM, j - 3))
                        if j >= 3 and steps[j - 3] in ROPE:
                            dve.wait_ge(sem(f"{tag}_roped"), upto_step(steps, ROPE, j - 3))
                        dve.wait_ge(unit_done, u0 + j + 1)
                        dve.tensor_tensor(tiles[j % 3][:, 0:n], bank[j % 2][:, 0:n], tok[:, 0:n], ALU.mult
                                          ).then_inc(sem(f"{tag}_taken"), 1)
                    i = j - 1
                    if 0 <= i < len(steps) and steps[i] in NORM:
                        k, kind, c = upto_step(steps, NORM, i), steps[i], chunk_of(steps, i)
                        m = HD if kind == "dk" else P
                        t = tiles[i % 3][0:m, 0:n]
                        out = {"fq": fq, "fk": fk, "mq": mq, "km": km}[kind][:, c, :] if kind not in ("dk", "dq") else t
                        gain = {"f": "fox_", "d": "dsa_", "m": "mem_", "k": "mem_"}[kind[0]] \
                            + ("k" if kind == "km" else kind[1]) + "_norm"
                        dve.wait_ge(sem(f"{tag}_rooted"), k)
                        root = rt[(k - 1) % 2][0:m]
                        own(dve.reciprocal(root, root))
                        dve.scalar_tensor_tensor(out=out, in0=t, scalar=v(gain)[0:m], in1=root, op0=ALU.mult,
                                                 op1=ALU.mult).then_inc(sem(f"{tag}_normed"), 1)
                    if 0 <= i < len(steps) and steps[i] in TURN:
                        k, kind, c = upto_step(steps, TURN, i), steps[i], chunk_of(steps, i)
                        dve.wait_ge(sem(f"{tag}_turned"), k)
                        src = bank[4 + k % 2][:, 0:n].rearrange("p (b f) -> p b f", f=P)
                        if kind in ("fv", "vm"):
                            dst = fv if kind == "fv" else vm
                            dve.tensor_copy(dst[:, :, c * P:(c + 1) * P], src).then_inc(sem(f"{tag}_turned_out"), 1)
                        elif kind == "dk":
                            dve.tensor_copy(dv[:, :, :], src[:, :, 0:HD]).then_inc(sem(f"{tag}_turned_out"), 1)
                        else:
                            for b in range(QB):
                                ins = dve.tensor_tensor(forget[:, 0, b, :], src[:, b, 0:HEADS],
                                                        vec[:, VEC_COLS["b_forget"][0]:][:, 0:HEADS], ALU.add)
                            ins.then_inc(sem("forget_in"), 1)
                            dve.tensor_scalar(iw[:, :, :], src[:, :, HEADS:2 * HEADS],
                                              HEADS ** -0.5 * HD ** -0.5, None, ALU.mult
                                              ).then_inc(sem(f"{tag}_turned_out"), 1)
                    i = j - 2
                    if 0 <= i < len(steps) and steps[i] in ROPE:
                        k, kind, c = upto_step(steps, ROPE, i), steps[i], chunk_of(steps, i)
                        m = HD if kind in ("dk", "ik") else P
                        t = tiles[i % 3][0:m, :]
                        out = {"iq": iq[:, c, :], "dq": dq[:, c, :], "ik": ki[0:HD, :], "dk": kd[0:HD, :]}[kind]
                        dve.wait_ge(sem(f"{tag}_rotated"), k)
                        if k > 1:
                            dve.wait_ge(sem(f"{tag}_roped"), k - 1)
                        dve.tensor_tensor(tiles[7][0:m, :], bank[3][0:m, :], sin[0:m, :], ALU.mult)
                        own(dve.tensor_tensor(t, t, cos[0:m, :], ALU.mult))
                        dve.tensor_tensor(out, t, tiles[7][0:m, :], ALU.add).then_inc(sem(f"{tag}_roped"), 1)
                    if extra:
                        extra(j)

            for c, val in enumerate((EPS, LN_EPS, float(np.pi / 2), 1.0)):
                dve.memset(eps[:, c:c + 1], val).then_inc(sem("eps_set"), 1)
            dve.wait_ge(sem("vectors_loaded"), 16)
            for name, scale in (("fox_q_norm", HD ** -0.5), ("dsa_q_norm", HD ** -0.5), ("mem_q_norm", P ** -0.5)):
                own(dve.tensor_scalar(v(name), v(name), scale, None, ALU.mult))
            dve.wait_ge(sem("positions_loaded"), 16)
            own(dve.tensor_copy(turns[:, :], pos[:, :]))
            own(dve.tensor_scalar(ang[:, :], turns[:, :], v("inv_freq"), None, ALU.mult))
            own(dve.tensor_scalar(turns_raw[:, :], ang[:, :], 1.0 / TURN_RAD, ROUNDER, ALU.mult, ALU.add))
            own(dve.tensor_scalar(turns[:, :], turns_raw[:, :], -ROUNDER, None, ALU.add))
            for part in TURN_PARTS:
                own(dve.scalar_tensor_tensor(out=ang[:, :], in0=turns[:, :], scalar=-part, in1=ang[:, :],
                                             op0=ALU.mult, op1=ALU.add))
            dve.tensor_scalar(ang[:, :], ang[:, :], PI_BELOW, -PI_BELOW, ALU.min, ALU.max
                              ).then_inc(sem("angles"), 1)
            for m in range(DK):
                low("mem", "mem_norm", m, mem_in, mem_h, mem_l, MEM)
            factor("mem", mem_rstd[:, :], rt_feed[:, 0:MEM])
            stepped(mem_cfg, lambda j: j < DK and low("ffn1", "ffn1_norm", j, h, xh, xl))
            dve.wait_ge(sem("sine"), 2)
            factor("ffn1", rstd[:, :], rt_feed[:, :])
            gate_up("g1", U_GU1)
            feed("mix", "mix_norm", "g1", U_IN - 1, 0.5)
            factor("mix", rstd[:, :], rt_feed[:, :])

            def in_extra(j):
                if j == 2:
                    dve.wait_ge(sem("forget_ln"), 1)
                    dve.scalar_tensor_tensor(out=forget[:, 0].rearrange("p b h -> p (b h)"),
                                             in0=forget[:, 0].rearrange("p b h -> p (b h)"), scalar=0.0,
                                             in1=forget[:, 1].rearrange("p b h -> p (b h)"),
                                             op0=ALU.min, op1=ALU.subtract).then_inc(sem("forget_logs"), 1)
                if j == 5:
                    dve.wait_ge(sem("forget_summed"), 1)
                    dve.tensor_copy(cum[0:HEADS, :], bank[6][0:HEADS, :]).then_inc(sem("forget_out"), 1)

            stepped(in_cfg, in_extra)

            def bias(hd):
                dve.wait_ge(sem("bias"), hd + 1)
                dve.tensor_scalar(fbias[hd % 2][:, :], bank[2][:, :], -1.0, None, ALU.mult
                                  ).then_inc(sem("bias_out"), 1)

            def kept(q):
                return sel[:, sel_at[q]:sel_at[q] + (q + 1) * P]

            def search(r):
                q, r = 1 + r // ROUNDS, r % ROUNDS
                own(dve.max(mx8[:, :], kept(q)))
                own(dve.match_replace(kept(q), mx8[:, :], kept(q), TAKEN))
                if r == ROUNDS - 1:
                    own(dve.tensor_scalar(kept(q), kept(q), TAKEN / 2, MASKED, ALU.is_gt, ALU.mult))

            def shift(n):
                kind, hd, q, ext = ITEMS[n]
                s, c = n - N_IDX, n % 4
                if kind == "fox":
                    add = fbias[hd % 2][:, 0:ext]
                    dve.wait_ge(sem("bias_out"), hd + 1)
                elif kind == "dsa":
                    add = kept(q) if q else cmask[:, S - P:S]
                else:
                    add = cmask[:, 0:ext]
                dve.wait_ge(sem("scores"), n + 1)
                if s >= 2:
                    dve.wait_ge(sem("turned"), s - 1)
                dve.tensor_tensor_reduce(soft[n % 2][:, 0:ext], bank[3 + n % 2][:, 0:ext], add, -1.0, 3.0e38,
                                         ALU.add, ALU.min, stat[:, 0, c:c + 1]).then_inc(sem("shifted"), 1)

            def normalise(n):
                ext, s, c = ITEMS[n][3], n - N_IDX, n % 4
                dve.wait_ge(sem("exped"), s + 1)
                own(dve.reciprocal(stat[:, 2, c:c + 1], stat[:, 1, c:c + 1]))
                dve.tensor_scalar(soft[n % 2][:, 0:ext], soft[n % 2][:, 0:ext], stat[:, 2, c:c + 1], None,
                                  ALU.mult).then_inc(sem("probs"), 1)

            dve.wait_ge(sem("in_roped"), upto_step(IN_STEPS, ROPE, 99))
            dve.wait_ge(sem("in_normed"), upto_step(IN_STEPS, NORM, 99))
            dve.wait_ge(sem("in_turned_out"), upto_step(IN_STEPS, TURN, 99))
            pending = []
            for n in range(LAST + 1):
                if N_IDX <= n - 1 < len(ITEMS):
                    normalise(n - 1)
                if n < len(ITEMS):
                    kind, hd, q, ext = ITEMS[n]
                    if n == N_IDX:
                        bias(0)
                    if kind == "fox" and q == 3 and hd < HEADS - 1:
                        bias(hd + 1)
                    if kind == "idx":
                        dve.wait_ge(sem("relu_done"), n + 1)
                        dve.scalar_tensor_tensor(out=kept(q), in0=soft[n % 2][:, 0:ext], scalar=iw[:, q, hd:hd + 1],
                                                 in1=kept(q) if hd else cmask[:, S - ext:S],
                                                 op0=ALU.mult, op1=ALU.add).then_inc(sem("idx_added"), 1)
                        dve.wait_ge(sem("idx_added"), n + 1)
                    else:
                        shift(n)
                if n % 4 == 0 and 4 <= n <= 4 * GATES:
                    g = n // 4 - 1
                    dve.wait_ge(unit_done, gate_unit(g) + 1)
                    if g:
                        dve.wait_ge(sem("gate_ready"), g)
                    dve.tensor_tensor(gate_t[:, :], bank[g % 2][:, :], rstd[:, :], ALU.mult
                                      ).then_inc(sem("gates_taken"), 1)
                if n % 4 == 1 and 5 <= n <= 4 * GATES + 1:
                    g = (n - 5) // 4
                    dve.wait_ge(sem("gate_exp"), g + 1)
                    own(dve.tensor_scalar(gate_t[:, :], gate_t[:, :], 1.0, None, ALU.add))
                    dve.reciprocal(gate_slot(g), gate_t[:, :]).then_inc(sem("gate_ready"), 1)
                if ends_chunk(n - 3):
                    c = chunk_id(n - 3)
                    dve.wait_ge(sem("weighed"), n - 3 - N_IDX + 1)
                    dve.tensor_copy(chunk_home(c), bank[7][:, :]).then_inc(sem("heads_out"), 1)
                for c in pending:
                    dve.wait_ge(sem("out_high"), c + 1)
                    hi, lo_ = chunk_parts(c)
                    dve.tensor_tensor(lo_, chunk_home(c), hi.bitcast(F32), ALU.subtract
                                      ).then_inc(sem("out_split"), 1)
                pending = SPLITS.get(n, ())
                if SEARCH0 <= n < SEARCH0 + (QB - 1) * ROUNDS:
                    search(n - SEARCH0)

            def merge_low(m):
                dve.wait_ge(sem("merged_high"), m + 1)
                dve.tensor_tensor(mgl[:, m, :], tiles[3 + m % 2][:, :], mgh[:, m, :].bitcast(F32), ALU.subtract
                                  ).then_inc(sem("merged_low"), 1)

            dve.wait_ge(sem("gate_ready"), GATES)
            for m in range(DK):
                if m % 2:
                    dve.wait_ge(unit_done, U_BR + (12 * m + 11) // DK + 1)
                else:
                    dve.wait_ge(sem("branches_even"), m // 2 + 1)
                for n in range(3):
                    ins = dve.tensor_tensor(tiles[n][:, :], bank[3 * (m % 2) + n][:, :], gate_slot(n * DK + m),
                                            ALU.mult)
                ins.then_inc(sem("branches_read"), 1)
                dve.wait_ge(sem("branches_read"), m + 1)
                own(dve.tensor_tensor(tiles[0][:, :], tiles[0][:, :], tiles[1][:, :], ALU.add))
                if m >= 2:
                    dve.wait_ge(sem("merged_low"), m - 1)
                dve.tensor_tensor(tiles[3 + m % 2][:, :], tiles[0][:, :], tiles[2][:, :], ALU.add
                                  ).then_inc(sem("merge_summed"), 1)
                merge_low(m)
            feed("ffn2", "ffn2_norm", "wo", U_GU2 - 1, 1.0)
            factor("ffn2", rstd[:, :], rt_feed[:, :])
            gate_up("g2", U_GU2)
            feed("mix2", "g_mix_2", "g2", U_IN2 - 1, 0.5)
            factor("mix2", rstd[:, :], rt_feed[:, :])

            for c in range(4):
                dve.memset(glu[:, c, 0:TAPS - 1], 0.0)
                dve.memset(pool_in[:, c, 0:PADW], 0.0)
            dve.memset(psum_a[:, 0:PADW], 0.0)
            own(dve.memset(psum_b[:, 0:PADW], 0.0))

            def taps():
                for c in range(4):
                    for k in range(TAPS):
                        w = v("w_dw_2", c * TAPS + k)
                        src = glu[:, c, k:k + S]
                        if k == 0:
                            own(dve.tensor_scalar(conv[:, c, :], src, w, v("b_dw_2", c), ALU.mult, ALU.add))
                        elif k < TAPS - 1:
                            own(dve.scalar_tensor_tensor(out=conv[:, c, :], in0=src, scalar=w, in1=conv[:, c, :],
                                                         op0=ALU.mult, op1=ALU.add))
                        else:
                            dve.scalar_tensor_tensor(out=conv[:, c, :], in0=src, scalar=w, in1=conv[:, c, :],
                                                     op0=ALU.mult, op1=ALU.add).then_inc(sem("conv_done"), 1)
                            dve.wait_ge(sem("conv_done"), c + 1)
                        yield c

            conv_taps, done = taps(), 0
            for j, kind in enumerate(IN2_STEPS):
                c = chunk_of(IN2_STEPS, j)
                out = {"a": tiles[c % 2][:, :], "s": sig[:, c % 2, :], "p": pool_in[:, c, PADW:]}[kind]
                dve.wait_ge(unit_done, U_IN2 + j + 1)
                dve.tensor_tensor(out, bank[j % 2][:, :], rstd[:, :], ALU.mult).then_inc(sem("in2_taken"), 1)
                if kind == "s":
                    dve.wait_ge(sem("glu_sigmoid"), c + 1)
                    own(dve.scalar_tensor_tensor(out=glu[:, c, TAPS - 1:], in0=tiles[c % 2][:, :],
                                                 scalar=v("b_in_2", c), in1=sig[:, c % 2, :],
                                                 op0=ALU.add, op1=ALU.mult))
                ready = TAPS * sum(k == "s" for k in IN2_STEPS[:j + 1])
                for _ in range(min(7, ready - done)):
                    next(conv_taps)
                    done += 1
            for g, width in enumerate(WINDOWS):
                dve.wait_ge(sem("pool_biased"), g + 1)
                if g:
                    dve.wait_ge(sem("pooled"), g)
                src, shift_by, k = pool_in[:, g, :], 1, 0
                while shift_by < width:
                    dst = (psum_a, psum_b)[k % 2]
                    own(dve.tensor_tensor(dst[:, PADW:], src[:, PADW:], src[:, PADW - shift_by:PADW - shift_by + S],
                                          ALU.add))
                    src, shift_by, k = dst, shift_by * 2, k + 1
                o = VEC_COLS["pool_inv"][0] + g * PADW
                own(dve.tensor_tensor(src[:, PADW:2 * PADW], src[:, PADW:2 * PADW], vec[:, o:o + PADW], ALU.mult))
                own(dve.tensor_scalar(src[:, 2 * PADW:], src[:, 2 * PADW:], 1.0 / width, None, ALU.mult))
                dve.tensor_tensor(pooled[:, g, :], src[:, PADW:], pool_in[:, g, PADW:], ALU.subtract
                                  ).then_inc(sem("pooled"), 1)
            for g in range(4):
                dve.wait_ge(sem("mixed_high"), g + 1)
                dve.tensor_tensor(xl[:, 4 + g, :], ymix[:, 4 + g, :], xh[:, 4 + g, :].bitcast(F32), ALU.subtract
                                  ).then_inc(sem("mixed_low"), 1)
            for _ in conv_taps:
                pass
            dve.wait_ge(sem("ln_summed"), 1)
            own(dve.tensor_scalar(tiles[0][:, :], bank[6][:, :], 1.0 / (4 * P), None, ALU.mult))
            for c in range(4):
                dve.tensor_tensor(conv[:, c, :], conv[:, c, :], tiles[0][:, :], ALU.subtract
                                  ).then_inc(sem("centred"), 1)
            dve.wait_ge(sem("ln_root"), 1)
            own(dve.reciprocal(tiles[1][:, :], rt_feed[:, :]))
            for c in range(4):
                dve.wait_ge(sem("centred"), c + 1)
                dve.scalar_tensor_tensor(out=ymix[:, c, :], in0=conv[:, c, :], scalar=v("ln_g_2", c),
                                         in1=tiles[1][:, :], op0=ALU.mult, op1=ALU.mult
                                         ).then_inc(sem("ln_scaled"), 1)
            for c in range(4):
                dve.wait_ge(sem("mixed_high"), 4 + c + 1)
                dve.tensor_tensor(xl[:, c, :], ymix[:, c, :], xh[:, c, :].bitcast(F32), ALU.subtract
                                  ).then_inc(sem("mixed_low"), 1)
            feed("ffn3", "g_ffn_2", "wo2", U_GU3 - 1, 1.0)
            factor("ffn3", rstd[:, :], rt_feed[:, :])
            gate_up("g3", U_GU3)
            feed("final", None, "g3", UNITS - 1, 1.0, parts=False)
            factor("final", rstd[:, :], rt_feed[:, :])
            for m in range(DK):
                dve.scalar_tensor_tensor(out=out_t[:, m, :], in0=h[:, m, :], scalar=v("g_final_2", m),
                                         in1=rstd[:, :], op0=ALU.mult, op1=ALU.mult
                                         ).then_inc(sem("out_ready"), 1)



def column_units(w):
    n = w.shape[1] // P
    return w.reshape(DK, P, n, P).transpose(2, 1, 0, 3).reshape(n, P, DK * P)


def row_units(w):
    return w.reshape(-1, P, D)


def gate_up_units(gate, up):
    g, u = column_units(gate), column_units(up)
    return np.stack([g, u], axis=1).reshape(-1, P, DK * P)


def in_units(w):
    sizes = (BW, BW, BW, HEADS, BW, HD, HD, BW, HD, HEADS, BW, 3 * D)
    cuts = np.split(w, np.cumsum(sizes)[:-1], axis=1)
    fq, fk, fv, ff, dq, dk, dv, iq, ik, iw, mq, g = cuts
    pad = np.zeros((D, P - HD - 2 * HEADS), w.dtype)
    cols = np.concatenate([ik, ff, iw, pad, iq, fq, fk, fv, dk, dv, dq, mq, g], axis=1)
    return column_units(cols)


def branch_units(w):
    b = w.reshape(3, BK, P, DK, P).transpose(3, 0, 1, 2, 4).reshape(-1, P, P)
    return b.reshape(N_BR, DK, P, P).transpose(0, 2, 1, 3).reshape(N_BR, P, DK * P)


def pair_units(w):
    u = column_units(w)
    order = [x for c in range(4) for x in (c, 4 + c)] + [8, 9, 10, 11]
    return u[order]


def by_chunk(x):
    return np.ascontiguousarray(x.T.reshape(DK, P, -1).transpose(1, 0, 2))


def vectors(a):
    out = np.zeros((P, NV), np.float32)

    def put(name, cols):
        o, n = VEC_COLS[name]
        out[:, o:o + n] = cols

    for name in ("ffn1_norm", "mix_norm", "mem_norm", "ffn2_norm", "g_mix_2", "g_ffn_2"):
        put(name, a[name][0].reshape(-1, P).T)
    put("g_final_2", a["g_final_2"].reshape(-1, P).T)
    for name in ("fox_q_norm", "fox_k_norm", "dsa_q_norm", "dsa_k_norm"):
        put(name, np.tile(a[name][0], 2)[:, None])
    for name in ("mem_q_norm", "mem_k_norm"):
        put(name, a[name][0][:, None])
    put("b_forget", np.broadcast_to(a["b_forget"][0], (P, HEADS)))
    for name in ("b_in_2", "b_dw_2", "ln_g_2", "ln_b_2", "s_pool_2"):
        put(name, a[name][0].reshape(-1, P).T)
    put("w_dw_2", a["w_dw_2"][0].reshape(TAPS, 4, P).transpose(2, 1, 0).reshape(P, 4 * TAPS))
    put("inv_freq", np.tile(inverse_frequencies(), 4)[:, None])
    t = np.arange(PADW)
    put("pool_inv", np.broadcast_to(np.concatenate([1.0 / np.minimum(t + 1, w) for w in WINDOWS]), (P, 4 * PADW)))
    return out


def inverse_frequencies():
    return np.float32(10000.0) ** (-np.arange(0, HD, 2, dtype=np.float32) / np.float32(HD))


def constants():
    i = np.arange(P)
    ident = np.eye(P, dtype=np.float32)
    by_head = (i[:, None] // HD == i[None, :] // HD).astype(np.float32)
    rot = np.zeros((P, P), np.float32)
    for m in range(P):
        first = m % HD < HD // 2
        rot[m + HD // 2 if first else m - HD // 2, m] = -1.0 if first else 1.0
    mask = np.zeros((P, S), np.float32)
    mask[:, S - P:] = np.where(i[None, :] <= i[:, None], 0.0, MASKED)
    tri = np.ones((P, S), np.float32)
    tri[:, :P] = i[:, None] <= i[None, :]
    return {"identity": ident, "ones": np.ones((P, P), np.float32), "ones_by_head": by_head,
            "rotate_halves": rot, "causal_mask": mask, "triangle": tri}


def kernel(**inputs):
    import concourse.bacc as bacc
    from concourse.bass_utils import run_bass_kernel_spmd as run

    a = {k: np.asarray(x) for k, x in inputs.items()}
    stream = np.concatenate([
        column_units(a["w_mem_kv"][0]),
        gate_up_units(a["ffn1_w_gate"][0], a["ffn1_w_up"][0]), row_units(a["ffn1_w_down"][0]),
        in_units(a["w_in"][0]), branch_units(a["w_branch"][0]), row_units(a["w_out"][0]),
        gate_up_units(a["ffn2_w_gate"][0], a["ffn2_w_up"][0]), row_units(a["ffn2_w_down"][0]),
        pair_units(a["w_in_2"][0]), row_units(a["w_out_2"][0])[[4, 5, 6, 7, 0, 1, 2, 3]],
        gate_up_units(a["w_gate_2"][0], a["w_up_2"][0]), row_units(a["w_down_2"][0]),
    ])
    arrays = {
        "weights": np.ascontiguousarray(stream),
        "x_t": by_chunk(a["x"][0]),
        "mem_t": by_chunk(a["mem"][0]),
        "positions": np.ascontiguousarray(np.broadcast_to(a["positions"], (P, S))),
        "pool_weights": np.ascontiguousarray(a["w_pool_2"][0].transpose(1, 0, 2)),
        "vectors": vectors(a),
        **constants(),
    }
    nc = bacc.Bacc("TRN2", target_bir_lowering=False, num_devices=1)
    T = {n: nc.dram_tensor(n, x.shape, mybir.dt.from_np(x.dtype), kind="ExternalInput").ap()
         for n, x in arrays.items()}
    T["out_t"] = nc.dram_tensor("out_t", (P, DK, S), F32, kind="ExternalOutput").ap()
    build(nc, T)
    r = run(nc, [arrays], core_ids=[0])
    got = r.results[0]["out_t"]
    return np.ascontiguousarray(got.transpose(2, 1, 0).reshape(1, S, D))
```

```python
from contextlib import ExitStack

import numpy as np

import concourse.bass as bass
from concourse import mybir

ALU = mybir.AluOpType
ACT = mybir.ActivationFunctionType
F32 = mybir.dt.float32
F32R = mybir.dt.float32r
I32 = mybir.dt.int32

P = 128
D = 1024
S = 512
MEM = 256
DK = D // P
BW = 512
BK = BW // P
HEADS = 8
HD = 64
MHEADS = 4
FF = 2816
FC = FF // P
QB = S // P
TOPK = min(256, S // 4)
TAPS = 31
WINDOWS = (2, 4, 8, 16)
PADW = WINDOWS[-1]
EPS = 1e-6
LN_EPS = 1e-5
MASKED = -1.0e30
TAKEN = -3.0e38
TURN_RAD = float(2 * np.pi)
TURN_PARTS = (6.28125, 0.0019378662109375, -2.562999725341797e-06, 3.968374517882012e-09)
ROUNDER = 1.5 * 2.0 ** 23
PI_BELOW = 3.1415925
RAW = 4
SPL = 2

IN_STEPS = (["ik"] + ["iq"] * 4 + ["fq"] * 4 + ["fk"] * 3 + ["fk", "km"] + ["fv", "km"] * 2 + ["fv", "km"]
            + ["fv", "vm"] + ["dk", "vm"] + ["dq", "vm"] * 2 + ["dq"] * 2 + ["mq"] * 4)
GATES = 3 * DK

N_GU, N_DN, N_IN, N_BR, N_WO, N_IN2, N_WO2 = 2 * FC, FC, len(IN_STEPS) + GATES, 12, 8, 12, 8
U_GU1 = 0
U_DN1 = U_GU1 + N_GU
U_IN = U_DN1 + N_DN
U_BR = U_IN + N_IN
U_WO = U_BR + N_BR
U_GU2 = U_WO + N_WO
U_DN2 = U_GU2 + N_GU
U_IN2 = U_DN2 + N_DN
U_WO2 = U_IN2 + N_IN2
U_GU3 = U_WO2 + N_WO2
U_DN3 = U_GU3 + N_GU
UNITS = U_DN3 + N_DN

VEC_COLS = {}
for _name, _n in (("ffn1_norm", 8), ("mix_norm", 8), ("mem_norm", 8), ("ffn2_norm", 8), ("g_mix_2", 8),
                  ("g_ffn_2", 8), ("g_final_2", 8), ("fox_q_norm", 1), ("fox_k_norm", 1), ("dsa_q_norm", 1),
                  ("dsa_k_norm", 1), ("mem_q_norm", 1), ("mem_k_norm", 1), ("b_forget", HEADS), ("b_in_2", 12),
                  ("w_dw_2", 4 * TAPS), ("b_dw_2", 4), ("ln_g_2", 4), ("ln_b_2", 4), ("s_pool_2", 4),
                  ("inv_freq", 1), ("pool_inv", len(WINDOWS) * PADW)):
    VEC_COLS[_name] = (sum(n for _, n in VEC_COLS.values()), _n)
NV = sum(n for _, n in VEC_COLS.values())

IN2_STEPS = ["a", "s"] * 4 + ["p"] * 4

ITEMS = ([("idx", h, q, (q + 1) * P) for q in range(1, QB) for h in range(HEADS)]
         + [("fox", h, q, (q + 1) * P) for h in range(HEADS) for q in range(QB)]
         + [("dsa", h, q, (q + 1) * P) for h in range(HEADS) for q in range(QB)]
         + [("mem", h, q, MEM) for h in range(MHEADS) for q in range(QB)])
N_IDX = sum(it[0] == "idx" for it in ITEMS)
TURN_LAG, WEIGH_LAG = 2, 3
ROUNDS = TOPK // 8
FLUSH = 3
FILLS = [16] * FLUSH + [{"idx": 6, "fox": 6, "dsa": 5, "mem": 4}[it[0]] for it in ITEMS] + [0] * WEIGH_LAG
GATE_MM = 3 * DK


def gate_steps():
    done, out = 0, []
    for n, k in enumerate(FILLS):
        done += k
        while len(out) < GATES and done >= GATE_MM * (len(out) + 1):
            out.append(n - FLUSH)
    return out + [len(ITEMS) + WEIGH_LAG - 1] * (GATES - len(out))


GATE_STEP = gate_steps()


def build(nc, T):
    ctx = ExitStack()
    with ctx:
        base = [16512]

        def at(name, shape, dt, offset=None):
            size = int(np.prod(shape[1:])) * 4
            if offset is None:
                offset = base[0]
                base[0] += size + (-size) % 32
            return nc.alloc_sbuf_tensor_at(name, shape, dt, offset=offset)

        raw = at("raw_weights", [P, RAW, DK * P], F32)
        wh = at("weights_high", [P, SPL, DK * P], F32R)
        wl = at("weights_low", [P, SPL, DK * P], F32R)
        h = at("residual", [P, DK, S], F32)
        x_at = base[0]
        xh = at("input_high", [P, DK, S], F32R)
        xl = at("input_low", [P, DK, S], F32R)
        big = base[0]
        base[0] += 2 * FC * S * 4
        hh = at("hidden_high", [P, FC, S], F32R, big)
        hl = at("hidden_low", [P, FC, S], F32R, big + FC * S * 4)
        K2 = S * 4
        fq = at("fox_q", [P, 4, S], F32, big)
        kd = at("dsa_k", [P, S], F32, big + 4 * K2)
        fv = at("fox_v", [P, QB, BW], F32, big + 5 * K2)
        fk = at("fox_k", [P, 4, S], F32, big + 9 * K2)
        iq = at("idx_q", [P, 4, S], F32, big + 13 * K2)
        ki = at("idx_k", [P, S], F32, big + 17 * K2)
        dq = at("dsa_q", [P, 4, S], F32, big + 18 * K2)
        mq = at("mem_q", [P, 4, S], F32, big + 22 * K2)
        dv = at("dsa_v", [P, QB, HD], F32, big + 26 * K2)
        sel = at("top_keys", [P, 9 * P], F32, big + 26 * K2 + 1024)
        tri = at("triangle", [P, S], F32, big + 26 * K2 + 1024)
        gates_own = at("gates", [P, 15, S], F32, big + 29 * K2)
        gates_late = at("gates_late", [P, 4, S], F32, big + 13 * K2)
        gates_last = at("gates_last", [P, 4, S], F32, big + 9 * K2)
        gates_end = at("gates_end", [P, 1, S], F32, big + 8 * K2)
        och = at("mem_out_high", [P, 4, S], F32R, big)
        ocl = at("mem_out_low", [P, 4, S], F32R, big + 4 * K2)
        mgh = at("merged_high", [P, DK, S], F32R, big + 18 * K2)
        mgl = at("merged_low", [P, DK, S], F32R, big + 29 * K2)
        glu = at("glu_padded", [P, 4, TAPS - 1 + S], F32, big)
        conv = at("conv_out", [P, 4, S], F32, big + 5 * K2)
        pool_in = at("pool_in", [P, 4, PADW + S], F32, big + 9 * K2)
        psum_a = at("pool_sum_a", [P, PADW + S], F32, big + 14 * K2)
        psum_b = at("pool_sum_b", [P, PADW + S], F32, big + 16 * K2)
        pooled = at("pooled", [P, 4, S], F32, big + 18 * K2)
        ymix = at("mixed", [P, DK, S], F32, big + 22 * K2)
        sig = at("glu_gate", [P, 2, S], F32, big + 30 * K2)
        wpool = at("pool_weights", [P, 4, P], F32, big + 32 * K2)

        vec = at("vectors", [P, NV], F32)
        ident = at("identity", [P, P], F32)
        ones = at("ones", [P, P], F32)
        bd = at("ones_by_head", [P, P], F32)
        rot = at("rotate_halves", [P, P], F32)
        cmask = at("causal_mask", [P, S], F32)
        rstd = at("token_factor", [P, S], F32)
        cos = at("rope_cos", [P, S], F32)
        sin = at("rope_sin", [P, S], F32)
        km = at("mem_k", [P, 4, MEM], F32)
        vm = at("mem_v", [P, MEM // P, BW], F32)
        iw = at("idx_weights", [P, QB, HEADS], F32)
        eps = at("epsilons", [P, 4], F32)
        forget = at("log_forget", [P, 2, QB, HEADS], F32)
        mx8 = at("top8", [P, 8], F32)
        stat = at("softmax_stats", [P, 3, 4], F32)
        root = at("token_root", [P, 2, QB], F32)
        t_at = base[0]
        tiles = [at(f"tile{i}", [P, S], F32) for i in range(9)]
        assert base[0] <= 229368, base[0]

        def v(name, c=0):
            o = VEC_COLS[name][0] + c
            return vec[:, o:o + 1]

        def gate_slot(g):
            if g < 15:
                return gates_own[:, g, :]
            if g < 19:
                return gates_late[:, g - 15, :]
            return gates_last[:, g - 19, :] if g < 23 else gates_end[:, 0, :]

        mem_in = at("mem_in", [P, DK, MEM], F32, big + 29 * K2)
        mem_h = at("mem_high", [P, DK, MEM], F32R, big + 33 * K2)
        mem_l = at("mem_low", [P, DK, MEM], F32R, big + 37 * K2)
        mem_rstd = at("mem_token_factor", [P, MEM], F32, big + 41 * K2)
        head_root = [at(f"head_root{i}", [P, S], F32, big + (42 + i) * K2) for i in range(2)]
        pos = at("positions_in", [P, S], I32, big + 15 * K2)
        ang, turns, turns_raw = (at(f"angle{i}", [P, S], F32, big + (16 + i) * K2) for i in range(3))
        out_t = at("out_t", [P, DK, S], F32, x_at)

        sel_at = [None, 0, 2 * P, 5 * P]

        bank = [ctx.enter_context(nc.psum_tensor(f"bank{i}", [P, S], F32)) for i in range(8)]

        sems = {}

        def sem(name):
            if name not in sems:
                sems[name] = ctx.enter_context(nc.semaphore(name))
            return sems[name]

        raw_loaded = [sem(f"raw_loaded{i}") for i in range(RAW)]
        high_done, low_done, unit_done = sem("high_done"), sem("low_done"), sem("unit_done")

        t_in, sq_in, rope_t = [tiles[i] for i in (0, 1, 2, 5)], tiles[3:5], tiles[7]
        soft, probs_t, fbias, cum = tiles[2:5], tiles[5:7], tiles[0:2], tiles[8]
        proj = [bank[0], bank[1], bank[7]]

        NORM = ("fq", "fk", "dk", "dq", "mq", "km")
        ROPE = ("iq", "ik", "dq", "dk")
        TURN = ("fv", "vm", "ik", "dk")

        INPUTS = ("ffn1", "mix", "ffn2", "mix2", "ffn3", "final")
        NORMS = ("ffn1", "mix", "mem", "ffn2", "mix2", "ln", "ffn3", "final")

        def fed(name, m):
            return INPUTS.index(name) * DK + m + 1

        def added(name, m):
            return fed(name, m) - DK

        def squares(name, m):
            return (INPUTS.index(name) + (name not in ("ffn1", "mix"))) * (DK - 1) + m

        def nth(name):
            return NORMS.index(name) + 1

        def upto_step(steps, kinds, j):
            return sum(k in kinds for k in steps[:j + 1])

        def chunk_of(steps, j):
            return steps[:j].count(steps[j])

        def tokens(kind):
            return MEM if kind in ("km", "vm") else S

        def heads(kind):
            return 1 if kind in ("mq", "km") else 2

        def chunk_id(n):
            kind, hd = ITEMS[n][:2]
            return {"fox": hd // 2, "dsa": 4 + hd // 2, "mem": 8 + hd}[kind]

        def ends_chunk(n):
            return N_IDX <= n < len(ITEMS) and (n == len(ITEMS) - 1 or chunk_id(n) != chunk_id(n + 1))

        def chunk_home(c):
            return (fq, dq, mq)[c // 4][:, c % 4, :]

        def chunk_parts(c):
            return (och[:, c - 8, :], ocl[:, c - 8, :]) if c >= 8 else (xh[:, c, :], xl[:, c, :])

        SPLIT0 = max(GATE_STEP[-1] + 2, len(ITEMS) - 4)
        SPLITS = {SPLIT0: (0, 1), SPLIT0 + 1: (2, 3), SPLIT0 + 2: (4, 5), SPLIT0 + 3: (6, 7), SPLIT0 + 4: (8,),
                  SPLIT0 + 5: (9,), SPLIT0 + 6: (10,), SPLIT0 + 7: (11,)}
        LAST = SPLIT0 + 8
        MEM_STEP = 0
        SEARCH0 = HEADS

        def gate_unit(g):
            return U_IN + len(IN_STEPS) + g

        def gates_at(n):
            return [g for g in range(GATES) if max(GATE_STEP[g] + 1, 0) == n]

        block = ctx.enter_context(nc.Block())

        @block.sync
        def _(sp):
            sp.dma_start(vec[:, :], T["vectors"]).then_inc(sem("vectors_loaded"), 16)
            for c in range(4):
                sp.dma_start(h[:, 2 * c:2 * c + 2, :], T["x_t"][:, 2 * c:2 * c + 2, :]).then_inc(sem(f"x_loaded{c}"), 16)
                if c < 2:
                    sp.dma_start(raw[:, c, :], T["weights"][c]).then_inc(raw_loaded[c], 16)
            for dst, src in ((ident, "identity"), (ones, "ones"), (bd, "ones_by_head"),
                             (rot, "rotate_halves"), (cmask, "causal_mask")):
                sp.dma_start(dst[:, :], T[src]).then_inc(sem("constants_loaded"), 16)
            for u in range(2, RAW):
                sp.dma_start(raw[:, u, :], T["weights"][u]).then_inc(raw_loaded[u], 16)
            sp.dma_start(pos[:, :], T["positions"]).then_inc(sem("positions_loaded"), 16)
            with sp.Fori(1, UNITS // RAW) as i:
                for s in range(RAW):
                    sp.wait_ge(low_done, i * RAW + (s - RAW + 1))
                    sp.dma_start(raw[:, s, :], T["weights"][bass.ds(i * RAW + s, 1)].rearrange("a p n -> p (a n)")
                                 ).then_inc(raw_loaded[s], 16)
            for m in range(DK):
                sp.wait_ge(sem("out_ready"), m + 1)
                sp.dma_start(T["out_t"][:, m, :], out_t[:, m, :]).then_inc(sem("out_stored"), 16)
            sp.wait_ge(sem("out_stored"), 16 * DK)

        @block.gpsimd
        def _(pool):
            def low_part(u, i=None):
                pool.wait_ge(high_done, u + 1 if i is None else i * RAW + (u + 1))
                pool.tensor_tensor(wl[:, u % SPL, :], raw[:, u % RAW, :], wh[:, u % SPL, :].bitcast(F32),
                                   ALU.subtract).then_inc(low_done, 1)

            def low_parts(first, end):
                start, stop = -(-first // RAW), end // RAW
                for u in range(first, start * RAW):
                    low_part(u)
                with pool.Fori(start, stop) as i:
                    for s in range(RAW):
                        low_part(s, i)
                for u in range(stop * RAW, end):
                    low_part(u)

            added_up = [0]

            def add_square(total, square):
                pool.tensor_tensor(total, total, square, ALU.add).then_inc(sem("squares_added"), 1)
                added_up[0] += 1
                pool.wait_ge(sem("squares_added"), added_up[0])

            def add_squares(name):
                for m in range(1, DK):
                    pool.wait_ge(sem("input_square"), fed(name, m))
                    add_square(tiles[0][:, :], tiles[m][:, :])

            low_part(0)
            low_part(1)
            add_squares("ffn1")
            low_parts(2, U_IN + 2)
            add_squares("mix")
            for j in range(2, len(IN_STEPS)):
                low_part(U_IN + j)
                m = j - MEM_STEP - 4
                if 1 <= m < DK:
                    pool.wait_ge(sem("mem_square"), m + 1)
                    add_square(mem_in[:, 0, :], mem_in[:, m, :])
                if m == DK:
                    break
            low_parts(U_IN + j + 1, U_GU2 + 2)
            add_squares("ffn2")
            low_parts(U_GU2 + 2, U_IN2 + 2)
            add_squares("mix2")
            low_parts(U_IN2 + 2, U_GU3 + 2)
            add_squares("ffn3")
            low_parts(U_GU3 + 2, UNITS)
            add_squares("final")

        @block.tensor
        def _(pe):
            def products(out, u, k, rh, rl, start, stop):
                w = slice(k * P, (k + 1) * P)
                pe.matmul(out, wh[:, u % SPL, w], rh, start=start, stop=False)
                pe.matmul(out, wl[:, u % SPL, w], rh, start=False, stop=False)
                return pe.matmul(out, wh[:, u % SPL, w], rl, start=False, stop=stop)

            def project(u, out, rh, rl, low_at, n=S):
                pe.wait_ge(low_done, low_at)
                for k in range(DK):
                    mm = products(out, u, k, rh[:, k, 0:n], rl[:, k, 0:n], k == 0, k == DK - 1)
                mm.then_inc(unit_done, 1)

            def spread_unit(name, u, rh, rl, low_at, first=False, last=False):
                pe.wait_ge(low_done, low_at)
                for m in (list(range(4, 8)) + list(range(4)) if first else range(DK)):
                    mm = products(bank[m][:, :], u, m, rh, rl, first, last)
                    if last and m < DK - 1:
                        mm.then_inc(sem(f"{name}_gathered"), 1)
                mm.then_inc(unit_done, 1)

            def pair_start(name, u0, out0, out1):
                for k in range(DK + 3):
                    for unit, out, c in ((u0, out0, k), (u0 + 1, out1, k - 3)):
                        if not 0 <= c < DK:
                            continue
                        if c == 0:
                            pe.wait_ge(low_done, unit + 1)
                        if unit == u0:
                            pe.wait_ge(sem("input_low"), fed(name, c))
                            if c == 0 and name != "ffn1":
                                pe.wait_ge(sem("residual_added"), added(name, 1))
                        mm = products(out, unit, c, xh[:, c, :], xl[:, c, :], c == 0, c == DK - 1)
                        if c == DK - 1:
                            mm.then_inc(unit_done, 1)
                sums(name)

            def sums(name):
                pe.wait_ge(sem("squares_added"), squares(name, DK - 1))
                for b in range(QB):
                    mm = pe.matmul(bank[4][:, b:b + 1], tiles[0][:, b * P:(b + 1) * P], ones[:, 0:1],
                                   start=True, stop=True)
                mm.then_inc(sem("norm_sum"), 1)

            def spread_factor(name):
                pe.wait_ge(sem("norm_inverse"), nth(name))
                for b in range(QB):
                    mm = pe.matmul(bank[5][:, b * P:(b + 1) * P], root[:, 1, b:b + 1].to_broadcast([P, P]),
                                   ident[:, :], start=True, stop=True)
                mm.then_inc(sem("norm_spread"), 1)

            def gate_up(name, feed, u0):
                pair_start(feed, u0, bank[0][:, :], bank[1][:, :])
                project(u0 + 2, bank[2][:, :], xh, xl, u0 + 3)
                spread_factor(feed)
                project(u0 + 3, bank[3][:, :], xh, xl, u0 + 4)
                with pe.Fori(1, FC // 2) as i:
                    for c in range(2):
                        pe.wait_ge(sem(f"{name}_banks"), i * 2 + (c - 1))
                        for g in range(2):
                            project(u0 + 2 * c + g, bank[2 * c + g][:, :], xh, xl, i * 4 + (u0 + 2 * c + g + 1))

            def down(name, feed, u0):
                pe.wait_ge(sem(f"{feed}_factor"), 1)
                pe.wait_ge(sem(f"{name}_banks"), FC)
                pe.wait_ge(sem(f"{name}_split"), FC)
                for f in range(2):
                    spread_unit(name, u0 + f, hh[:, f, :], hl[:, f, :], u0 + f + 1, first=(f == 0))
                with pe.Fori(0, (FC - 6) // 4) as i:
                    for c in range(4):
                        f = bass.ds(i * 4 + (c + 2), 1)
                        spread_unit(name, u0 + 2 + c, hh[:, f, :].rearrange("p a n -> p (a n)"),
                                    hl[:, f, :].rearrange("p a n -> p (a n)"), i * 4 + (u0 + c + 3))
                pe.wait_ge(sem(f"{name}_split"), FC + 1)
                for f in range(FC - 4, FC):
                    spread_unit(name, u0 + f, hh[:, f, :], hl[:, f, :], u0 + f + 1, last=(f == FC - 1))

            def stepped(fill):
                n_steps = len(IN_STEPS)
                for j in range(2, n_steps + FLUSH):
                    if j == 2:
                        pair_start("mix", U_IN, proj[0][:, :], proj[1][:, :])
                    if j < n_steps:
                        n = tokens(IN_STEPS[j])
                        if j >= 3:
                            pe.wait_ge(sem("in_taken"), j - 2)
                        if IN_STEPS[j] == "km" and chunk_of(IN_STEPS, j) == 0:
                            pe.wait_ge(sem("mem_low"), DK)
                        rh, rl = (mem_h, mem_l) if n == MEM else (xh, xl)
                        project(U_IN + j, proj[j % 3][:, 0:n], rh, rl, U_IN + j + 1, n)
                    else:
                        fill(FILLS[j - n_steps])
                    if j == 2:
                        spread_factor("mix")
                    for i in ((0, 1) if j == 2 else (j - 1,)):
                        if i >= n_steps:
                            continue
                        kind, n = IN_STEPS[i], tokens(IN_STEPS[i])
                        if kind in NORM:
                            k = upto_step(IN_STEPS, NORM, i)
                            pe.wait_ge(sem("in_squared"), k)
                            if k > 1:
                                pe.wait_ge(sem("in_rooted"), k - 1)
                            if j == MEM_STEP + 12:
                                pe.wait_ge(sem("norm_root"), nth("mem"))
                            pe.matmul(bank[2][:, 0:n], (bd if heads(kind) == 2 else ones)[:, :],
                                      sq_in[k % 2][:, 0:n], start=True, stop=True).then_inc(sem("in_summed"), 1)
                        if kind in TURN:
                            k = upto_step(IN_STEPS, TURN, i)
                            pe.wait_ge(sem("in_taken"), i + 1)
                            if k > 2:
                                pe.wait_ge(sem("in_turned_out"), k - 2)
                            lo = HD if kind in ("ik", "dk") else 0
                            for b in range(n // P):
                                mm = pe.transpose(bank[4 + k % 2][:, b * P:b * P + P - lo],
                                                  t_in[i % 4][lo:P, b * P:(b + 1) * P], ident[lo:P, lo:P])
                            mm.then_inc(sem("in_turned"), 1)
                    i = j - 3
                    if i >= 0 and IN_STEPS[i] in ROPE:
                        kind = IN_STEPS[i]
                        k = upto_step(IN_STEPS, ROPE, i)
                        pe.wait_ge(sem("in_taken"), i + 1)
                        if kind in NORM:
                            pe.wait_ge(sem("in_normed"), upto_step(IN_STEPS, NORM, i))
                        if k > 1:
                            pe.wait_ge(sem("in_roped"), k - 1)
                        m = HD if kind in ("dk", "ik") else P
                        pe.matmul(bank[3][0:m, :], rot[0:m, 0:m], t_in[i % 4][0:m, :], start=True, stop=True
                                  ).then_inc(sem("in_rotated"), 1)
                    if j == 4:
                        pe.wait_ge(sem("forget_logs"), 1)
                        pe.wait_ge(sem("triangle_loaded"), 16)
                        for b in range(QB):
                            mm = pe.matmul(bank[6][0:HEADS, b * P:S], forget[:, 0, b, :], tri[:, 0:S - b * P],
                                           start=(b == 0), stop=(b == QB - 1))
                        mm.then_inc(sem("forget_summed"), 1)
                    if j == 6:
                        pe.wait_ge(sem("forget_out"), 1)
                    if j == MEM_STEP + 11:
                        pe.wait_ge(sem("squares_added"), squares("mix", DK - 1) + DK - 1)
                        pe.wait_ge(sem("in_rooted"), upto_step(IN_STEPS, NORM, j - 1))
                        for b in range(MEM // P):
                            mm = pe.matmul(bank[2][:, b:b + 1], mem_in[:, 0, b * P:(b + 1) * P], ones[:, 0:1],
                                           start=True, stop=True)
                        mm.then_inc(sem("norm_sum"), 1)
                    if j == MEM_STEP + 12:
                        pe.wait_ge(sem("norm_inverse"), nth("mem"))
                        for b in range(MEM // P):
                            mm = pe.matmul(bank[6][:, b * P:(b + 1) * P], root[:, 1, b:b + 1].to_broadcast([P, P]),
                                           ident[:, :], start=True, stop=True)
                        mm.then_inc(sem("norm_spread"), 1)

            pe.wait_ge(sem("constants_loaded"), 16 * 5)
            gate_up("g1", "ffn1", U_GU1)
            down("g1", "ffn1", U_DN1)

            def gate_products():
                for g in range(GATES):
                    u = gate_unit(g)
                    if g == 0:
                        pe.wait_ge(sem("in_taken"), len(IN_STEPS))
                    for k in range(DK):
                        for part in range(3):
                            if k == 0 and part == 0:
                                pe.wait_ge(low_done, u + 1)
                                if g >= 2:
                                    pe.wait_ge(sem("gates_taken"), g - 1)
                            w = slice(k * P, (k + 1) * P)
                            mm = pe.matmul(bank[g % 2][:, :], (wl if part == 1 else wh)[:, u % SPL, w],
                                           (xl if part == 2 else xh)[:, k, :],
                                           start=(k == 0 and part == 0), stop=(k == DK - 1 and part == 2))
                            if k == DK - 1 and part == 2:
                                mm.then_inc(unit_done, 1)
                            yield

            filler = gate_products()

            def fill(n):
                for _ in range(n):
                    next(filler, None)

            stepped(fill)

            def scores(n):
                kind, hd, q, ext = ITEMS[n]
                lo = HD * (hd % 2)
                if kind == "mem":
                    left, right = mq[:, hd, q * P:(q + 1) * P], km[:, hd, 0:MEM]
                else:
                    a = {"idx": iq, "fox": fq, "dsa": dq}[kind]
                    left = a[lo:lo + HD, hd // 2, q * P:(q + 1) * P]
                    right = (fk[lo:lo + HD, hd // 2, 0:ext] if kind == "fox"
                             else (ki if kind == "idx" else kd)[lo:lo + HD, 0:ext])
                if 2 <= n < N_IDX + 2:
                    pe.wait_ge(sem("relu_done"), n - 1)
                elif n >= N_IDX + 2:
                    pe.wait_ge(sem("shifted"), n - 1 - N_IDX)
                mm = pe.matmul(bank[3 + n % 2][:, 0:ext], left, right, start=True, stop=(kind != "fox"))
                if kind == "fox":
                    mm = pe.matmul(bank[3 + n % 2][:, ext - P:ext], ident[:, :], cmask[:, S - P:S],
                                   start=False, stop=True)
                mm.then_inc(sem("scores"), 1)

            def fox_bias(hd):
                if hd:
                    pe.wait_ge(sem("bias_out"), hd)
                pe.matmul(bank[2][:, :], ident[0:HEADS, hd:hd + 1].to_broadcast([HEADS, P]), cum[0:HEADS, :],
                          start=True, stop=True).then_inc(sem("bias"), 1)

            def turn(n):
                s = n - N_IDX
                pe.wait_ge(sem("probs"), s + 1)
                if s >= 2:
                    pe.wait_ge(sem("turned_out"), s - 1)
                for b in range(ITEMS[n][3] // P):
                    mm = pe.transpose(bank[5 + s % 2][:, b * P:(b + 1) * P], soft[n % 3][:, b * P:(b + 1) * P],
                                      ident[:, :])
                mm.then_inc(sem("turned"), 1)

            def weigh(n):
                kind, hd, q, ext = ITEMS[n]
                s = n - N_IDX
                pe.wait_ge(sem("turned_out"), s + 1)
                if chunk_id(n):
                    pe.wait_ge(sem("heads_out"), chunk_id(n))
                lo, hi = (0, P) if kind == "mem" else (HD * (hd % 2), HD * (hd % 2) + HD)
                for b in range(ext // P):
                    val = {"fox": lambda: fv[:, b, hd * HD:(hd + 1) * HD], "dsa": lambda: dv[:, b, :],
                           "mem": lambda: vm[:, b, hd * P:(hd + 1) * P]}[kind]()
                    mm = pe.matmul(bank[7][lo:hi, q * P:(q + 1) * P], val, probs_t[s % 2][:, b * P:(b + 1) * P],
                                   start=(b == 0), stop=(b == ext // P - 1))
                mm.then_inc(sem("weighed"), 1)

            pe.wait_ge(sem("in_taken"), len(IN_STEPS))
            pe.wait_ge(sem("in_normed"), upto_step(IN_STEPS, NORM, 99))
            pe.wait_ge(sem("in_roped"), upto_step(IN_STEPS, ROPE, 99))
            pe.wait_ge(sem("in_turned_out"), upto_step(IN_STEPS, TURN, 99))
            pe.wait_ge(sem("shared_keys"), 32)
            for n in range(len(ITEMS) + WEIGH_LAG):
                if n < len(ITEMS):
                    kind, hd, q, _ = ITEMS[n]
                    if n == N_IDX:
                        pe.wait_ge(sem("forget_out"), 1)
                        fox_bias(0)
                    if kind == "fox" and q == 2 and hd < HEADS - 1:
                        fox_bias(hd + 1)
                    scores(n)
                k = FILLS[FLUSH + n]
                fill(k - k // 2)
                if N_IDX <= n - TURN_LAG < len(ITEMS):
                    turn(n - TURN_LAG)
                fill(k // 2)
                if n - WEIGH_LAG >= N_IDX:
                    weigh(n - WEIGH_LAG)
            for _ in filler:
                pass

            pe.wait_ge(sem("shifted"), len(ITEMS) - N_IDX)
            pe.wait_ge(sem("turned_out"), len(ITEMS) - N_IDX)
            pe.wait_ge(sem("gates_taken"), GATES)
            for m in range(DK):
                for n in range(3):
                    if n == 0 and m >= 2:
                        pe.wait_ge(sem("branches_read"), m - 1)
                    for k in range(BK):
                        b = (m * 3 + n) * BK + k
                        if b % DK == 0:
                            pe.wait_ge(low_done, U_BR + b // DK + 1)
                        if m == 0:
                            pe.wait_ge(sem("out_split"), n * BK + k + 1)
                        rh, rl, o = ((xh, xl, 0), (xh, xl, 4), (och, ocl, 0))[n]
                        mm = products(bank[3 * (m % 2) + n][:, :], U_BR + b // DK, b % DK,
                                      rh[:, o + k, :], rl[:, o + k, :], k == 0, k == BK - 1)
                        if b % DK == DK - 1:
                            mm.then_inc(unit_done, 1)
                        elif n == 2 and k == BK - 1:
                            mm.then_inc(sem("branches_even"), 1)
            pe.wait_ge(sem("branches_read"), DK)
            for f in range(N_WO):
                pe.wait_ge(sem("merged_low"), f + 1)
                spread_unit("wo", U_WO + f, mgh[:, f, :], mgl[:, f, :], U_WO + f + 1, first=(f == 0),
                            last=(f == N_WO - 1))

            gate_up("g2", "ffn2", U_GU2)
            down("g2", "ffn2", U_DN2)

            pair_start("mix2", U_IN2, proj[0][:, :], proj[1][:, :])
            for j in range(2, len(IN2_STEPS)):
                if j >= 3:
                    pe.wait_ge(sem("in2_taken"), j - 2)
                project(U_IN2 + j, proj[j % 3][:, :], xh, xl, U_IN2 + j + 1)
                if j == 2:
                    spread_factor("mix2")
            pe.wait_ge(sem("in2_taken"), len(IN2_STEPS))
            pe.wait_ge(sem("pool_weights_loaded"), 16)
            for g in range(len(WINDOWS)):
                pe.wait_ge(sem("pooled"), g + 1)
                pe.matmul(bank[2 + g][:, :], wpool[:, g, :], pooled[:, g, :], start=True, stop=True
                          ).then_inc(sem("pool_mapped"), 1)
            for c in range(4):
                pe.wait_ge(sem("conv_done"), c + 1)
                mm = pe.matmul(bank[6][:, :], ones[:, :], conv[:, c, :], start=(c == 0), stop=(c == 3))
            mm.then_inc(sem("ln_summed"), 1)
            for c in range(4):
                pe.wait_ge(sem("ln_square"), c + 1)
                for b in range(QB):
                    mm = pe.matmul(bank[7][:, b:b + 1], tiles[2 + c][:, b * P:(b + 1) * P], ones[:, 0:1],
                                   start=(c == 0 and b == 0), stop=(c == 3), skip_group_check=True)
            mm.then_inc(sem("norm_sum"), 1)
            pe.wait_ge(sem("norm_inverse"), nth("ln"))
            for b in range(QB):
                mm = pe.matmul(bank[6][:, b * P:(b + 1) * P], root[:, 1, b:b + 1].to_broadcast([P, P]),
                               ident[:, :], start=True, stop=True)
            mm.then_inc(sem("norm_spread"), 1)
            pe.wait_ge(sem("pool_out"), 4)
            pe.wait_ge(sem("ln_scaled"), 4)
            for f in range(N_WO2):
                pe.wait_ge(sem("mixed_low"), f + 1)
                f_in = (f + 4) % 8
                spread_unit("wo2", U_WO2 + f, xh[:, f_in, :], xl[:, f_in, :], U_WO2 + f + 1, first=(f == 0),
                            last=(f == N_WO2 - 1))

            gate_up("g3", "ffn3", U_GU3)
            down("g3", "ffn3", U_DN3)
            pe.wait_ge(sem("residual_added"), added("final", 4))
            sums("final")
            pe.wait_ge(sem("residual_added"), added("final", 5))
            spread_factor("final")

        @block.scalar
        def _(act):
            def high(u, i=None):
                wait, trip = (lambda c: c) if i is None else (lambda c: i * 4 + c), u // RAW + 1
                act.wait_ge(raw_loaded[u % RAW], 16 * trip if i is None else i * 16 + 16 * trip)
                if u >= SPL or i is not None:
                    act.wait_ge(unit_done, wait(u - SPL + 1))
                act.copy(wh[:, u % SPL, :], raw[:, u % RAW, :]).then_inc(high_done, 1)

            def after(u, i=None):
                if u + SPL < UNITS:
                    high(u + SPL, i=i)

            def feed_chunk(name, gain, m):
                if gain:
                    act.activation(xh[:, m, :], h[:, m, :], ACT.Copy, scale=v(gain, m)).then_inc(sem("input_high"), 1)
                act.activation(tiles[m][:, :], h[:, m, :], ACT.Square).then_inc(sem("input_square"), 1)

            def feed_root(name, src, n=QB, count=D, bias=0):
                act.wait_ge(sem("norm_sum"), nth(name))
                act.activation(root[:, 0, 0:n], src[:, 0:n], ACT.Sqrt, bias=eps[:, bias:bias + 1], scale=1.0 / count
                               ).then_inc(sem("norm_root"), 1)

            def feed(name, gain, u_last):
                for m in range(DK):
                    if m == 3:
                        after(u_last)
                    act.wait_ge(sem("residual_added"), added(name, m))
                    feed_chunk(name, gain, m)

            def stepped():
                n_steps = len(IN_STEPS)
                for j in range(n_steps + 1):
                    if j < n_steps:
                        after(U_IN + j)
                        if j == 0:
                            feed_root("mix", bank[4])
                        kind, n = IN_STEPS[j], tokens(IN_STEPS[j])
                        if kind in NORM:
                            k = upto_step(IN_STEPS, NORM, j)
                            act.wait_ge(sem("in_taken"), j + 1)
                            if k > 2:
                                act.wait_ge(sem("in_summed"), k - 2)
                            act.activation(sq_in[k % 2][:, 0:n], t_in[j % 4][:, 0:n], ACT.Square
                                           ).then_inc(sem("in_squared"), 1)
                    i = j - 1
                    if i >= 0 and IN_STEPS[i] in NORM:
                        kind, n = IN_STEPS[i], tokens(IN_STEPS[i])
                        k = upto_step(IN_STEPS, NORM, i)
                        act.wait_ge(sem("in_summed"), k)
                        if k > 2:
                            act.wait_ge(sem("in_normed"), k - 2)
                        act.activation(head_root[k % 2][:, 0:n], bank[2][:, 0:n], ACT.Sqrt, bias=eps[:, 0:1],
                                       scale=float(heads(kind)) / P).then_inc(sem("in_rooted"), 1)
                    if j == 2:
                        act.wait_ge(sem("forget_in"), 1)
                        act.activation(forget[:, 1], forget[:, 0], ACT.Abs).then_inc(sem("act_own"), 1)
                        act.wait_ge(sem("act_own"), 2)
                        act.activation(forget[:, 1], forget[:, 1], ACT.Exp, scale=-1.0).then_inc(sem("act_own"), 1)
                        act.wait_ge(sem("act_own"), 3)
                        act.activation(forget[:, 1], forget[:, 1], ACT.Ln, bias=eps[:, 3:4]
                                       ).then_inc(sem("forget_ln"), 1)
                    m = j - MEM_STEP
                    if 0 <= m < DK:
                        act.wait_ge(sem("mem_loaded"), 16)
                        act.activation(mem_h[:, m, :], mem_in[:, m, :], ACT.Copy, scale=v("mem_norm", m)
                                       ).then_inc(sem("mem_high"), 1)
                    if 0 <= m - 1 < DK:
                        act.wait_ge(sem("mem_low"), m)
                        act.activation(mem_in[:, m - 1, :], mem_in[:, m - 1, :], ACT.Square
                                       ).then_inc(sem("mem_square"), 1)
                    if m == 11:
                        feed_root("mem", bank[2], MEM // P)
                    for t, step in ((ki, 0), (kd, IN_STEPS.index("dk"))):
                        if j == step + 4:
                            act.wait_ge(sem("in_roped"), upto_step(IN_STEPS, ROPE, step))
                            act.dma_start(t[HD:P, :], t[0:HD, :]).then_inc(sem("shared_keys"), 16)

            def gate_up(name, feed_name, u0):
                def pair(i):
                    for c in range(2):
                        after(u0 + 2 * c, i)
                        if c == 0 and i is None:
                            feed_root(feed_name, bank[4])
                            after(u0 + 1)
                        one = (0 if i is None else i * 2) + (c + 1)
                        act.wait_ge(sem(f"{name}_gate"), one)
                        act.activation(tiles[c][:, :], tiles[c][:, :], ACT.Silu).then_inc(sem(f"{name}_silu"), 1)
                        if c or i is not None:
                            after(u0 + 2 * c + 1, i)
                        act.wait_ge(sem(f"{name}_act"), one)
                        f = bass.ds(i * 2 + c, 1) if i is not None else slice(c, c + 1)
                        act.copy(hh[:, f, :].rearrange("p a n -> p (a n)"), tiles[2 + c][:, :]
                                 ).then_inc(sem(f"{name}_high"), 1)

                pair(None)
                with act.Fori(1, FC // 2) as i:
                    pair(i)

            def down(u0, loads=()):
                with act.Fori(0, FC // 4) as i:
                    for c in range(4):
                        after(u0 + c, i)
                for dst, src, name in loads:
                    act.dma_start(dst, T[src]).then_inc(sem(name), 16)
                for f in range(FC // 4 * 4, FC - 1):
                    after(u0 + f)

            act.wait_ge(sem("vectors_loaded"), 16)
            for m in range(DK):
                if m % 2 == 0:
                    act.wait_ge(sem(f"x_loaded{m // 2}"), 16)
                feed_chunk("ffn1", "ffn1_norm", m)
                if m in (1, 3):
                    high(m // 2)
            act.wait_ge(sem("eps_set"), 4)
            act.wait_ge(sem("angles"), 1)
            act.activation(turns[:, :], ang[:, :], ACT.Abs).then_inc(sem("act_own"), 1)
            act.activation(sin[:, :], ang[:, :], ACT.Sin).then_inc(sem("sine"), 1)
            act.wait_ge(sem("act_own"), 1)
            act.activation(cos[:, :], turns[:, :], ACT.Sin, bias=eps[:, 2:3], scale=-1.0).then_inc(sem("sine"), 1)
            gate_up("g1", "ffn1", U_GU1)
            down(U_DN1, ((mem_in[:, :, :], "mem_t", "mem_loaded"), (tri[:, :], "triangle", "triangle_loaded")))
            feed("mix", "mix_norm", U_IN - 1)
            stepped()

            for n in range(LAST):
                for g in gates_at(n):
                    after(gate_unit(g))
                if n < N_IDX:
                    ext = ITEMS[n][3]
                    act.wait_ge(sem("scores"), n + 1)
                    if n >= 2:
                        act.wait_ge(sem("idx_added"), n - 1)
                    act.activation(soft[n % 3][:, 0:ext], bank[3 + n % 2][:, 0:ext], ACT.Relu
                                   ).then_inc(sem("relu_done"), 1)
                elif n < len(ITEMS):
                    ext, c = ITEMS[n][3], n % 4
                    act.wait_ge(sem("shifted"), n - N_IDX + 1)
                    act.activation(soft[n % 3][:, 0:ext], soft[n % 3][:, 0:ext], ACT.Exp, scale=-1.0,
                                   bias=stat[:, 0, c:c + 1], accum_out=stat[:, 1, c:c + 1]).then_inc(sem("exped"), 1)
                s = n - TURN_LAG - N_IDX
                if 0 <= s < len(ITEMS) - N_IDX:
                    ext = ITEMS[n - TURN_LAG][3]
                    act.wait_ge(sem("turned"), s + 1)
                    if s >= 2:
                        act.wait_ge(sem("weighed"), s - 1)
                    act.copy(probs_t[s % 2][:, 0:ext], bank[5 + s % 2][:, 0:ext]).then_inc(sem("turned_out"), 1)
                for c in SPLITS.get(n, ()):
                    act.wait_ge(sem("heads_out"), c + 1)
                    act.wait_ge(unit_done, U_BR)
                    if c >= 8:
                        act.wait_ge(sem("out_split"), 8)
                    act.copy(chunk_parts(c)[0], chunk_home(c)).then_inc(sem("out_high"), 1)

            def sigmoids(m):
                for n in range(3):
                    g = gate_slot(n * DK + m)
                    act.activation(g, g, ACT.Sigmoid).then_inc(sem("gate_ready"), 1)

            act.wait_ge(sem("gates_taken"), GATES)
            sigmoids(0)
            sigmoids(1)
            for u in range(U_BR, U_BR + N_BR):
                after(u)
                for m in range(DK):
                    if U_BR + (12 * m + 11) // DK == u:
                        act.wait_ge(sem("merge_summed"), m + 1)
                        act.copy(mgh[:, m, :], tiles[3 + m % 2][:, :]).then_inc(sem("merged_high"), 1)
                        if m + 2 < DK:
                            sigmoids(m + 2)
            for u in range(U_WO, U_GU2 - 1):
                after(u)
            feed("ffn2", "ffn2_norm", U_GU2 - 1)
            gate_up("g2", "ffn2", U_GU2)
            down(U_DN2, ((wpool[:, :, :], "pool_weights", "pool_weights_loaded"),))
            feed("mix2", "g_mix_2", U_IN2 - 1)
            for j, kind in enumerate(IN2_STEPS):
                after(U_IN2 + j)
                if j == 0:
                    feed_root("mix2", bank[4])
                c = chunk_of(IN2_STEPS, j)
                if kind == "s":
                    act.wait_ge(sem("in2_taken"), j + 1)
                    act.activation(sig[:, c % 2, :], sig[:, c % 2, :], ACT.Sigmoid, bias=v("b_in_2", 4 + c)
                                   ).then_inc(sem("glu_sigmoid"), 1)
                if kind == "p":
                    act.wait_ge(sem("in2_taken"), j + 1)
                    act.activation(pool_in[:, c, PADW:], pool_in[:, c, PADW:], ACT.Identity, bias=v("b_in_2", 8 + c)
                                   ).then_inc(sem("pool_biased"), 1)
            for g in range(4):
                act.wait_ge(sem("pool_mapped"), g + 1)
                act.activation(ymix[:, 4 + g, :], bank[2 + g][:, :], ACT.Copy, scale=v("s_pool_2", g)
                               ).then_inc(sem("pool_out"), 1)
                act.wait_ge(sem("pool_out"), g + 1)
                act.copy(xh[:, 4 + g, :], ymix[:, 4 + g, :]).then_inc(sem("mixed_high"), 1)
            for c in range(4):
                act.wait_ge(sem("centred"), c + 1)
                act.activation(tiles[2 + c][:, :], conv[:, c, :], ACT.Square).then_inc(sem("ln_square"), 1)
            feed_root("ln", bank[7], count=4 * P, bias=1)
            for c in range(4):
                act.wait_ge(sem("ln_scaled"), c + 1)
                act.activation(ymix[:, c, :], ymix[:, c, :], ACT.Silu, bias=v("ln_b_2", c)).then_inc(sem("ln_out"), 1)
                act.wait_ge(sem("ln_out"), c + 1)
                act.copy(xh[:, c, :], ymix[:, c, :]).then_inc(sem("mixed_high"), 1)
            for u in range(U_WO2, U_GU3 - 1):
                after(u)
            feed("ffn3", "g_ffn_2", U_GU3 - 1)
            gate_up("g3", "ffn3", U_GU3)
            down(U_DN3)
            feed("final", None, UNITS - 1)
            feed_root("final", bank[4])

        @block.vector
        def _(dve):
            owned = [0]

            def own(ins):
                owned[0] += 1
                ins.then_inc(sem("dve_own"), 1)
                dve.wait_ge(sem("dve_own"), owned[0])

            def low(name, gain, m):
                dve.wait_ge(sem("input_high"), fed(name, m))
                dve.scalar_tensor_tensor(out=xl[:, m, :], in0=h[:, m, :], scalar=v(gain, m),
                                         in1=xh[:, m, :].bitcast(F32), op0=ALU.mult, op1=ALU.subtract
                                         ).then_inc(sem("input_low"), 1)

            def inverse(name, n=QB):
                dve.wait_ge(sem("norm_root"), nth(name))
                dve.reciprocal(root[:, 1, 0:n], root[:, 0, 0:n]).then_inc(sem("norm_inverse"), 1)

            def factor(name):
                inverse(name)
                dve.wait_ge(sem("norm_spread"), nth(name))
                dve.tensor_copy(rstd[:, :], bank[5][:, :]).then_inc(sem(f"{name}_factor"), 1)
                dve.wait_ge(sem(f"{name}_factor"), 1)

            def feed(name, gain, gathered, u_last, share, parts=True):
                for m in range(DK):
                    if m < DK - 1:
                        dve.wait_ge(sem(f"{gathered}_gathered"), m + 1)
                    else:
                        dve.wait_ge(unit_done, u_last + 1)
                    dve.scalar_tensor_tensor(out=h[:, m, :], in0=bank[m][:, :], scalar=share,
                                             in1=h[:, m, :], op0=ALU.mult, op1=ALU.add
                                             ).then_inc(sem("residual_added"), 1)
                    if parts and m:
                        low(name, gain, m - 1)
                if parts:
                    low(name, gain, DK - 1)

            def gate_up(name, u0):
                dve.sem_inc(sem(f"{name}_split"), 1)
                with dve.Fori(0, FC // 2) as i:
                    for c in range(2):
                        one = i * 2 + (c + 1)
                        dve.wait_ge(unit_done, i * 4 + (u0 + 2 * c + 1))
                        dve.tensor_tensor(tiles[c][:, :], bank[2 * c][:, :], rstd[:, :], ALU.mult
                                          ).then_inc(sem(f"{name}_gate"), 1)
                        dve.wait_ge(unit_done, i * 4 + (u0 + 2 * c + 2))
                        dve.wait_ge(sem(f"{name}_split"), one)
                        dve.tensor_tensor(tiles[2 + c][:, :], bank[2 * c + 1][:, :], rstd[:, :], ALU.mult
                                          ).then_inc(sem(f"{name}_banks"), 1)
                        dve.wait_ge(sem(f"{name}_silu"), one)
                        dve.wait_ge(sem(f"{name}_banks"), one)
                        dve.tensor_tensor(tiles[2 + c][:, :], tiles[2 + c][:, :], tiles[c][:, :], ALU.mult
                                          ).then_inc(sem(f"{name}_act"), 1)
                        dve.wait_ge(sem(f"{name}_high"), one)
                        f = bass.ds(i * 2 + c, 1)
                        dve.tensor_tensor(hl[:, f, :].rearrange("p a n -> p (a n)"), tiles[2 + c][:, :],
                                          hh[:, f, :].rearrange("p a n -> p (a n)").bitcast(F32), ALU.subtract
                                          ).then_inc(sem(f"{name}_split"), 1)

            def stepped():
                n_steps = len(IN_STEPS)
                for j in range(n_steps + FLUSH):
                    if j < n_steps:
                        n = tokens(IN_STEPS[j])
                        i = j - 4
                        if i >= 0:
                            for kinds, name in ((TURN, "turned"), (NORM, "normed"), (ROPE, "roped")):
                                if IN_STEPS[i] in kinds:
                                    dve.wait_ge(sem(f"in_{name}"), upto_step(IN_STEPS, kinds, i))
                        dve.wait_ge(unit_done, U_IN + j + 1)
                        dve.tensor_tensor(t_in[j % 4][:, 0:n], proj[j % 3][:, 0:n],
                                          (mem_rstd if n == MEM else rstd)[:, 0:n], ALU.mult
                                          ).then_inc(sem("in_taken"), 1)
                    i = j - 1
                    if 0 <= i < n_steps and IN_STEPS[i] in TURN:
                        kind, n, c = IN_STEPS[i], tokens(IN_STEPS[i]), chunk_of(IN_STEPS, i)
                        k = upto_step(IN_STEPS, TURN, i)
                        dve.wait_ge(sem("in_turned"), k)
                        src = bank[4 + k % 2][:, 0:n].rearrange("p (b f) -> p b f", f=P)
                        if kind in ("fv", "vm"):
                            dst = fv if kind == "fv" else vm
                            dve.tensor_copy(dst[:, :, c * P:(c + 1) * P], src).then_inc(sem("in_turned_out"), 1)
                        elif kind == "dk":
                            dve.tensor_copy(dv[:, :, :], src[:, :, 0:HD]).then_inc(sem("in_turned_out"), 1)
                        else:
                            for b in range(QB):
                                ins = dve.tensor_tensor(forget[:, 0, b, :], src[:, b, 0:HEADS],
                                                        vec[:, VEC_COLS["b_forget"][0]:][:, 0:HEADS], ALU.add)
                            ins.then_inc(sem("forget_in"), 1)
                            dve.tensor_scalar(iw[:, :, :], src[:, :, HEADS:2 * HEADS],
                                              HEADS ** -0.5 * HD ** -0.5, None, ALU.mult
                                              ).then_inc(sem("in_turned_out"), 1)
                    i = j - 2
                    if 0 <= i < n_steps and IN_STEPS[i] in NORM:
                        kind, n, c = IN_STEPS[i], tokens(IN_STEPS[i]), chunk_of(IN_STEPS, i)
                        m = HD if kind == "dk" else P
                        t = t_in[i % 4][0:m, 0:n]
                        out = {"fq": fq, "fk": fk, "mq": mq, "km": km}[kind][:, c, :] if kind[0] != "d" else t
                        gain = ({"f": "fox_", "d": "dsa_", "m": "mem_", "k": "mem_"}[kind[0]]
                                + ("k" if kind == "km" else kind[1]) + "_norm")
                        k = upto_step(IN_STEPS, NORM, i)
                        dve.wait_ge(sem("in_inverse"), k)
                        dve.scalar_tensor_tensor(out=out, in0=t, scalar=v(gain)[0:m],
                                                 in1=head_root[k % 2][0:m, 0:n], op0=ALU.mult, op1=ALU.mult
                                                 ).then_inc(sem("in_normed"), 1)
                    i = j - 3
                    if i >= 0 and IN_STEPS[i] in ROPE:
                        k, kind, c = upto_step(IN_STEPS, ROPE, i), IN_STEPS[i], chunk_of(IN_STEPS, i)
                        m = HD if kind in ("dk", "ik") else P
                        t = t_in[i % 4][0:m, :]
                        out = {"iq": iq[:, c, :], "dq": dq[:, c, :], "ik": ki[0:HD, :], "dk": kd[0:HD, :]}[kind]
                        dve.wait_ge(sem("in_rotated"), k)
                        if k > 1:
                            dve.wait_ge(sem("in_roped"), k - 1)
                        dve.tensor_tensor(rope_t[0:m, :], bank[3][0:m, :], sin[0:m, :], ALU.mult)
                        own(dve.tensor_tensor(t, t, cos[0:m, :], ALU.mult))
                        dve.tensor_tensor(out, t, rope_t[0:m, :], ALU.add).then_inc(sem("in_roped"), 1)
                    i = j - 1
                    if 0 <= i < n_steps and IN_STEPS[i] in NORM:
                        k, n = upto_step(IN_STEPS, NORM, i), tokens(IN_STEPS[i])
                        dve.wait_ge(sem("in_rooted"), k)
                        root_k = head_root[k % 2][:, 0:n]
                        dve.reciprocal(root_k, root_k).then_inc(sem("in_inverse"), 1)
                    if j == 2:
                        dve.wait_ge(sem("forget_ln"), 1)
                        dve.scalar_tensor_tensor(out=forget[:, 0].rearrange("p b h -> p (b h)"),
                                                 in0=forget[:, 0].rearrange("p b h -> p (b h)"), scalar=0.0,
                                                 in1=forget[:, 1].rearrange("p b h -> p (b h)"),
                                                 op0=ALU.min, op1=ALU.subtract).then_inc(sem("forget_logs"), 1)
                    if j == 5:
                        dve.wait_ge(sem("forget_summed"), 1)
                        dve.tensor_copy(cum[0:HEADS, :], bank[6][0:HEADS, :]).then_inc(sem("forget_out"), 1)
                    m = j - MEM_STEP
                    if 0 <= m < DK:
                        dve.wait_ge(sem("mem_high"), m + 1)
                        dve.scalar_tensor_tensor(out=mem_l[:, m, :], in0=mem_in[:, m, :], scalar=v("mem_norm", m),
                                                 in1=mem_h[:, m, :].bitcast(F32), op0=ALU.mult, op1=ALU.subtract
                                                 ).then_inc(sem("mem_low"), 1)
                    if m == 12:
                        inverse("mem", MEM // P)
                        dve.wait_ge(sem("norm_spread"), nth("mem"))
                        dve.tensor_copy(mem_rstd[:, :], bank[6][:, 0:MEM]).then_inc(sem("mem_factor"), 1)
                        dve.wait_ge(sem("mem_factor"), 1)

            for c, val in enumerate((EPS, LN_EPS, float(np.pi / 2), 1.0)):
                dve.memset(eps[:, c:c + 1], val).then_inc(sem("eps_set"), 1)
            dve.wait_ge(sem("vectors_loaded"), 16)
            for name, scale in (("fox_q_norm", HD ** -0.5), ("dsa_q_norm", HD ** -0.5), ("mem_q_norm", P ** -0.5)):
                own(dve.tensor_scalar(v(name), v(name), scale, None, ALU.mult))
            dve.wait_ge(sem("positions_loaded"), 16)
            own(dve.tensor_copy(turns[:, :], pos[:, :]))
            own(dve.tensor_scalar(ang[:, :], turns[:, :], v("inv_freq"), None, ALU.mult))
            own(dve.tensor_scalar(turns_raw[:, :], ang[:, :], 1.0 / TURN_RAD, ROUNDER, ALU.mult, ALU.add))
            own(dve.tensor_scalar(turns[:, :], turns_raw[:, :], -ROUNDER, None, ALU.add))
            for part in TURN_PARTS:
                own(dve.scalar_tensor_tensor(out=ang[:, :], in0=turns[:, :], scalar=-part, in1=ang[:, :],
                                             op0=ALU.mult, op1=ALU.add))
            dve.tensor_scalar(ang[:, :], ang[:, :], PI_BELOW, -PI_BELOW, ALU.min, ALU.max
                              ).then_inc(sem("angles"), 1)
            for m in range(DK):
                low("ffn1", "ffn1_norm", m)
            dve.wait_ge(sem("sine"), 2)
            factor("ffn1")
            gate_up("g1", U_GU1)
            feed("mix", "mix_norm", "g1", U_IN - 1, 0.5)
            factor("mix")
            stepped()

            def bias(hd):
                dve.wait_ge(sem("bias"), hd + 1)
                dve.tensor_scalar(fbias[hd % 2][:, :], bank[2][:, :], -1.0, None, ALU.mult
                                  ).then_inc(sem("bias_out"), 1)

            def kept(q):
                return sel[:, sel_at[q]:sel_at[q] + (q + 1) * P]

            def search(r):
                q, r = 1 + r // ROUNDS, r % ROUNDS
                own(dve.max(mx8[:, :], kept(q)))
                own(dve.match_replace(kept(q), mx8[:, :], kept(q), TAKEN))
                if r == ROUNDS - 1:
                    own(dve.tensor_scalar(kept(q), kept(q), TAKEN / 2, MASKED, ALU.is_gt, ALU.mult))

            def shift(n):
                kind, hd, q, ext = ITEMS[n]
                s, c = n - N_IDX, n % 4
                if kind == "fox":
                    add = fbias[hd % 2][:, 0:ext]
                    dve.wait_ge(sem("bias_out"), hd + 1)
                elif kind == "dsa":
                    add = kept(q) if q else cmask[:, S - P:S]
                else:
                    add = cmask[:, 0:ext]
                dve.wait_ge(sem("scores"), n + 1)
                if s >= 3:
                    dve.wait_ge(sem("turned"), s - 2)
                dve.tensor_tensor_reduce(soft[n % 3][:, 0:ext], bank[3 + n % 2][:, 0:ext], add, -1.0, 3.0e38,
                                         ALU.add, ALU.min, stat[:, 0, c:c + 1]).then_inc(sem("shifted"), 1)

            def normalise(n):
                ext, s, c = ITEMS[n][3], n - N_IDX, n % 4
                dve.wait_ge(sem("exped"), s + 1)
                own(dve.reciprocal(stat[:, 2, c:c + 1], stat[:, 1, c:c + 1]))
                dve.tensor_scalar(soft[n % 3][:, 0:ext], soft[n % 3][:, 0:ext], stat[:, 2, c:c + 1], None,
                                  ALU.mult).then_inc(sem("probs"), 1)

            dve.wait_ge(sem("in_roped"), upto_step(IN_STEPS, ROPE, 99))
            dve.wait_ge(sem("in_normed"), upto_step(IN_STEPS, NORM, 99))
            dve.wait_ge(sem("in_turned_out"), upto_step(IN_STEPS, TURN, 99))
            pending = []
            for n in range(LAST + 1):
                if N_IDX <= n - 1 < len(ITEMS):
                    normalise(n - 1)
                if n < len(ITEMS):
                    kind, hd, q, ext = ITEMS[n]
                    if n == N_IDX:
                        bias(0)
                    if kind == "fox" and q == 3 and hd < HEADS - 1:
                        bias(hd + 1)
                    if kind == "idx":
                        dve.wait_ge(sem("relu_done"), n + 1)
                        dve.scalar_tensor_tensor(out=kept(q), in0=soft[n % 3][:, 0:ext], scalar=iw[:, q, hd:hd + 1],
                                                 in1=kept(q) if hd else cmask[:, S - ext:S],
                                                 op0=ALU.mult, op1=ALU.add).then_inc(sem("idx_added"), 1)
                        dve.wait_ge(sem("idx_added"), n + 1)
                    else:
                        shift(n)
                for g in gates_at(n):
                    dve.wait_ge(unit_done, gate_unit(g) + 1)
                    dve.tensor_tensor(gate_slot(g), bank[g % 2][:, :], rstd[:, :], ALU.mult
                                      ).then_inc(sem("gates_taken"), 1)
                if ends_chunk(n - WEIGH_LAG - 1):
                    c = chunk_id(n - WEIGH_LAG - 1)
                    dve.wait_ge(sem("weighed"), n - WEIGH_LAG - N_IDX)
                    dve.tensor_copy(chunk_home(c), bank[7][:, :]).then_inc(sem("heads_out"), 1)
                for c in pending:
                    dve.wait_ge(sem("out_high"), c + 1)
                    hi, lo_ = chunk_parts(c)
                    dve.tensor_tensor(lo_, chunk_home(c), hi.bitcast(F32), ALU.subtract
                                      ).then_inc(sem("out_split"), 1)
                pending = SPLITS.get(n, ())
                if SEARCH0 <= n < SEARCH0 + (QB - 1) * ROUNDS:
                    search(n - SEARCH0)

            def merge_low(m):
                dve.wait_ge(sem("merged_high"), m + 1)
                dve.tensor_tensor(mgl[:, m, :], tiles[3 + m % 2][:, :], mgh[:, m, :].bitcast(F32), ALU.subtract
                                  ).then_inc(sem("merged_low"), 1)

            for m in range(DK):
                dve.wait_ge(sem("gate_ready"), 3 * (m + 1))
                if m % 2:
                    dve.wait_ge(unit_done, U_BR + (12 * m + 11) // DK + 1)
                else:
                    dve.wait_ge(sem("branches_even"), m // 2 + 1)
                for n in range(3):
                    ins = dve.tensor_tensor(tiles[n][:, :], bank[3 * (m % 2) + n][:, :], gate_slot(n * DK + m),
                                            ALU.mult)
                ins.then_inc(sem("branches_read"), 1)
                dve.wait_ge(sem("branches_read"), m + 1)
                own(dve.tensor_tensor(tiles[0][:, :], tiles[0][:, :], tiles[1][:, :], ALU.add))
                if m >= 2:
                    dve.wait_ge(sem("merged_low"), m - 1)
                dve.tensor_tensor(tiles[3 + m % 2][:, :], tiles[0][:, :], tiles[2][:, :], ALU.add
                                  ).then_inc(sem("merge_summed"), 1)
                merge_low(m)
            feed("ffn2", "ffn2_norm", "wo", U_GU2 - 1, 1.0)
            factor("ffn2")
            gate_up("g2", U_GU2)
            feed("mix2", "g_mix_2", "g2", U_IN2 - 1, 0.5)
            factor("mix2")

            for c in range(4):
                dve.memset(glu[:, c, 0:TAPS - 1], 0.0)
                dve.memset(pool_in[:, c, 0:PADW], 0.0)
            dve.memset(psum_a[:, 0:PADW], 0.0)
            own(dve.memset(psum_b[:, 0:PADW], 0.0))

            def taps():
                for c in range(4):
                    for k in range(TAPS):
                        w = v("w_dw_2", c * TAPS + k)
                        src = glu[:, c, k:k + S]
                        if k == 0:
                            own(dve.tensor_scalar(conv[:, c, :], src, w, v("b_dw_2", c), ALU.mult, ALU.add))
                        elif k < TAPS - 1:
                            own(dve.scalar_tensor_tensor(out=conv[:, c, :], in0=src, scalar=w, in1=conv[:, c, :],
                                                         op0=ALU.mult, op1=ALU.add))
                        else:
                            dve.scalar_tensor_tensor(out=conv[:, c, :], in0=src, scalar=w, in1=conv[:, c, :],
                                                     op0=ALU.mult, op1=ALU.add).then_inc(sem("conv_done"), 1)
                            dve.wait_ge(sem("conv_done"), c + 1)
                        yield c

            conv_taps, done = taps(), 0
            for j, kind in enumerate(IN2_STEPS):
                c = chunk_of(IN2_STEPS, j)
                out = {"a": tiles[c % 2][:, :], "s": sig[:, c % 2, :], "p": pool_in[:, c, PADW:]}[kind]
                dve.wait_ge(unit_done, U_IN2 + j + 1)
                dve.tensor_tensor(out, proj[j % 3][:, :], rstd[:, :], ALU.mult).then_inc(sem("in2_taken"), 1)
                if kind == "s":
                    dve.wait_ge(sem("glu_sigmoid"), c + 1)
                    own(dve.scalar_tensor_tensor(out=glu[:, c, TAPS - 1:], in0=tiles[c % 2][:, :],
                                                 scalar=v("b_in_2", c), in1=sig[:, c % 2, :],
                                                 op0=ALU.add, op1=ALU.mult))
                ready = TAPS * sum(k == "s" for k in IN2_STEPS[:j + 1])
                for _ in range(min(7, ready - done)):
                    next(conv_taps)
                    done += 1
            for g, width in enumerate(WINDOWS):
                dve.wait_ge(sem("pool_biased"), g + 1)
                if g:
                    dve.wait_ge(sem("pooled"), g)
                src, shift_by, k = pool_in[:, g, :], 1, 0
                while shift_by < width:
                    dst = (psum_a, psum_b)[k % 2]
                    own(dve.tensor_tensor(dst[:, PADW:], src[:, PADW:], src[:, PADW - shift_by:PADW - shift_by + S],
                                          ALU.add))
                    src, shift_by, k = dst, shift_by * 2, k + 1
                o = VEC_COLS["pool_inv"][0] + g * PADW
                own(dve.tensor_tensor(src[:, PADW:2 * PADW], src[:, PADW:2 * PADW], vec[:, o:o + PADW], ALU.mult))
                own(dve.tensor_scalar(src[:, 2 * PADW:], src[:, 2 * PADW:], 1.0 / width, None, ALU.mult))
                dve.tensor_tensor(pooled[:, g, :], src[:, PADW:], pool_in[:, g, PADW:], ALU.subtract
                                  ).then_inc(sem("pooled"), 1)
            for g in range(4):
                dve.wait_ge(sem("mixed_high"), g + 1)
                dve.tensor_tensor(xl[:, 4 + g, :], ymix[:, 4 + g, :], xh[:, 4 + g, :].bitcast(F32), ALU.subtract
                                  ).then_inc(sem("mixed_low"), 1)
            for _ in conv_taps:
                pass
            dve.wait_ge(sem("ln_summed"), 1)
            own(dve.tensor_scalar(tiles[0][:, :], bank[6][:, :], 1.0 / (4 * P), None, ALU.mult))
            for c in range(4):
                dve.tensor_tensor(conv[:, c, :], conv[:, c, :], tiles[0][:, :], ALU.subtract
                                  ).then_inc(sem("centred"), 1)
            inverse("ln")
            dve.wait_ge(sem("norm_spread"), nth("ln"))
            for c in range(4):
                dve.wait_ge(sem("centred"), c + 1)
                dve.scalar_tensor_tensor(out=ymix[:, c, :], in0=conv[:, c, :], scalar=v("ln_g_2", c),
                                         in1=bank[6][:, :], op0=ALU.mult, op1=ALU.mult
                                         ).then_inc(sem("ln_scaled"), 1)
            for c in range(4):
                dve.wait_ge(sem("mixed_high"), 4 + c + 1)
                dve.tensor_tensor(xl[:, c, :], ymix[:, c, :], xh[:, c, :].bitcast(F32), ALU.subtract
                                  ).then_inc(sem("mixed_low"), 1)
            feed("ffn3", "g_ffn_2", "wo2", U_GU3 - 1, 1.0)
            factor("ffn3")
            gate_up("g3", U_GU3)
            feed("final", None, "g3", UNITS - 1, 1.0, parts=False)
            factor("final")
            for m in range(DK):
                dve.scalar_tensor_tensor(out=out_t[:, m, :], in0=h[:, m, :], scalar=v("g_final_2", m),
                                         in1=rstd[:, :], op0=ALU.mult, op1=ALU.mult
                                         ).then_inc(sem("out_ready"), 1)



def column_units(w):
    n = w.shape[1] // P
    return w.reshape(DK, P, n, P).transpose(2, 1, 0, 3).reshape(n, P, DK * P)


def row_units(w):
    return w.reshape(-1, P, D)


def gate_up_units(gate, up):
    g, u = column_units(gate), column_units(up)
    return np.stack([g, u], axis=1).reshape(-1, P, DK * P)


def in_units(w, w_mem):
    sizes = (BW, BW, BW, HEADS, BW, HD, HD, BW, HD, HEADS, BW, 3 * D)
    fq, fk, fv, ff, dq, dk, dv, iq, ik, iw, mq, g = np.split(w, np.cumsum(sizes)[:-1], axis=1)
    pad = np.zeros((D, P - HD - 2 * HEADS), w.dtype)
    cols = {"ik": np.concatenate([ik, ff, iw, pad], axis=1), "dk": np.concatenate([dk, dv], axis=1),
            "iq": iq, "fq": fq, "fk": fk, "fv": fv, "dq": dq, "mq": mq, "km": w_mem[:, :BW], "vm": w_mem[:, BW:]}
    units = {k: column_units(x) for k, x in cols.items()}
    steps = [units[k][IN_STEPS[:j].count(k)] for j, k in enumerate(IN_STEPS)]
    return np.concatenate([np.stack(steps), column_units(g)])


def branch_units(w):
    b = w.reshape(3, BK, P, DK, P).transpose(3, 0, 1, 2, 4).reshape(-1, P, P)
    return b.reshape(N_BR, DK, P, P).transpose(0, 2, 1, 3).reshape(N_BR, P, DK * P)


def pair_units(w):
    u = column_units(w)
    order = [x for c in range(4) for x in (c, 4 + c)] + [8, 9, 10, 11]
    return u[order]


def by_chunk(x):
    return np.ascontiguousarray(x.T.reshape(DK, P, -1).transpose(1, 0, 2))


def vectors(a):
    out = np.zeros((P, NV), np.float32)

    def put(name, cols):
        o, n = VEC_COLS[name]
        out[:, o:o + n] = cols

    for name in ("ffn1_norm", "mix_norm", "mem_norm", "ffn2_norm", "g_mix_2", "g_ffn_2"):
        put(name, a[name][0].reshape(-1, P).T)
    put("g_final_2", a["g_final_2"].reshape(-1, P).T)
    for name in ("fox_q_norm", "fox_k_norm", "dsa_q_norm", "dsa_k_norm"):
        put(name, np.tile(a[name][0], 2)[:, None])
    for name in ("mem_q_norm", "mem_k_norm"):
        put(name, a[name][0][:, None])
    put("b_forget", np.broadcast_to(a["b_forget"][0], (P, HEADS)))
    for name in ("b_in_2", "b_dw_2", "ln_g_2", "ln_b_2", "s_pool_2"):
        put(name, a[name][0].reshape(-1, P).T)
    put("w_dw_2", a["w_dw_2"][0].reshape(TAPS, 4, P).transpose(2, 1, 0).reshape(P, 4 * TAPS))
    put("inv_freq", np.tile(inverse_frequencies(), 4)[:, None])
    t = np.arange(PADW)
    put("pool_inv", np.broadcast_to(np.concatenate([1.0 / np.minimum(t + 1, w) for w in WINDOWS]), (P, 4 * PADW)))
    return out


def inverse_frequencies():
    return np.float32(10000.0) ** (-np.arange(0, HD, 2, dtype=np.float32) / np.float32(HD))


def constants():
    i = np.arange(P)
    ident = np.eye(P, dtype=np.float32)
    by_head = (i[:, None] // HD == i[None, :] // HD).astype(np.float32)
    rot = np.zeros((P, P), np.float32)
    for m in range(P):
        first = m % HD < HD // 2
        rot[m + HD // 2 if first else m - HD // 2, m] = -1.0 if first else 1.0
    mask = np.zeros((P, S), np.float32)
    mask[:, S - P:] = np.where(i[None, :] <= i[:, None], 0.0, MASKED)
    tri = np.ones((P, S), np.float32)
    tri[:, :P] = i[:, None] <= i[None, :]
    return {"identity": ident, "ones": np.ones((P, P), np.float32), "ones_by_head": by_head,
            "rotate_halves": rot, "causal_mask": mask, "triangle": tri}


def kernel(**inputs):
    import concourse.bacc as bacc
    from concourse.bass_utils import run_bass_kernel_spmd as run

    a = {k: np.asarray(x) for k, x in inputs.items()}
    stream = np.concatenate([
        gate_up_units(a["ffn1_w_gate"][0], a["ffn1_w_up"][0]), row_units(a["ffn1_w_down"][0]),
        in_units(a["w_in"][0], a["w_mem_kv"][0]), branch_units(a["w_branch"][0]), row_units(a["w_out"][0]),
        gate_up_units(a["ffn2_w_gate"][0], a["ffn2_w_up"][0]), row_units(a["ffn2_w_down"][0]),
        pair_units(a["w_in_2"][0]), row_units(a["w_out_2"][0])[[4, 5, 6, 7, 0, 1, 2, 3]],
        gate_up_units(a["w_gate_2"][0], a["w_up_2"][0]), row_units(a["w_down_2"][0]),
    ])
    arrays = {
        "weights": np.ascontiguousarray(stream),
        "x_t": by_chunk(a["x"][0]),
        "mem_t": by_chunk(a["mem"][0]),
        "positions": np.ascontiguousarray(np.broadcast_to(a["positions"], (P, S))),
        "pool_weights": np.ascontiguousarray(a["w_pool_2"][0].transpose(1, 0, 2)),
        "vectors": vectors(a),
        **constants(),
    }
    nc = bacc.Bacc("TRN2", target_bir_lowering=False, num_devices=1)
    T = {n: nc.dram_tensor(n, x.shape, mybir.dt.from_np(x.dtype), kind="ExternalInput").ap()
         for n, x in arrays.items()}
    T["out_t"] = nc.dram_tensor("out_t", (P, DK, S), F32, kind="ExternalOutput").ap()
    build(nc, T)
    r = run(nc, [arrays], core_ids=[0])
    got = r.results[0]["out_t"]
    return np.ascontiguousarray(got.transpose(2, 1, 0).reshape(1, S, D))
```

```python
from contextlib import ExitStack

import numpy as np

import concourse.bass as bass
from concourse import mybir

ALU = mybir.AluOpType
ACT = mybir.ActivationFunctionType
F32 = mybir.dt.float32
F32R = mybir.dt.float32r
I32 = mybir.dt.int32

P = 128
D = 1024
S = 512
MEM = 256
DK = D // P
BW = 512
BK = BW // P
HEADS = 8
HD = 64
MHEADS = 4
FF = 2816
FC = FF // P
QB = S // P
TOPK = min(256, S // 4)
TAPS = 31
WINDOWS = (2, 4, 8, 16)
PADW = WINDOWS[-1]
EPS = 1e-6
LN_EPS = 1e-5
MASKED = -1.0e30
TAKEN = -3.0e38
TURN_RAD = float(2 * np.pi)
TURN_PARTS = (6.28125, 0.0019378662109375, -2.562999725341797e-06, 3.968374517882012e-09)
ROUNDER = 1.5 * 2.0 ** 23
PI_BELOW = 3.1415925
RAW = 4
SPL = 2

IN_STEPS = (["ik"] + ["fq"] * 4 + ["fk"] * 4 + ["iq", "mq", "iq", "dq"] + ["fv", "km", "vm", "dq"] * 3
            + ["fv", "km", "vm", "dk", "mq", "iq", "mq", "mq", "iq"])
GATES = 3 * DK

N_GU, N_DN, N_IN, N_BR, N_WO, N_IN2, N_WO2 = 2 * FC, FC, len(IN_STEPS) + GATES, 12, 8, 12, 8
U_GU1 = 0
U_DN1 = U_GU1 + N_GU
U_IN = U_DN1 + N_DN
U_BR = U_IN + N_IN
U_WO = U_BR + N_BR
U_GU2 = U_WO + N_WO
U_DN2 = U_GU2 + N_GU
U_IN2 = U_DN2 + N_DN
U_WO2 = U_IN2 + N_IN2
U_GU3 = U_WO2 + N_WO2
U_DN3 = U_GU3 + N_GU
UNITS = U_DN3 + N_DN

VEC_COLS = {}
for _name, _n in (("ffn1_norm", 8), ("mix_norm", 8), ("mem_norm", 8), ("ffn2_norm", 8), ("g_mix_2", 8),
                  ("g_ffn_2", 8), ("g_final_2", 8), ("fox_q_norm", 1), ("fox_k_norm", 1), ("dsa_q_norm", 1),
                  ("dsa_k_norm", 1), ("mem_q_norm", 1), ("mem_k_norm", 1), ("b_forget", HEADS), ("b_in_2", 12),
                  ("w_dw_2", 4 * TAPS), ("b_dw_2", 4), ("ln_g_2", 4), ("ln_b_2", 4), ("s_pool_2", 4),
                  ("inv_freq", 1), ("pool_inv", len(WINDOWS) * PADW)):
    VEC_COLS[_name] = (sum(n for _, n in VEC_COLS.values()), _n)
NV = sum(n for _, n in VEC_COLS.values())

IN2_STEPS = ["a", "s"] * 4 + ["p"] * 4
POOL_TAPS = {0: range(6, TAPS)}
PE_TAPS = {3: range(3, TAPS)}
DVE_TAPS = {c: range(POOL_TAPS.get(c, PE_TAPS.get(c, range(TAPS, TAPS))).start) for c in range(4)}
DVE_STEP_TAPS = 6
DVE_WINDOW_TAPS = 3
POOL_STEP_TAPS = 2
DVE_LAST_TAPS = 8
BEFORE_MAPS = 12

ITEMS = ([("idx", h, q, (q + 1) * P) for q in range(1, QB) for h in range(HEADS)]
         + [("fox", h, q, (q + 1) * P) for h in range(HEADS) for q in range(QB)]
         + [("dsa", h, q, (q + 1) * P) for h in range(HEADS) for q in range(QB)]
         + [("mem", h, q, MEM) for h in range(MHEADS) for q in range(QB)])
N_IDX = sum(it[0] == "idx" for it in ITEMS)
TURN_LAG, WEIGH_LAG = 2, 4
ROUNDS = TOPK // 8
FLUSH = 3
FILLS = [14, 14, 20] + [{"idx": 6, "fox": 5, "dsa": 5, "mem": 4}[it[0]] for it in ITEMS] + [0] * WEIGH_LAG
GATE_MM = 3 * DK


POOL_HALF = [(k, m) for k in range(4, DK) for m in range(2, DK)] + [(k, m) for k in range(4, DK) for m in range(2)]


def gate_steps():
    done, out = 0, []
    for n, k in enumerate(FILLS):
        done += k
        while len(out) < GATES and done >= GATE_MM * (len(out) + 1):
            out.append(n - FLUSH)
    return out + [len(ITEMS) + WEIGH_LAG - 1] * (GATES - len(out))


GATE_STEP = gate_steps()
LAST_READ = [next(n for n in range(len(FILLS)) if sum(FILLS[:n + 1]) >= GATE_MM * (GATES - 1) + 3 * k + 3) - FLUSH
             for k in range(DK)]


def build(nc, T):
    ctx = ExitStack()
    with ctx:
        base = [16512]

        def at(name, shape, dt, offset=None):
            size = int(np.prod(shape[1:])) * 4
            if offset is None:
                offset = base[0]
                base[0] += size + (-size) % 32
            return nc.alloc_sbuf_tensor_at(name, shape, dt, offset=offset)

        raw = at("raw_weights", [P, RAW, DK * P], F32)
        wh = at("weights_high", [P, SPL, DK * P], F32R)
        wl = at("weights_low", [P, SPL, DK * P], F32R)
        h = at("residual", [P, DK, S], F32)
        x_at = base[0]
        xh = at("input_high", [P, DK, S], F32R)
        xl = at("input_low", [P, DK, S], F32R)
        big = base[0]
        base[0] += 2 * FC * S * 4
        hh = at("hidden_high", [P, FC, S], F32R, big)
        hl = at("hidden_low", [P, FC, S], F32R, big + FC * S * 4)
        K2 = S * 4
        fq = at("fox_q", [P, 4, S], F32, big)
        kd = at("dsa_k", [P, S], F32, big + 4 * K2)
        fv = at("fox_v", [P, QB, BW], F32, big + 5 * K2)
        fk = at("fox_k", [P, 4, S], F32, big + 9 * K2)
        iq = at("idx_q", [P, 4, S], F32, big + 13 * K2)
        ki = at("idx_k", [P, S], F32, big + 17 * K2)
        dq = at("dsa_q", [P, 4, S], F32, big + 18 * K2)
        mq = at("mem_q", [P, 4, S], F32, big + 22 * K2)
        dv = at("dsa_v", [P, QB, HD], F32, big + 26 * K2)
        sel = at("top_keys", [P, 9 * P], F32, big + 26 * K2 + 1024)
        tri = at("triangle", [P, S], F32, big + 26 * K2 + 1024)
        gates_own = at("gates", [P, 15, S], F32, big + 29 * K2)
        gates_late = at("gates_late", [P, 4, S], F32, big + 13 * K2)
        gates_last = at("gates_last", [P, 4, S], F32, big + 9 * K2)
        gates_end = at("gates_end", [P, 1, S], F32, big + 8 * K2)
        och = at("mem_out_high", [P, 4, S], F32R, big)
        ocl = at("mem_out_low", [P, 4, S], F32R, big + 4 * K2)
        mgh = at("merged_high", [P, DK, S], F32R, big + 18 * K2)
        mgl = at("merged_low", [P, DK, S], F32R, big + 29 * K2)
        glu = at("glu_padded", [P, 4, TAPS - 1 + S], F32, big)
        conv = at("conv_out", [P, 4, S], F32, big + 5 * K2)
        pool_in = at("pool_in", [P, 4, PADW + S], F32, big + 9 * K2)
        psum_a = at("pool_sum_a", [P, PADW + S], F32, big + 14 * K2)
        psum_b = at("pool_sum_b", [P, PADW + S], F32, big + 16 * K2)
        pooled = at("pooled", [P, 4, S], F32, big + 18 * K2)
        ymix = at("mixed", [P, DK, S], F32, big + 22 * K2)
        sig = at("glu_gate", [P, 2, S], F32, big + 30 * K2)
        diagonals = at("tap_diagonals", [P, sum(len(t) for t in PE_TAPS.values()), P], F32, big + 33 * K2)
        wpool = at("pool_weights", [P, 4, P], F32, big + 32 * K2)

        vec = at("vectors", [P, NV], F32)
        ident = at("identity", [P, P], F32)
        ones = at("ones", [P, P], F32)
        bd = at("ones_by_head", [P, P], F32)
        cmask = at("causal_mask", [P, S], F32)
        rstd = at("token_factor", [P, S], F32)
        cos = at("rope_cos", [P, S], F32)
        sin = at("rope_sin", [P, S], F32)
        km = at("mem_k", [P, 4, MEM], F32)
        vm = at("mem_v", [P, MEM // P, BW], F32)
        iw = at("idx_weights", [P, QB, HEADS], F32)
        eps = at("epsilons", [P, 4], F32)
        forget = at("log_forget", [P, 2, QB, HEADS], F32)
        mx8 = at("top8", [P, 8], F32)
        stat = at("softmax_stats", [P, 3, 4], F32)
        root = at("token_root", [P, 2, QB], F32)
        t_at = base[0]
        tiles = [at(f"tile{i}", [P, S], F32) for i in range(9)]
        ident_r = at("identity_rounded", [P, P], F32R)
        mask_r = at("causal_mask_rounded", [P, P], F32R, big + 28 * K2 + 1536)
        assert base[0] <= 229368, base[0]

        def v(name, c=0):
            o = VEC_COLS[name][0] + c
            return vec[:, o:o + 1]

        def gate_slot(g):
            if g < 15:
                return gates_own[:, g, :]
            if g < 19:
                return gates_late[:, g - 15, :]
            return gates_last[:, g - 19, :] if g < 23 else gates_end[:, 0, :]

        mem_in = at("mem_in", [P, DK, MEM], F32, big + 29 * K2)
        mem_h = at("mem_high", [P, DK, MEM], F32R, big + 33 * K2)
        mem_l = at("mem_low", [P, DK, MEM], F32R, big + 37 * K2)
        mem_rstd = at("mem_token_factor", [P, MEM], F32, big + 41 * K2)
        head_root = [at(f"head_root{i}", [P, S], F32, big + (42 + i) * K2) for i in range(2)]
        pos = at("positions_in", [P, S], I32, t_at + 8 * K2)
        ang, turns, turns_raw = tiles[4:7]
        out_t = at("out_t", [P, DK, S], F32, x_at)

        sel_at = [None, 0, 2 * P, 5 * P]

        bank = [ctx.enter_context(nc.psum_tensor(f"bank{i}", [P, S], F32)) for i in range(8)]

        sems = {}

        def sem(name):
            if name not in sems:
                sems[name] = ctx.enter_context(nc.semaphore(name))
            return sems[name]

        raw_loaded = [sem(f"raw_loaded{i}") for i in range(RAW)]
        high_done, low_done, unit_done = sem("high_done"), sem("low_done"), sem("unit_done")

        t_in, sq_in, halves = [tiles[i] for i in (0, 1, 2, 5)], tiles[3:5], tiles[6:8]
        soft, probs_t, fbias, cum = tiles[2:5], tiles[5:7], tiles[0:2], tiles[8]
        proj = [bank[0], bank[1], bank[7]]

        scaled, conv_pool = tiles[4:8], tiles[8]
        ln_mean, ln_sq = tiles[0][:, :], [tiles[1][:, :], tiles[2][:, :], tiles[3][:, :], sig[:, 0, :]]

        NORM = ("fq", "fk", "dk", "dq", "mq", "km")
        ROPE = ("iq", "ik", "dq", "dk")
        TURN = ("fv", "vm", "ik", "dk")

        INPUTS = ("ffn1", "mix", "ffn2", "mix2", "ffn3", "final")
        NORMS = ("ffn1", "mix", "mem", "ffn2", "mix2", "ln", "ffn3", "final")

        def fed(name, m):
            return INPUTS.index(name) * DK + m + 1

        def added(name, m):
            return fed(name, m) - DK

        def squares(name):
            return (INPUTS.index(name) + 1) * (POOL_SQUARES - 1) + (DK - 1) * (name not in ("ffn1", "mix"))

        def nth(name):
            return NORMS.index(name) + 1

        def upto_step(steps, kinds, j):
            return sum(k in kinds for k in steps[:j + 1])

        def chunk_of(steps, j):
            return steps[:j].count(steps[j])

        def tokens(kind):
            return MEM if kind in ("km", "vm") else S

        def heads(kind):
            return 1 if kind in ("mq", "km") else 2

        def chunk_id(n):
            kind, hd = ITEMS[n][:2]
            return {"fox": hd // 2, "dsa": 4 + hd // 2, "mem": 8 + hd}[kind]

        def heads_bank(c):
            return bank[7 if c % 2 else 2]

        def ends_chunk(n):
            return N_IDX <= n < len(ITEMS) and (n == len(ITEMS) - 1 or chunk_id(n) != chunk_id(n + 1))

        def chunk_home(c):
            return (fq, dq, mq)[c // 4][:, c % 4, :]

        def chunk_parts(c):
            return (och[:, c - 8, :], ocl[:, c - 8, :]) if c >= 8 else (xh[:, c, :], xl[:, c, :])

        SPLITS = {}
        for c in range(8):
            SPLITS.setdefault(LAST_READ[c] + 1, []).append(c)
        for c in range(8, 12):
            end = max(n for n in range(N_IDX, len(ITEMS)) if chunk_id(n) == c) + WEIGH_LAG + 1
            SPLITS.setdefault(max(end, LAST_READ[DK - 1] + 2), []).append(c)
        LAST = max(SPLITS) + 1
        POOL_SQUARES = 5
        MEM_STEP = 0
        SEARCH0 = HEADS

        def gate_unit(g):
            return U_IN + len(IN_STEPS) + g

        def gates_at(n):
            return [g for g in range(GATES) if GATE_STEP[g] + 1 == n]

        N_POOL_TAPS = sum(len(t) for t in POOL_TAPS.values())

        def pool_taps(j):
            if j < 2:
                return 0
            if j == len(IN2_STEPS) - 1:
                return N_POOL_TAPS - POOL_STEP_TAPS * (j - 2)
            return POOL_STEP_TAPS

        block = ctx.enter_context(nc.Block())

        @block.sync
        def _(sp):
            sp.dma_start(raw[:, 0, :], T["weights"][0]).then_inc(raw_loaded[0], 16)
            sp.dma_start(vec[:, :], T["vectors"]).then_inc(sem("vectors_loaded"), 16)
            for c in range(4):
                sp.dma_start(h[:, 2 * c:2 * c + 2, :], T["x_t"][:, 2 * c:2 * c + 2, :]).then_inc(sem(f"x_loaded{c}"), 16)
                if c == 0:
                    sp.dma_start(raw[:, 1, :], T["weights"][1]).then_inc(raw_loaded[1], 16)
            for dst, src in ((ident, "identity"), (ones, "ones"), (bd, "ones_by_head"),
                             (cmask, "causal_mask")):
                sp.dma_start(dst[:, :], T[src]).then_inc(sem("constants_loaded"), 16)
            for u in range(2, RAW):
                sp.dma_start(raw[:, u, :], T["weights"][u]).then_inc(raw_loaded[u], 16)
            sp.dma_start(pos[:, :], T["positions"]).then_inc(sem("positions_loaded"), 16)
            with sp.Fori(1, UNITS // RAW) as i:
                for s in range(RAW):
                    sp.wait_ge(low_done, i * RAW + (s - RAW + 1))
                    sp.dma_start(raw[:, s, :], T["weights"][bass.ds(i * RAW + s, 1)].rearrange("a p n -> p (a n)")
                                 ).then_inc(raw_loaded[s], 16)
            for m in range(DK):
                sp.wait_ge(sem("out_ready"), m + 1)
                sp.dma_start(T["out_t"][:, m, :], out_t[:, m, :]).then_inc(sem("out_stored"), 16)
            sp.wait_ge(sem("out_stored"), 16 * DK)

        @block.gpsimd
        def _(pool):
            def low_part(u, i=None):
                pool.wait_ge(high_done, u + 1 if i is None else i * RAW + (u + 1))
                pool.tensor_tensor(wl[:, u % SPL, :], raw[:, u % RAW, :], wh[:, u % SPL, :].bitcast(F32),
                                   ALU.subtract).then_inc(low_done, 1)

            def low_parts(first, end):
                start, stop = -(-first // RAW), end // RAW
                for u in range(first, start * RAW):
                    low_part(u)
                with pool.Fori(start, stop) as i:
                    for s in range(RAW):
                        low_part(s, i)
                for u in range(stop * RAW, end):
                    low_part(u)

            added_up = [0]

            def add_square(total, square):
                pool.tensor_tensor(total, total, square, ALU.add).then_inc(sem("squares_added"), 1)
                added_up[0] += 1
                pool.wait_ge(sem("squares_added"), added_up[0])

            def add_squares(name):
                for m in range(1, POOL_SQUARES):
                    pool.wait_ge(sem("input_square"), fed(name, m))
                    add_square(tiles[0][:, :], tiles[m][:, :])

            low_part(0)
            low_part(1)
            add_squares("ffn1")
            low_parts(2, U_IN + 2)
            add_squares("mix")
            for j in range(2, len(IN_STEPS)):
                low_part(U_IN + j)
                m = j - MEM_STEP - 4
                if 1 <= m < DK:
                    pool.wait_ge(sem("mem_square"), m + 1)
                    add_square(mem_in[:, 0, :], mem_in[:, m, :])
                if m == DK:
                    break
            low_parts(U_IN + j + 1, gate_unit(0) + 2)
            for g in range(GATES):
                low_part(gate_unit(g) + 2)
                pool.wait_ge(sem("gates_out"), g + 1)
                pool.tensor_tensor(gate_slot(g), gate_slot(g), rstd[:, :], ALU.mult).then_inc(sem("gates_scaled"), 1)
            low_parts(U_BR + 2, U_GU2 + 2)
            add_squares("ffn2")
            low_parts(U_GU2 + 2, U_IN2 + 2)
            add_squares("mix2")
            tap = 0
            for j in range(len(IN2_STEPS)):
                low_part(U_IN2 + j + 2)
                for _ in range(pool_taps(j)):
                    if tap:
                        pool.wait_ge(sem("tap_scaled"), tap + 1)
                        pool.tensor_tensor(conv_pool[:, :], scaled[0][:, :] if tap == 1 else conv_pool[:, :],
                                           scaled[tap % 4][:, :], ALU.add).then_inc(sem("tap_added"), 1)
                        pool.wait_ge(sem("tap_added"), tap)
                    tap += 1
            low_parts(U_WO2 + 2, U_GU3 + 2)
            add_squares("ffn3")
            low_parts(U_GU3 + 2, UNITS)
            add_squares("final")

        @block.tensor
        def _(pe):
            def products(out, u, k, rh, rl, start, stop):
                w = slice(k * P, (k + 1) * P)
                pe.matmul(out, wh[:, u % SPL, w], rh, start=start, stop=False)
                pe.matmul(out, wl[:, u % SPL, w], rh, start=False, stop=False)
                return pe.matmul(out, wh[:, u % SPL, w], rl, start=False, stop=stop)

            def project(u, out, rh, rl, low_at, n=S):
                pe.wait_ge(low_done, low_at)
                for k in range(DK):
                    mm = products(out, u, k, rh[:, k, 0:n], rl[:, k, 0:n], k == 0, k == DK - 1)
                mm.then_inc(unit_done, 1)

            def spread_unit(name, u, rh, rl, low_at, first=(), last=False, held=(None,)):
                pe.wait_ge(low_done, low_at)
                for m in first or range(DK):
                    if first and m == held[0]:
                        pe.wait_ge(sem(held[1]), held[2])
                    mm = products(bank[m][:, :], u, m, rh, rl, bool(first), last)
                    if last and m < DK - 1:
                        mm.then_inc(sem(f"{name}_gathered"), 1)
                mm.then_inc(unit_done, 1)

            def pair_start(name, u0, out0, out1):
                for k in range(DK + 3):
                    for unit, out, c in ((u0, out0, k), (u0 + 1, out1, k - 3)):
                        if not 0 <= c < DK:
                            continue
                        if c == 0:
                            pe.wait_ge(low_done, unit + 1)
                        if unit == u0:
                            pe.wait_ge(sem("input_low"), fed(name, c))
                            if c == 0 and name != "ffn1":
                                pe.wait_ge(sem("residual_added"), added(name, 1))
                        mm = products(out, unit, c, xh[:, c, :], xl[:, c, :], c == 0, c == DK - 1)
                        if c == DK - 1:
                            mm.then_inc(unit_done, 1)
                sums(name)

            def sums(name):
                if name == "ffn1":
                    pe.wait_ge(sem("constants_loaded"), 16 * 4)
                pe.wait_ge(sem("squares_totalled"), (INPUTS.index(name) + 1) * (DK - POOL_SQUARES))
                for b in range(QB):
                    mm = pe.matmul(bank[4][:, b:b + 1], tiles[0][:, b * P:(b + 1) * P], ones[:, 0:1],
                                   start=True, stop=True)
                mm.then_inc(sem("norm_sum"), 1)

            def spread_factor(name):
                pe.wait_ge(sem("norm_inverse"), nth(name))
                for b in range(QB):
                    mm = pe.matmul(bank[5][:, b * P:(b + 1) * P], root[:, 1, b:b + 1].to_broadcast([P, P]),
                                   ident[:, :], start=True, stop=True)
                mm.then_inc(sem("norm_spread"), 1)

            def gate_up(name, feed, u0):
                pair_start(feed, u0, bank[0][:, :], bank[1][:, :])
                spread_factor(feed)
                project(u0 + 2, bank[2][:, :], xh, xl, u0 + 3)
                project(u0 + 3, bank[3][:, :], xh, xl, u0 + 4)
                with pe.Fori(1, FC // 2) as i:
                    for c in range(2):
                        pe.wait_ge(sem(f"{name}_banks"), i * 2 + (c - 1))
                        for g in range(2):
                            project(u0 + 2 * c + g, bank[2 * c + g][:, :], xh, xl, i * 4 + (u0 + 2 * c + g + 1))

            def down(name, feed, u0):
                pe.wait_ge(sem(f"{feed}_factor"), 1)
                pe.wait_ge(sem(f"{name}_split"), 3)
                for f in range(2):
                    spread_unit(name, u0 + f, hh[:, f, :], hl[:, f, :], u0 + f + 1, first=(4, 5, 6, 7, 0, 1, 2, 3) if f == 0 else (), held=(0, f"{name}_banks", FC))
                pe.wait_ge(sem(f"{name}_split"), FC)
                with pe.Fori(0, (FC - 6) // 4) as i:
                    for c in range(4):
                        f = bass.ds(i * 4 + (c + 2), 1)
                        spread_unit(name, u0 + 2 + c, hh[:, f, :].rearrange("p a n -> p (a n)"),
                                    hl[:, f, :].rearrange("p a n -> p (a n)"), i * 4 + (u0 + c + 3))
                pe.wait_ge(sem(f"{name}_split"), FC + 1)
                for f in range(FC - 4, FC):
                    spread_unit(name, u0 + f, hh[:, f, :], hl[:, f, :], u0 + f + 1, last=(f == FC - 1))

            def stepped(fill):
                n_steps = len(IN_STEPS)
                for j in range(2, n_steps + FLUSH):
                    if j == 2:
                        pair_start("mix", U_IN, proj[0][:, :], proj[1][:, :])
                    if j < n_steps:
                        n = tokens(IN_STEPS[j])
                        if j >= 3:
                            pe.wait_ge(sem("in_taken"), j - 2)
                        if IN_STEPS[j] == "km" and chunk_of(IN_STEPS, j) == 0:
                            pe.wait_ge(sem("mem_low"), DK)
                        if j == 2:
                            spread_factor("mix")
                        rh, rl = (mem_h, mem_l) if n == MEM else (xh, xl)
                        project(U_IN + j, proj[j % 3][:, 0:n], rh, rl, U_IN + j + 1, n)
                    else:
                        fill(FILLS[j - n_steps])
                    for i in ((0, 1) if j == 2 else (j - 1,)):
                        if i >= n_steps:
                            continue
                        kind, n = IN_STEPS[i], tokens(IN_STEPS[i])
                        if kind in NORM:
                            k = upto_step(IN_STEPS, NORM, i)
                            pe.wait_ge(sem("in_squared"), k)
                            if k > 1:
                                pe.wait_ge(sem("in_rooted"), k - 1)
                            pe.matmul(bank[2][:, 0:n], (bd if heads(kind) == 2 else ones)[:, :],
                                      sq_in[k % 2][:, 0:n], start=True, stop=True).then_inc(sem("in_summed"), 1)
                        if kind in TURN:
                            k = upto_step(IN_STEPS, TURN, i)
                            pe.wait_ge(sem("in_taken"), i + 1)
                            if k > 2:
                                pe.wait_ge(sem("in_turned_out"), k - 2)
                            lo = HD if kind in ("ik", "dk") else 0
                            for b in range(n // P):
                                mm = pe.transpose(bank[4 + k % 2][:, b * P:b * P + P - lo],
                                                  t_in[i % 4][lo:P, b * P:(b + 1) * P], ident[lo:P, lo:P])
                            mm.then_inc(sem("in_turned"), 1)
                    if j == 4:
                        pe.wait_ge(sem("forget_logs"), 1)
                        pe.wait_ge(sem("triangle_loaded"), 16)
                        for b in range(QB):
                            mm = pe.matmul(bank[6][0:HEADS, b * P:S], forget[:, 0, b, :], tri[:, 0:S - b * P],
                                           start=(b == 0), stop=(b == QB - 1))
                        mm.then_inc(sem("forget_summed"), 1)
                    if j == 6:
                        pe.wait_ge(sem("forget_out"), 1)
                    if j == MEM_STEP + 11:
                        pe.wait_ge(sem("squares_added"), squares("mix") + DK - 1)
                        for b in range(MEM // P):
                            mm = pe.matmul(bank[6][:, b:b + 1], mem_in[:, 0, b * P:(b + 1) * P], ones[:, 0:1],
                                           start=True, stop=True)
                        mm.then_inc(sem("norm_sum"), 1)
                    if j == MEM_STEP + 12:
                        pe.wait_ge(sem("norm_inverse"), nth("mem"))
                        for b in range(MEM // P):
                            mm = pe.matmul(bank[6][:, b * P:(b + 1) * P], root[:, 1, b:b + 1].to_broadcast([P, P]),
                                           ident[:, :], start=True, stop=True)
                        mm.then_inc(sem("norm_spread"), 1)

            gate_up("g1", "ffn1", U_GU1)
            down("g1", "ffn1", U_DN1)

            def gate_products():
                for g in range(GATES):
                    u = gate_unit(g)
                    if g == 0:
                        pe.wait_ge(sem("in_taken"), len(IN_STEPS))
                    for k in range(DK):
                        for part in range(3):
                            if k == 0 and part == 0:
                                pe.wait_ge(low_done, u + 1)
                                if g >= 2:
                                    pe.wait_ge(sem("gates_out"), g - 1)
                            w = slice(k * P, (k + 1) * P)
                            mm = pe.matmul(bank[g % 2][:, :], (wl if part == 1 else wh)[:, u % SPL, w],
                                           (xl if part == 2 else xh)[:, k, :],
                                           start=(k == 0 and part == 0), stop=(k == DK - 1 and part == 2))
                            if k == DK - 1 and part == 2:
                                mm.then_inc(unit_done, 1)
                            elif g == GATES - 1 and part == 2:
                                mm.then_inc(sem("input_read"), 1)
                            yield

            filler = gate_products()

            def fill(n):
                for _ in range(n):
                    next(filler, None)

            stepped(fill)

            def scores(n):
                kind, hd, q, ext = ITEMS[n]
                lo = HD * (hd % 2)
                if kind == "mem":
                    left, right = mq[:, hd, q * P:(q + 1) * P], km[:, hd, 0:MEM]
                else:
                    a = {"idx": iq, "fox": fq, "dsa": dq}[kind]
                    left = a[lo:lo + HD, hd // 2, q * P:(q + 1) * P]
                    right = (fk[lo:lo + HD, hd // 2, 0:ext] if kind == "fox"
                             else (ki if kind == "idx" else kd)[lo:lo + HD, 0:ext])
                if 2 <= n < N_IDX + 2:
                    pe.wait_ge(sem("relu_done"), n - 1)
                elif n >= N_IDX + 2:
                    pe.wait_ge(sem("shifted"), n - 1 - N_IDX)
                mm = pe.matmul(bank[3 + n % 2][:, 0:ext], left, right, start=True, stop=(kind != "fox"))
                if kind == "fox":
                    mm = pe.matmul(bank[3 + n % 2][:, ext - P:ext], ident_r[:, :], mask_r[:, :],
                                   start=False, stop=True)
                mm.then_inc(sem("scores"), 1)

            def turn(n):
                s = n - N_IDX
                pe.wait_ge(sem("probs"), s + 1)
                if s >= 2:
                    pe.wait_ge(sem("turned_out"), s - 1)
                for b in range(ITEMS[n][3] // P):
                    mm = pe.transpose(bank[5 + s % 2][:, b * P:(b + 1) * P], soft[n % 3][:, b * P:(b + 1) * P],
                                      ident[:, :])
                mm.then_inc(sem("turned"), 1)

            def weigh(n):
                kind, hd, q, ext = ITEMS[n]
                s = n - N_IDX
                pe.wait_ge(sem("turned_out"), s + 1)
                if chunk_id(n) >= 2:
                    pe.wait_ge(sem("heads_out"), chunk_id(n) - 1)
                lo, hi = (0, P) if kind == "mem" else (HD * (hd % 2), HD * (hd % 2) + HD)
                for b in range(ext // P):
                    val = {"fox": lambda: fv[:, b, hd * HD:(hd + 1) * HD], "dsa": lambda: dv[:, b, :],
                           "mem": lambda: vm[:, b, hd * P:(hd + 1) * P]}[kind]()
                    mm = pe.matmul(heads_bank(chunk_id(n))[lo:hi, q * P:(q + 1) * P], val, probs_t[s % 2][:, b * P:(b + 1) * P],
                                   start=(b == 0), stop=(b == ext // P - 1))
                mm.then_inc(sem("weighed"), 1)

            pe.wait_ge(sem("in_taken"), len(IN_STEPS))
            pe.wait_ge(sem("in_normed"), upto_step(IN_STEPS, NORM, 99))
            pe.wait_ge(sem("in_roped"), upto_step(IN_STEPS, ROPE, 99))
            pe.wait_ge(sem("in_turned_out"), upto_step(IN_STEPS, TURN, 99))
            pe.wait_ge(sem("shared_keys"), 32)
            pe.wait_ge(sem("mask_rounded"), 1)
            for n in range(len(ITEMS) + WEIGH_LAG):
                if n < len(ITEMS):
                    kind, hd, q, _ = ITEMS[n]
                    scores(n)
                k = FILLS[FLUSH + n]
                fill(k - k // 2)
                if N_IDX <= n - TURN_LAG < len(ITEMS):
                    turn(n - TURN_LAG)
                fill(k // 2)
                if n - WEIGH_LAG >= N_IDX:
                    weigh(n - WEIGH_LAG)
            for _ in filler:
                pass

            pe.wait_ge(sem("shifted"), len(ITEMS) - N_IDX)
            pe.wait_ge(sem("turned_out"), len(ITEMS) - N_IDX)
            pe.wait_ge(sem("gates_out"), GATES)
            for m in range(DK):
                for n in range(3):
                    if n == 0 and m >= 2:
                        pe.wait_ge(sem("branches_read"), m - 1)
                    if n == 2 and m == 0:
                        pe.wait_ge(sem("heads_out"), 11)
                    for k in range(BK):
                        b = (m * 3 + n) * BK + k
                        if b % DK == 0:
                            pe.wait_ge(low_done, U_BR + b // DK + 1)
                        if m == 0:
                            pe.wait_ge(sem("out_split"), n * BK + k + 1)
                        rh, rl, o = ((xh, xl, 0), (xh, xl, 4), (och, ocl, 0))[n]
                        mm = products(bank[3 * (m % 2) + n][:, :], U_BR + b // DK, b % DK,
                                      rh[:, o + k, :], rl[:, o + k, :], k == 0, k == BK - 1)
                        if b % DK == DK - 1:
                            mm.then_inc(unit_done, 1)
                        elif n == 2 and k == BK - 1:
                            mm.then_inc(sem("branches_even"), 1)
            pe.wait_ge(sem("branches_read"), DK - 1)
            for f in range(N_WO):
                pe.wait_ge(sem("merged_low"), f + 1)
                spread_unit("wo", U_WO + f, mgh[:, f, :], mgl[:, f, :], U_WO + f + 1,
                            first=(6, 7, 0, 1, 2, 3, 4, 5) if f == 0 else (), held=(3, "branches_read", DK),
                            last=(f == N_WO - 1))

            gate_up("g2", "ffn2", U_GU2)
            down("g2", "ffn2", U_DN2)

            pair_start("mix2", U_IN2, proj[0][:, :], proj[1][:, :])
            for j in range(2, len(IN2_STEPS)):
                if j >= 3:
                    pe.wait_ge(sem("in2_taken"), j - 2)
                if j == 2:
                    spread_factor("mix2")
                project(U_IN2 + j, proj[j % 3][:, :], xh, xl, U_IN2 + j + 1)
            taps = [(c, k) for c, ks in PE_TAPS.items() for k in ks]
            pe.wait_ge(sem("diagonals_built"), 1)
            pe.wait_ge(sem("glu_done"), 4)
            for t, (c, k) in enumerate(taps):
                if t == BEFORE_MAPS:
                    pe.wait_ge(sem("in2_taken"), len(IN2_STEPS))
                    pe.wait_ge(sem("pool_weights_loaded"), 16)
                    for g in range(len(WINDOWS)):
                        pe.wait_ge(sem("pooled"), g + 1)
                        pe.matmul(bank[2 + g][:, :], wpool[:, g, :], pooled[:, g, :], start=True, stop=True
                                  ).then_inc(sem("pool_mapped"), 1)
                if t == 0:
                    pe.wait_ge(sem("in2_taken"), 10)
                mm = pe.matmul(bank[0][:, :], diagonals[:, t, :], glu[:, c, k:k + S], start=(t == 0),
                               stop=(t == len(taps) - 1))
            mm.then_inc(sem("taps_gathered"), 1)

            def pool_half(first, end):
                for b in range(first, end):
                    u, (k, m) = U_WO2 + b // DK, POOL_HALF[b]
                    if b % DK == 0:
                        pe.wait_ge(low_done, u + 1)
                    if m == 2:
                        pe.wait_ge(sem("mixed_low"), k - 3)
                    mm = products(bank[m][:, :], u, b % DK, xh[:, k, :], xl[:, k, :], k == 4, False)
                    if b % DK == DK - 1:
                        mm.then_inc(unit_done, 1)

            pe.wait_ge(sem("pool_out"), 4)
            pool_half(0, DK)
            pe.wait_ge(sem("conv_done"), 4)
            for c in range(4):
                mm = pe.matmul(bank[0][:, :], ones[:, :], conv[:, c, :], start=(c == 0), stop=(c == 3))
            mm.then_inc(sem("ln_summed"), 1)
            pool_half(DK, 2 * DK)
            pe.wait_ge(sem("ln_squares_added"), 3)
            for b in range(QB):
                mm = pe.matmul(bank[1][:, b:b + 1], ln_sq[0][:, b * P:(b + 1) * P], ones[:, 0:1],
                               start=True, stop=True)
            mm.then_inc(sem("norm_sum"), 1)
            pool_half(2 * DK, 2 * DK + 3)
            pe.wait_ge(sem("norm_inverse"), nth("ln"))
            for b in range(QB):
                mm = pe.matmul(bank[0][:, b * P:(b + 1) * P], root[:, 1, b:b + 1].to_broadcast([P, P]),
                               ident[:, :], start=True, stop=True)
            mm.then_inc(sem("norm_spread"), 1)
            pool_half(2 * DK + 3, 3 * DK)
            pe.wait_ge(sem("ln_scaled"), 4)
            pool_half(3 * DK, 4 * DK)
            for c in range(4):
                pe.wait_ge(sem("mixed_low"), 4 + c + 1)
                spread_unit("wo2", U_WO2 + 4 + c, xh[:, c, :], xl[:, c, :], U_WO2 + 4 + c + 1, last=(c == 3))

            gate_up("g3", "ffn3", U_GU3)
            down("g3", "ffn3", U_DN3)
            pe.wait_ge(sem("residual_added"), added("final", 4))
            sums("final")
            pe.wait_ge(sem("residual_added"), added("final", 5))
            spread_factor("final")

        @block.scalar
        def _(act):
            def high(u, i=None):
                wait, trip = (lambda c: c) if i is None else (lambda c: i * 4 + c), u // RAW + 1
                act.wait_ge(raw_loaded[u % RAW], 16 * trip if i is None else i * 16 + 16 * trip)
                if u >= SPL or i is not None:
                    act.wait_ge(unit_done, wait(u - SPL + 1))
                act.copy(wh[:, u % SPL, :], raw[:, u % RAW, :]).then_inc(high_done, 1)

            def after(u, i=None):
                if u + SPL < UNITS:
                    high(u + SPL, i=i)

            def feed_chunk(name, gain, m):
                if gain:
                    act.activation(xh[:, m, :], h[:, m, :], ACT.Copy, scale=v(gain, m)).then_inc(sem("input_high"), 1)
                act.activation(tiles[m][:, :], h[:, m, :], ACT.Square).then_inc(sem("input_square"), 1)

            def feed_root(name, src, n=QB, count=D, bias=0):
                act.wait_ge(sem("norm_sum"), nth(name))
                act.activation(root[:, 0, 0:n], src[:, 0:n], ACT.Sqrt, bias=eps[:, bias:bias + 1], scale=1.0 / count
                               ).then_inc(sem("norm_root"), 1)

            def feed(name, gain, u_last):
                for m in range(DK):
                    if m == 3:
                        after(u_last)
                    act.wait_ge(sem("residual_added"), added(name, m))
                    feed_chunk(name, gain, m)

            def take_gates(n):
                for g in gates_at(n):
                    after(gate_unit(g))
                    act.copy(gate_slot(g), bank[g % 2][:, :]).then_inc(sem("gates_out"), 1)

            def stepped():
                n_steps = len(IN_STEPS)
                for j in range(n_steps + FLUSH):
                    take_gates(j - n_steps - FLUSH)
                    if j < n_steps:
                        after(U_IN + j)
                        if j == 0:
                            feed_root("mix", bank[4])
                        kind, n = IN_STEPS[j], tokens(IN_STEPS[j])
                        if kind in NORM:
                            k = upto_step(IN_STEPS, NORM, j)
                            act.wait_ge(sem("in_taken"), j + 1)
                            if k > 2:
                                act.wait_ge(sem("in_summed"), k - 2)
                            act.activation(sq_in[k % 2][:, 0:n], t_in[j % 4][:, 0:n], ACT.Square
                                           ).then_inc(sem("in_squared"), 1)
                    i = j - 1
                    if 0 <= i < n_steps and IN_STEPS[i] in NORM:
                        kind, n = IN_STEPS[i], tokens(IN_STEPS[i])
                        k = upto_step(IN_STEPS, NORM, i)
                        act.wait_ge(sem("in_summed"), k)
                        if k > 2:
                            act.wait_ge(sem("in_normed"), k - 2)
                        act.activation(head_root[k % 2][:, 0:n], bank[2][:, 0:n], ACT.Sqrt, bias=eps[:, 0:1],
                                       scale=float(heads(kind)) / P).then_inc(sem("in_rooted"), 1)
                    if j == 2:
                        act.wait_ge(sem("forget_in"), 1)
                        act.activation(forget[:, 1], forget[:, 0], ACT.Abs).then_inc(sem("act_own"), 1)
                        act.wait_ge(sem("act_own"), 2)
                        act.activation(forget[:, 1], forget[:, 1], ACT.Exp, scale=-1.0).then_inc(sem("act_own"), 1)
                        act.wait_ge(sem("act_own"), 3)
                        act.activation(forget[:, 1], forget[:, 1], ACT.Ln, bias=eps[:, 3:4]
                                       ).then_inc(sem("forget_ln"), 1)
                    m = j - MEM_STEP
                    if 0 <= m < DK:
                        act.wait_ge(sem("mem_loaded"), 16)
                        act.activation(mem_h[:, m, :], mem_in[:, m, :], ACT.Copy, scale=v("mem_norm", m)
                                       ).then_inc(sem("mem_high"), 1)
                    if 0 <= m - 1 < DK:
                        act.wait_ge(sem("mem_low"), m)
                        act.activation(mem_in[:, m - 1, :], mem_in[:, m - 1, :], ACT.Square
                                       ).then_inc(sem("mem_square"), 1)
                    if m == 11:
                        feed_root("mem", bank[6], MEM // P)
                    i = j - 2
                    if 0 <= i < n_steps and IN_STEPS[i] in ROPE:
                        kind, k = IN_STEPS[i], upto_step(IN_STEPS, ROPE, i)
                        act.wait_ge(sem("in_taken"), i + 1)
                        if kind in NORM:
                            act.wait_ge(sem("in_normed"), upto_step(IN_STEPS, NORM, i))
                        if k > 2:
                            act.wait_ge(sem("in_roped"), k - 2)
                        half = HD // 2
                        for to in range(0, HD if kind in ("dk", "ik") else P, half):
                            of = to + (half if to % HD == 0 else -half)
                            act.dma_start(halves[k % 2][to:to + half, :], t_in[i % 4][of:of + half, :]
                                          ).then_inc(sem(f"in_rotated{k % 2}"), 16)
                    if j == 7:
                        act.wait_ge(sem("forget_out"), 1)
                        act.dma_start(T["forget_sums"], cum[0:HEADS, :]).then_inc(sem("forget_stored"), 16)
                    for t, step in ((ki, 0), (kd, IN_STEPS.index("dk"))):
                        if j == step + 4:
                            act.wait_ge(sem("in_roped"), upto_step(IN_STEPS, ROPE, step))
                            act.dma_start(t[HD:P, :], t[0:HD, :]).then_inc(sem("shared_keys"), 16)

            def gate_up(name, feed_name, u0):
                def pair(i):
                    for c in range(2):
                        after(u0 + 2 * c, i)
                        if c == 0 and i is None:
                            feed_root(feed_name, bank[4])
                            after(u0 + 1)
                        one = (0 if i is None else i * 2) + (c + 1)
                        act.wait_ge(sem(f"{name}_gate"), one)
                        act.activation(tiles[c][:, :], tiles[c][:, :], ACT.Silu).then_inc(sem(f"{name}_silu"), 1)
                        if c or i is not None:
                            after(u0 + 2 * c + 1, i)
                        act.wait_ge(sem(f"{name}_act"), one)
                        f = bass.ds(i * 2 + c, 1) if i is not None else slice(c, c + 1)
                        act.copy(hh[:, f, :].rearrange("p a n -> p (a n)"), tiles[2 + c][:, :]
                                 ).then_inc(sem(f"{name}_high"), 1)

                pair(None)
                with act.Fori(1, FC // 2) as i:
                    pair(i)

            def rotary_tables():
                act.wait_ge(sem("angles"), 1)
                act.activation(turns[:, :], ang[:, :], ACT.Abs).then_inc(sem("act_own"), 1)
                act.activation(sin[:, :], ang[:, :], ACT.Sin).then_inc(sem("sine"), 1)
                act.wait_ge(sem("act_own"), 1)
                act.activation(cos[:, :], turns[:, :], ACT.Sin, bias=eps[:, 2:3], scale=-1.0
                               ).then_inc(sem("sine"), 1)

            def down(u0, loads=(), between=None):
                for f in range(2):
                    after(u0 + f)
                if between:
                    between()
                with act.Fori(0, (FC - 6) // 4) as i:
                    for c in range(4):
                        after(u0 + 2 + c, i)
                for f in range(FC - 4, FC - 2):
                    after(u0 + f)
                for dst, src, name in loads:
                    act.dma_start(dst, T[src]).then_inc(sem(name), 16)
                after(u0 + FC - 2)

            high(0)
            act.wait_ge(sem("vectors_loaded"), 16)
            for m in range(DK):
                if m % 2 == 0:
                    act.wait_ge(sem(f"x_loaded{m // 2}"), 16)
                feed_chunk("ffn1", "ffn1_norm", m)
                if m == 1:
                    high(1)
            act.wait_ge(sem("eps_set"), 4)
            gate_up("g1", "ffn1", U_GU1)
            down(U_DN1, ((mem_in[:, :, :], "mem_t", "mem_loaded"), (tri[:, :], "triangle", "triangle_loaded")),
                 rotary_tables)
            feed("mix", "mix_norm", U_IN - 1)
            stepped()

            def bias(hd):
                act.dma_start(fbias[hd % 2][:, :], T["forget_sums"][hd, :].partition_broadcast(P)
                              ).then_inc(sem(f"bias_loaded{hd % 2}"), 16)

            act.wait_ge(sem("in_normed"), upto_step(IN_STEPS, NORM, 99))
            act.wait_ge(sem("in_roped"), upto_step(IN_STEPS, ROPE, 99))
            act.wait_ge(sem("in_turned"), upto_step(IN_STEPS, TURN, 99))
            act.wait_ge(sem("forget_stored"), 16)
            for hd in range(2):
                bias(hd)
            for n in range(LAST):
                take_gates(n)
                if n < N_IDX:
                    ext = ITEMS[n][3]
                    act.wait_ge(sem("scores"), n + 1)
                    if n >= 2:
                        act.wait_ge(sem("idx_added"), n - 1)
                    act.activation(soft[n % 3][:, 0:ext], bank[3 + n % 2][:, 0:ext], ACT.Relu
                                   ).then_inc(sem("relu_done"), 1)
                elif n < len(ITEMS):
                    kind, hd, q, ext = ITEMS[n]
                    c = n % 4
                    act.wait_ge(sem("shifted"), n - N_IDX + 1)
                    if kind == "fox" and q == 0 and 1 <= hd < HEADS - 1:
                        bias(hd + 1)
                    act.activation(soft[n % 3][:, 0:ext], soft[n % 3][:, 0:ext], ACT.Exp, scale=-1.0,
                                   bias=stat[:, 0, c:c + 1], accum_out=stat[:, 1, c:c + 1]).then_inc(sem("exped"), 1)
                s = n - TURN_LAG - N_IDX
                if 0 <= s < len(ITEMS) - N_IDX:
                    ext = ITEMS[n - TURN_LAG][3]
                    act.wait_ge(sem("turned"), s + 1)
                    if s >= 2:
                        act.wait_ge(sem("weighed"), s - 1)
                    act.copy(probs_t[s % 2][:, 0:ext], bank[5 + s % 2][:, 0:ext]).then_inc(sem("turned_out"), 1)
                if ends_chunk(n - WEIGH_LAG - 1):
                    c = chunk_id(n - WEIGH_LAG - 1)
                    act.wait_ge(sem("weighed"), n - WEIGH_LAG - N_IDX)
                    act.copy(chunk_home(c), heads_bank(c)[:, :]).then_inc(sem("heads_out"), 1)
                for c in SPLITS.get(n, ()):
                    act.wait_ge(sem("heads_out"), c + 1)
                    if c < DK - 1:
                        act.wait_ge(sem("input_read"), c + 1)
                    elif c == DK - 1:
                        act.wait_ge(unit_done, U_BR)
                    else:
                        act.wait_ge(sem("out_split"), 8)
                    act.copy(chunk_parts(c)[0], chunk_home(c)).then_inc(sem("out_high"), 1)

            def sigmoids(m):
                for n in range(3):
                    g = gate_slot(n * DK + m)
                    act.activation(g, g, ACT.Sigmoid).then_inc(sem("gate_ready"), 1)

            act.wait_ge(sem("gates_scaled"), GATES)
            sigmoids(0)
            sigmoids(1)
            for u in range(U_BR, U_BR + N_BR):
                after(u)
                for m in range(DK):
                    if U_BR + (12 * m + 11) // DK == u:
                        act.wait_ge(sem("merge_summed"), m + 1)
                        act.copy(mgh[:, m, :], tiles[3 + m % 2][:, :]).then_inc(sem("merged_high"), 1)
                        if m + 2 < DK:
                            sigmoids(m + 2)
            for u in range(U_WO, U_GU2 - 1):
                after(u)
            feed("ffn2", "ffn2_norm", U_GU2 - 1)
            gate_up("g2", "ffn2", U_GU2)
            down(U_DN2, ((wpool[:, :, :], "pool_weights", "pool_weights_loaded"),))
            feed("mix2", "g_mix_2", U_IN2 - 1)
            taps, tap = [(c, k) for c, ks in POOL_TAPS.items() for k in ks], 0
            for j, kind in enumerate(IN2_STEPS):
                after(U_IN2 + j)
                if j == 0:
                    feed_root("mix2", bank[4])
                c = chunk_of(IN2_STEPS, j)
                for _ in range(pool_taps(j)):
                    ch, k = taps[tap]
                    if tap >= 4:
                        act.wait_ge(sem("tap_added"), tap - 4 if tap > 4 else 1)
                    act.wait_ge(sem("glu_done"), ch + 1)
                    act.activation(scaled[tap % 4][:, :], glu[:, ch, k:k + S], ACT.Copy,
                                   scale=v("w_dw_2", ch * TAPS + k)).then_inc(sem("tap_scaled"), 1)
                    tap += 1
                if kind == "s":
                    act.wait_ge(sem("in2_taken"), j + 1)
                    act.activation(sig[:, c % 2, :], sig[:, c % 2, :], ACT.Sigmoid, bias=v("b_in_2", 4 + c)
                                   ).then_inc(sem("glu_sigmoid"), 1)
                if kind == "p":
                    act.wait_ge(sem("in2_taken"), j + 1)
                    act.activation(pool_in[:, c, PADW:], pool_in[:, c, PADW:], ACT.Identity, bias=v("b_in_2", 8 + c)
                                   ).then_inc(sem("pool_biased"), 1)
            for g in range(4):
                act.wait_ge(sem("pool_mapped"), g + 1)
                act.activation(ymix[:, 4 + g, :], bank[2 + g][:, :], ACT.Copy, scale=v("s_pool_2", g)
                               ).then_inc(sem("pool_out"), 1)
                act.wait_ge(sem("pool_out"), g + 1)
                act.copy(xh[:, 4 + g, :], ymix[:, 4 + g, :]).then_inc(sem("mixed_high"), 1)
            after(U_WO2)
            for c in range(4):
                act.wait_ge(sem("centred"), c + 1)
                act.activation(ln_sq[c], conv[:, c, :], ACT.Square).then_inc(sem("ln_square"), 1)
            after(U_WO2 + 1)
            feed_root("ln", bank[1], count=4 * P, bias=1)
            for c in range(4):
                act.wait_ge(sem("ln_scaled"), c + 1)
                act.activation(ymix[:, c, :], ymix[:, c, :], ACT.Silu, bias=v("ln_b_2", c)).then_inc(sem("ln_out"), 1)
                act.wait_ge(sem("ln_out"), c + 1)
                act.copy(xh[:, c, :], ymix[:, c, :]).then_inc(sem("mixed_high"), 1)
                if c in (0, 2):
                    after(U_WO2 + 2 + c // 2)
            for u in range(U_WO2 + 4, U_GU3 - 1):
                after(u)
            feed("ffn3", "g_ffn_2", U_GU3 - 1)
            gate_up("g3", "ffn3", U_GU3)
            down(U_DN3)
            feed("final", None, UNITS - 1)
            feed_root("final", bank[4])

        @block.vector
        def _(dve):
            owned = [0]

            def own(ins):
                owned[0] += 1
                ins.then_inc(sem("dve_own"), 1)
                dve.wait_ge(sem("dve_own"), owned[0])

            def low(name, gain, m):
                dve.wait_ge(sem("input_high"), fed(name, m))
                dve.scalar_tensor_tensor(out=xl[:, m, :], in0=h[:, m, :], scalar=v(gain, m),
                                         in1=xh[:, m, :].bitcast(F32), op0=ALU.mult, op1=ALU.subtract
                                         ).then_inc(sem("input_low"), 1)

            def inverse(name, n=QB):
                dve.wait_ge(sem("norm_root"), nth(name))
                dve.reciprocal(root[:, 1, 0:n], root[:, 0, 0:n]).then_inc(sem("norm_inverse"), 1)

            def total_squares(name):
                for i, m in enumerate((*range(POOL_SQUARES + 1, DK), 0)):
                    if m:
                        dve.wait_ge(sem("input_square"), fed(name, m))
                    else:
                        dve.wait_ge(sem("squares_added"), squares(name))
                    total = tiles[POOL_SQUARES] if m else tiles[0]
                    dve.tensor_tensor(total[:, :], tiles[POOL_SQUARES][:, :], tiles[m][:, :], ALU.add
                                      ).then_inc(sem("squares_totalled"), 1)
                    dve.wait_ge(sem("squares_totalled"), INPUTS.index(name) * (DK - POOL_SQUARES) + i + 1)

            def factor(name):
                total_squares(name)
                inverse(name)
                dve.wait_ge(sem("norm_spread"), nth(name))
                dve.tensor_copy(rstd[:, :], bank[5][:, :]).then_inc(sem(f"{name}_factor"), 1)
                dve.wait_ge(sem(f"{name}_factor"), 1)

            def feed(name, gain, gathered, u_last, share, parts=True):
                for m in range(DK):
                    if m < DK - 1:
                        dve.wait_ge(sem(f"{gathered}_gathered"), m + 1)
                    else:
                        dve.wait_ge(unit_done, u_last + 1)
                    dve.scalar_tensor_tensor(out=h[:, m, :], in0=bank[m][:, :], scalar=share,
                                             in1=h[:, m, :], op0=ALU.mult, op1=ALU.add
                                             ).then_inc(sem("residual_added"), 1)
                    if parts and m:
                        low(name, gain, m - 1)
                if parts:
                    low(name, gain, DK - 1)

            def gate_up(name, u0):
                dve.sem_inc(sem(f"{name}_split"), 1)
                with dve.Fori(0, FC // 2) as i:
                    for c in range(2):
                        one = i * 2 + (c + 1)
                        dve.wait_ge(unit_done, i * 4 + (u0 + 2 * c + 1))
                        dve.tensor_tensor(tiles[c][:, :], bank[2 * c][:, :], rstd[:, :], ALU.mult
                                          ).then_inc(sem(f"{name}_gate"), 1)
                        dve.wait_ge(unit_done, i * 4 + (u0 + 2 * c + 2))
                        dve.wait_ge(sem(f"{name}_split"), one)
                        dve.tensor_tensor(tiles[2 + c][:, :], bank[2 * c + 1][:, :], rstd[:, :], ALU.mult
                                          ).then_inc(sem(f"{name}_banks"), 1)
                        dve.wait_ge(sem(f"{name}_silu"), one)
                        dve.wait_ge(sem(f"{name}_banks"), one)
                        dve.tensor_tensor(tiles[2 + c][:, :], tiles[2 + c][:, :], tiles[c][:, :], ALU.mult
                                          ).then_inc(sem(f"{name}_act"), 1)
                        dve.wait_ge(sem(f"{name}_high"), one)
                        f = bass.ds(i * 2 + c, 1)
                        dve.tensor_tensor(hl[:, f, :].rearrange("p a n -> p (a n)"), tiles[2 + c][:, :],
                                          hh[:, f, :].rearrange("p a n -> p (a n)").bitcast(F32), ALU.subtract
                                          ).then_inc(sem(f"{name}_split"), 1)

            def stepped():
                n_steps = len(IN_STEPS)
                for j in range(n_steps + FLUSH):
                    if j - MEM_STEP == 12:
                        inverse("mem", MEM // P)
                    if j < n_steps:
                        n = tokens(IN_STEPS[j])
                        i = j - 4
                        if i >= 0:
                            for kinds, name in ((TURN, "turned"), (NORM, "normed"), (ROPE, "roped")):
                                if IN_STEPS[i] in kinds:
                                    dve.wait_ge(sem(f"in_{name}"), upto_step(IN_STEPS, kinds, i))
                        dve.wait_ge(unit_done, U_IN + j + 1)
                        dve.tensor_tensor(t_in[j % 4][:, 0:n], proj[j % 3][:, 0:n],
                                          (mem_rstd if n == MEM else rstd)[:, 0:n], ALU.mult
                                          ).then_inc(sem("in_taken"), 1)
                    i = j - 1
                    if 0 <= i < n_steps and IN_STEPS[i] in TURN:
                        kind, n, c = IN_STEPS[i], tokens(IN_STEPS[i]), chunk_of(IN_STEPS, i)
                        k = upto_step(IN_STEPS, TURN, i)
                        dve.wait_ge(sem("in_turned"), k)
                        src = bank[4 + k % 2][:, 0:n].rearrange("p (b f) -> p b f", f=P)
                        if kind in ("fv", "vm"):
                            dst = fv if kind == "fv" else vm
                            dve.tensor_copy(dst[:, :, c * P:(c + 1) * P], src).then_inc(sem("in_turned_out"), 1)
                        elif kind == "dk":
                            dve.tensor_copy(dv[:, :, :], src[:, :, 0:HD]).then_inc(sem("in_turned_out"), 1)
                        else:
                            for b in range(QB):
                                ins = dve.tensor_tensor(forget[:, 0, b, :], src[:, b, 0:HEADS],
                                                        vec[:, VEC_COLS["b_forget"][0]:][:, 0:HEADS], ALU.add)
                            ins.then_inc(sem("forget_in"), 1)
                            dve.tensor_scalar(iw[:, :, :], src[:, :, HEADS:2 * HEADS],
                                              HEADS ** -0.5 * HD ** -0.5, None, ALU.mult
                                              ).then_inc(sem("in_turned_out"), 1)
                    i = j - 2
                    if 0 <= i < n_steps and IN_STEPS[i] in NORM:
                        kind, n, c = IN_STEPS[i], tokens(IN_STEPS[i]), chunk_of(IN_STEPS, i)
                        m = HD if kind == "dk" else P
                        t = t_in[i % 4][0:m, 0:n]
                        out = {"fq": fq, "fk": fk, "mq": mq, "km": km}[kind][:, c, :] if kind[0] != "d" else t
                        gain = ({"f": "fox_", "d": "dsa_", "m": "mem_", "k": "mem_"}[kind[0]]
                                + ("k" if kind == "km" else kind[1]) + "_norm")
                        k = upto_step(IN_STEPS, NORM, i)
                        dve.wait_ge(sem("in_inverse"), k)
                        dve.scalar_tensor_tensor(out=out, in0=t, scalar=v(gain)[0:m],
                                                 in1=head_root[k % 2][0:m, 0:n], op0=ALU.mult, op1=ALU.mult
                                                 ).then_inc(sem("in_normed"), 1)
                    i = j - 3
                    if i >= 0 and IN_STEPS[i] in ROPE:
                        k, kind, c = upto_step(IN_STEPS, ROPE, i), IN_STEPS[i], chunk_of(IN_STEPS, i)
                        m = HD if kind in ("dk", "ik") else P
                        t = t_in[i % 4][0:m, :]
                        out = {"iq": iq[:, c, :], "dq": dq[:, c, :], "ik": ki[0:HD, :], "dk": kd[0:HD, :]}[kind]
                        moves = sum(2 if IN_STEPS[x] in ("dk", "ik") else 4 for x in range(i + 1)
                                    if IN_STEPS[x] in ROPE and upto_step(IN_STEPS, ROPE, x) % 2 == k % 2)
                        dve.wait_ge(sem(f"in_rotated{k % 2}"), 16 * moves)
                        dve.tensor_tensor(halves[k % 2][0:m, :], halves[k % 2][0:m, :], sin[0:m, :], ALU.mult)
                        own(dve.tensor_tensor(t, t, cos[0:m, :], ALU.mult))
                        dve.tensor_tensor(out, t, halves[k % 2][0:m, :], ALU.add).then_inc(sem("in_roped"), 1)
                    m = j - MEM_STEP
                    i = j - 1
                    if 0 <= i < n_steps and IN_STEPS[i] in NORM:
                        k, n = upto_step(IN_STEPS, NORM, i), tokens(IN_STEPS[i])
                        dve.wait_ge(sem("in_rooted"), k)
                        root_k = head_root[k % 2][:, 0:n]
                        dve.reciprocal(root_k, root_k).then_inc(sem("in_inverse"), 1)
                    if j == 2:
                        dve.wait_ge(sem("forget_ln"), 1)
                        dve.scalar_tensor_tensor(out=forget[:, 0].rearrange("p b h -> p (b h)"),
                                                 in0=forget[:, 0].rearrange("p b h -> p (b h)"), scalar=0.0,
                                                 in1=forget[:, 1].rearrange("p b h -> p (b h)"),
                                                 op0=ALU.min, op1=ALU.subtract).then_inc(sem("forget_logs"), 1)
                    if j == 5:
                        dve.wait_ge(sem("forget_summed"), 1)
                        dve.tensor_scalar(cum[0:HEADS, :], bank[6][0:HEADS, :], -1.0, None, ALU.mult).then_inc(sem("forget_out"), 1)
                    m = j - MEM_STEP
                    if 0 <= m < DK:
                        dve.wait_ge(sem("mem_high"), m + 1)
                        dve.scalar_tensor_tensor(out=mem_l[:, m, :], in0=mem_in[:, m, :], scalar=v("mem_norm", m),
                                                 in1=mem_h[:, m, :].bitcast(F32), op0=ALU.mult, op1=ALU.subtract
                                                 ).then_inc(sem("mem_low"), 1)
                    if m == 12:
                        dve.wait_ge(sem("norm_spread"), nth("mem"))
                        dve.tensor_copy(mem_rstd[:, :], bank[6][:, 0:MEM]).then_inc(sem("mem_factor"), 1)
                        dve.wait_ge(sem("mem_factor"), 1)

            for c, val in enumerate((EPS, LN_EPS, float(np.pi / 2), 1.0)):
                dve.memset(eps[:, c:c + 1], val).then_inc(sem("eps_set"), 1)
            dve.wait_ge(sem("vectors_loaded"), 16)
            for name, scale in (("fox_q_norm", HD ** -0.5), ("dsa_q_norm", HD ** -0.5), ("mem_q_norm", P ** -0.5)):
                own(dve.tensor_scalar(v(name), v(name), scale, None, ALU.mult))
            for m in range(DK):
                low("ffn1", "ffn1_norm", m)
            dve.wait_ge(sem("constants_loaded"), 16 * 4)
            dve.tensor_copy(ident_r[:, :], ident[:, :])
            factor("ffn1")
            gate_up("g1", U_GU1)
            dve.wait_ge(sem("positions_loaded"), 16)
            own(dve.tensor_copy(turns[:, :], pos[:, :]))
            own(dve.tensor_scalar(ang[:, :], turns[:, :], v("inv_freq"), None, ALU.mult))
            own(dve.tensor_scalar(turns_raw[:, :], ang[:, :], 1.0 / TURN_RAD, ROUNDER, ALU.mult, ALU.add))
            own(dve.tensor_scalar(turns[:, :], turns_raw[:, :], -ROUNDER, None, ALU.add))
            for part in TURN_PARTS:
                own(dve.scalar_tensor_tensor(out=ang[:, :], in0=turns[:, :], scalar=-part, in1=ang[:, :],
                                             op0=ALU.mult, op1=ALU.add))
            dve.tensor_scalar(ang[:, :], ang[:, :], PI_BELOW, -PI_BELOW, ALU.min, ALU.max
                              ).then_inc(sem("angles"), 1)
            dve.wait_ge(sem("sine"), 2)
            for to in range(0, P, HD):
                half = slice(to, to + HD // 2)
                dve.tensor_scalar(sin[half, :], sin[half, :], -1.0, None, ALU.mult).then_inc(sem("sine_signed"), 1)
            feed("mix", "mix_norm", "g1", U_IN - 1, 0.5)
            factor("mix")
            dve.wait_ge(sem("sine_signed"), P // HD)
            stepped()

            def kept(q):
                return sel[:, sel_at[q]:sel_at[q] + (q + 1) * P]

            def search(r):
                q, r = 1 + r // ROUNDS, r % ROUNDS
                own(dve.max(mx8[:, :], kept(q)))
                own(dve.match_replace(kept(q), mx8[:, :], kept(q), TAKEN))
                if r == ROUNDS - 1:
                    own(dve.tensor_scalar(kept(q), kept(q), TAKEN / 2, MASKED, ALU.is_gt, ALU.mult))

            def shift(n):
                kind, hd, q, ext = ITEMS[n]
                s, c = n - N_IDX, n % 4
                if kind == "fox":
                    add = fbias[hd % 2][:, 0:ext]
                    dve.wait_ge(sem(f"bias_loaded{hd % 2}"), 16 * (hd // 2 + 1))
                elif kind == "dsa":
                    add = kept(q) if q else cmask[:, S - P:S]
                else:
                    add = cmask[:, 0:ext]
                dve.wait_ge(sem("scores"), n + 1)
                if s >= 3:
                    dve.wait_ge(sem("turned"), s - 2)
                dve.tensor_tensor_reduce(soft[n % 3][:, 0:ext], bank[3 + n % 2][:, 0:ext], add, -1.0, 3.0e38,
                                         ALU.add, ALU.min, stat[:, 0, c:c + 1]).then_inc(sem("shifted"), 1)

            def normalise(n):
                ext, s, c = ITEMS[n][3], n - N_IDX, n % 4
                dve.wait_ge(sem("exped"), s + 1)
                own(dve.reciprocal(stat[:, 2, c:c + 1], stat[:, 1, c:c + 1]))
                dve.tensor_scalar(soft[n % 3][:, 0:ext], soft[n % 3][:, 0:ext], stat[:, 2, c:c + 1], None,
                                  ALU.mult).then_inc(sem("probs"), 1)

            dve.wait_ge(sem("in_roped"), upto_step(IN_STEPS, ROPE, 99))
            dve.wait_ge(sem("in_normed"), upto_step(IN_STEPS, NORM, 99))
            dve.wait_ge(sem("in_turned_out"), upto_step(IN_STEPS, TURN, 99))
            dve.tensor_copy(mask_r[:, :], cmask[:, S - P:S]).then_inc(sem("mask_rounded"), 1)
            pending = []
            for n in range(LAST + 1):
                if N_IDX <= n - 1 < len(ITEMS):
                    normalise(n - 1)
                if n < len(ITEMS):
                    kind, hd, q, ext = ITEMS[n]
                    if kind == "idx":
                        dve.wait_ge(sem("relu_done"), n + 1)
                        dve.scalar_tensor_tensor(out=kept(q), in0=soft[n % 3][:, 0:ext], scalar=iw[:, q, hd:hd + 1],
                                                 in1=kept(q) if hd else cmask[:, S - ext:S],
                                                 op0=ALU.mult, op1=ALU.add).then_inc(sem("idx_added"), 1)
                        dve.wait_ge(sem("idx_added"), n + 1)
                    else:
                        shift(n)
                for c in pending:
                    dve.wait_ge(sem("out_high"), c + 1)
                    hi, lo_ = chunk_parts(c)
                    dve.tensor_tensor(lo_, chunk_home(c), hi.bitcast(F32), ALU.subtract
                                      ).then_inc(sem("out_split"), 1)
                pending = SPLITS.get(n, ())
                if SEARCH0 <= n < SEARCH0 + (QB - 1) * ROUNDS:
                    search(n - SEARCH0)

            def merge_low(m):
                dve.wait_ge(sem("merged_high"), m + 1)
                dve.tensor_tensor(mgl[:, m, :], tiles[3 + m % 2][:, :], mgh[:, m, :].bitcast(F32), ALU.subtract
                                  ).then_inc(sem("merged_low"), 1)

            for m in range(DK):
                dve.wait_ge(sem("gate_ready"), 3 * (m + 1))
                if m % 2:
                    dve.wait_ge(unit_done, U_BR + (12 * m + 11) // DK + 1)
                else:
                    dve.wait_ge(sem("branches_even"), m // 2 + 1)
                for n in range(3):
                    ins = dve.tensor_tensor(tiles[n][:, :], bank[3 * (m % 2) + n][:, :], gate_slot(n * DK + m),
                                            ALU.mult)
                ins.then_inc(sem("branches_read"), 1)
                dve.wait_ge(sem("branches_read"), m + 1)
                own(dve.tensor_tensor(tiles[0][:, :], tiles[0][:, :], tiles[1][:, :], ALU.add))
                if m >= 2:
                    dve.wait_ge(sem("merged_low"), m - 1)
                dve.tensor_tensor(tiles[3 + m % 2][:, :], tiles[0][:, :], tiles[2][:, :], ALU.add
                                  ).then_inc(sem("merge_summed"), 1)
                merge_low(m)
            feed("ffn2", "ffn2_norm", "wo", U_GU2 - 1, 1.0)
            factor("ffn2")
            gate_up("g2", U_GU2)
            dve.wait_ge(unit_done, U_DN2 + 18)
            for t, (c, k) in enumerate((c, k) for c, ks in PE_TAPS.items() for k in ks):
                dve.tensor_scalar(diagonals[:, t, :], ident[:, :], v("w_dw_2", c * TAPS + k), None, ALU.mult)
            for c in range(4):
                dve.memset(glu[:, c, 0:TAPS - 1], 0.0)
                dve.memset(pool_in[:, c, 0:PADW], 0.0)
            dve.memset(psum_a[:, 0:PADW], 0.0)
            dve.memset(psum_b[:, 0:PADW], 0.0).then_inc(sem("diagonals_built"), 1)
            dve.wait_ge(sem("diagonals_built"), 1)
            feed("mix2", "g_mix_2", "g2", U_IN2 - 1, 0.5)
            factor("mix2")

            def taps():
                for c in range(4):
                    for k in DVE_TAPS[c]:
                        w = v("w_dw_2", c * TAPS + k)
                        src = glu[:, c, k:k + S]
                        if k == 0:
                            ins = dve.tensor_scalar(conv[:, c, :], src, w, v("b_dw_2", c), ALU.mult, ALU.add)
                        else:
                            ins = dve.scalar_tensor_tensor(out=conv[:, c, :], in0=src, scalar=w, in1=conv[:, c, :],
                                                           op0=ALU.mult, op1=ALU.add)
                        if k == DVE_TAPS[c][-1] and len(DVE_TAPS[c]) == TAPS:
                            ins.then_inc(sem("conv_done"), 1)
                        else:
                            own(ins)
                        yield c

            def windows(g):
                width = WINDOWS[g]
                dve.wait_ge(sem("pool_biased"), g + 1)
                if g:
                    dve.wait_ge(sem("pooled"), g)
                src, shift_by, k = pool_in[:, g, :], 1, 0
                while shift_by < width:
                    dst = (psum_a, psum_b)[k % 2]
                    own(dve.tensor_tensor(dst[:, PADW:], src[:, PADW:], src[:, PADW - shift_by:PADW - shift_by + S],
                                          ALU.add))
                    src, shift_by, k = dst, shift_by * 2, k + 1
                o = VEC_COLS["pool_inv"][0] + g * PADW
                own(dve.tensor_tensor(src[:, PADW:2 * PADW], src[:, PADW:2 * PADW], vec[:, o:o + PADW], ALU.mult))
                dve.tensor_tensor(pooled[:, g, 0:PADW], src[:, PADW:2 * PADW], pool_in[:, g, PADW:2 * PADW],
                                  ALU.subtract)
                dve.scalar_tensor_tensor(out=pooled[:, g, PADW:], in0=src[:, 2 * PADW:], scalar=1.0 / width,
                                         in1=pool_in[:, g, 2 * PADW:], op0=ALU.mult, op1=ALU.subtract
                                         ).then_inc(sem("pooled"), 1)

            conv_taps, done = taps(), 0
            for j, kind in enumerate(IN2_STEPS):
                c = chunk_of(IN2_STEPS, j)
                out = {"a": tiles[c % 2][:, :], "s": sig[:, c % 2, :], "p": pool_in[:, c, PADW:]}[kind]
                dve.wait_ge(unit_done, U_IN2 + j + 1)
                dve.tensor_tensor(out, proj[j % 3][:, :], rstd[:, :], ALU.mult).then_inc(sem("in2_taken"), 1)
                if kind == "s":
                    dve.wait_ge(sem("glu_sigmoid"), c + 1)
                    dve.scalar_tensor_tensor(out=glu[:, c, TAPS - 1:], in0=tiles[c % 2][:, :],
                                             scalar=v("b_in_2", c), in1=sig[:, c % 2, :],
                                             op0=ALU.add, op1=ALU.mult).then_inc(sem("glu_done"), 1)
                    dve.wait_ge(sem("glu_done"), c + 1)
                ready = sum(len(DVE_TAPS[i]) for i in range(sum(k == "s" for k in IN2_STEPS[:j + 1])))
                step_taps = DVE_STEP_TAPS
                if kind == "p" and c:
                    windows(c - 1)
                    step_taps = DVE_WINDOW_TAPS
                for _ in range(min(step_taps, ready - done)):
                    next(conv_taps)
                    done += 1
            windows(3)
            total = sum(len(t) for t in DVE_TAPS.values())
            while done < total - DVE_LAST_TAPS:
                next(conv_taps)
                done += 1
            for g in range(4):
                dve.wait_ge(sem("mixed_high"), g + 1)
                dve.tensor_tensor(xl[:, 4 + g, :], ymix[:, 4 + g, :], xh[:, 4 + g, :].bitcast(F32), ALU.subtract
                                  ).then_inc(sem("mixed_low"), 1)
            for _ in conv_taps:
                pass
            for c in PE_TAPS:
                dve.wait_ge(sem("taps_gathered"), 1)
                dve.tensor_tensor(conv[:, c, :], conv[:, c, :], bank[0][:, :], ALU.add).then_inc(sem("conv_done"), 1)
            for c in POOL_TAPS:
                dve.wait_ge(sem("tap_added"), N_POOL_TAPS - 1)
                dve.tensor_tensor(conv[:, c, :], conv[:, c, :], conv_pool[:, :], ALU.add
                                  ).then_inc(sem("conv_done"), 1)
            dve.wait_ge(sem("conv_done"), 4)
            dve.wait_ge(sem("ln_summed"), 1)
            own(dve.tensor_scalar(ln_mean, bank[0][:, :], 1.0 / (4 * P), None, ALU.mult))

            def add_ln_square(c):
                dve.wait_ge(sem("ln_square"), c + 1)
                dve.tensor_tensor(ln_sq[0], ln_sq[0], ln_sq[c], ALU.add).then_inc(sem("ln_squares_added"), 1)
                dve.wait_ge(sem("ln_squares_added"), c)

            for c in range(4):
                dve.tensor_tensor(conv[:, c, :], conv[:, c, :], ln_mean, ALU.subtract
                                  ).then_inc(sem("centred"), 1)
                if c >= 2:
                    add_ln_square(c - 1)
            add_ln_square(3)
            inverse("ln")
            dve.wait_ge(sem("norm_spread"), nth("ln"))
            for c in range(4):
                dve.wait_ge(sem("centred"), c + 1)
                dve.scalar_tensor_tensor(out=ymix[:, c, :], in0=conv[:, c, :], scalar=v("ln_g_2", c),
                                         in1=bank[0][:, :], op0=ALU.mult, op1=ALU.mult
                                         ).then_inc(sem("ln_scaled"), 1)
            for c in range(4):
                dve.wait_ge(sem("mixed_high"), 4 + c + 1)
                dve.tensor_tensor(xl[:, c, :], ymix[:, c, :], xh[:, c, :].bitcast(F32), ALU.subtract
                                  ).then_inc(sem("mixed_low"), 1)
            feed("ffn3", "g_ffn_2", "wo2", U_GU3 - 1, 1.0)
            factor("ffn3")
            gate_up("g3", U_GU3)
            feed("final", None, "g3", UNITS - 1, 1.0, parts=False)
            total_squares("final")
            inverse("final")
            dve.wait_ge(sem("norm_spread"), nth("final"))
            for m in range(DK):
                dve.scalar_tensor_tensor(out=out_t[:, m, :], in0=h[:, m, :], scalar=v("g_final_2", m),
                                         in1=bank[5][:, :], op0=ALU.mult, op1=ALU.mult
                                         ).then_inc(sem("out_ready"), 1)



def column_units(w):
    n = w.shape[1] // P
    return w.reshape(DK, P, n, P).transpose(2, 1, 0, 3).reshape(n, P, DK * P)


def row_units(w):
    return w.reshape(-1, P, D)


def gate_up_units(gate, up):
    g, u = column_units(gate), column_units(up)
    return np.stack([g, u], axis=1).reshape(-1, P, DK * P)


def mixed_units(w):
    b = w.reshape(DK, P, DK, P).transpose(0, 2, 1, 3)
    pools = np.stack([b[k, m] for k, m in POOL_HALF]).reshape(4, DK, P, P).transpose(0, 2, 1, 3)
    return np.concatenate([pools.reshape(4, P, DK * P), row_units(w[:BW])])


def in_units(w, w_mem):
    sizes = (BW, BW, BW, HEADS, BW, HD, HD, BW, HD, HEADS, BW, 3 * D)
    fq, fk, fv, ff, dq, dk, dv, iq, ik, iw, mq, g = np.split(w, np.cumsum(sizes)[:-1], axis=1)
    pad = np.zeros((D, P - HD - 2 * HEADS), w.dtype)
    cols = {"ik": np.concatenate([ik, ff, iw, pad], axis=1), "dk": np.concatenate([dk, dv], axis=1),
            "iq": iq, "fq": fq, "fk": fk, "fv": fv, "dq": dq, "mq": mq, "km": w_mem[:, :BW], "vm": w_mem[:, BW:]}
    units = {k: column_units(x) for k, x in cols.items()}
    steps = [units[k][IN_STEPS[:j].count(k)] for j, k in enumerate(IN_STEPS)]
    return np.concatenate([np.stack(steps), column_units(g)])


def branch_units(w):
    b = w.reshape(3, BK, P, DK, P).transpose(3, 0, 1, 2, 4).reshape(-1, P, P)
    return b.reshape(N_BR, DK, P, P).transpose(0, 2, 1, 3).reshape(N_BR, P, DK * P)


def pair_units(w):
    u = column_units(w)
    order = [x for c in range(4) for x in (c, 4 + c)] + [8, 9, 10, 11]
    return u[order]


def by_chunk(x):
    return np.ascontiguousarray(x.T.reshape(DK, P, -1).transpose(1, 0, 2))


def vectors(a):
    out = np.zeros((P, NV), np.float32)

    def put(name, cols):
        o, n = VEC_COLS[name]
        out[:, o:o + n] = cols

    for name in ("ffn1_norm", "mix_norm", "mem_norm", "ffn2_norm", "g_mix_2", "g_ffn_2"):
        put(name, a[name][0].reshape(-1, P).T)
    put("g_final_2", a["g_final_2"].reshape(-1, P).T)
    for name in ("fox_q_norm", "fox_k_norm", "dsa_q_norm", "dsa_k_norm"):
        put(name, np.tile(a[name][0], 2)[:, None])
    for name in ("mem_q_norm", "mem_k_norm"):
        put(name, a[name][0][:, None])
    put("b_forget", np.broadcast_to(a["b_forget"][0], (P, HEADS)))
    for name in ("b_in_2", "b_dw_2", "ln_g_2", "ln_b_2", "s_pool_2"):
        put(name, a[name][0].reshape(-1, P).T)
    put("w_dw_2", a["w_dw_2"][0].reshape(TAPS, 4, P).transpose(2, 1, 0).reshape(P, 4 * TAPS))
    put("inv_freq", np.tile(inverse_frequencies(), 4)[:, None])
    t = np.arange(PADW)
    put("pool_inv", np.broadcast_to(np.concatenate([1.0 / np.minimum(t + 1, w) for w in WINDOWS]), (P, 4 * PADW)))
    return out


def inverse_frequencies():
    return np.float32(10000.0) ** (-np.arange(0, HD, 2, dtype=np.float32) / np.float32(HD))


def constants():
    i = np.arange(P)
    ident = np.eye(P, dtype=np.float32)
    by_head = (i[:, None] // HD == i[None, :] // HD).astype(np.float32)
    mask = np.zeros((P, S), np.float32)
    mask[:, S - P:] = np.where(i[None, :] <= i[:, None], 0.0, MASKED)
    tri = np.ones((P, S), np.float32)
    tri[:, :P] = i[:, None] <= i[None, :]
    return {"identity": ident, "ones": np.ones((P, P), np.float32), "ones_by_head": by_head,
            "causal_mask": mask, "triangle": tri}


def kernel(**inputs):
    import concourse.bacc as bacc
    from concourse.bass_utils import run_bass_kernel_spmd as run

    a = {k: np.asarray(x) for k, x in inputs.items()}
    stream = np.concatenate([
        gate_up_units(a["ffn1_w_gate"][0], a["ffn1_w_up"][0]), row_units(a["ffn1_w_down"][0]),
        in_units(a["w_in"][0], a["w_mem_kv"][0]), branch_units(a["w_branch"][0]), row_units(a["w_out"][0]),
        gate_up_units(a["ffn2_w_gate"][0], a["ffn2_w_up"][0]), row_units(a["ffn2_w_down"][0]),
        pair_units(a["w_in_2"][0]), mixed_units(a["w_out_2"][0]),
        gate_up_units(a["w_gate_2"][0], a["w_up_2"][0]), row_units(a["w_down_2"][0]),
    ])
    arrays = {
        "weights": np.ascontiguousarray(stream),
        "x_t": by_chunk(a["x"][0]),
        "mem_t": by_chunk(a["mem"][0]),
        "positions": np.ascontiguousarray(np.broadcast_to(a["positions"], (P, S))),
        "pool_weights": np.ascontiguousarray(a["w_pool_2"][0].transpose(1, 0, 2)),
        "vectors": vectors(a),
        **constants(),
    }
    nc = bacc.Bacc("TRN2", target_bir_lowering=False, num_devices=1)
    T = {n: nc.dram_tensor(n, x.shape, mybir.dt.from_np(x.dtype), kind="ExternalInput").ap()
         for n, x in arrays.items()}
    T["out_t"] = nc.dram_tensor("out_t", (P, DK, S), F32, kind="ExternalOutput").ap()
    T["forget_sums"] = nc.dram_tensor("forget_sums", (HEADS, S), F32, kind="Internal").ap()
    build(nc, T)
    r = run(nc, [arrays], core_ids=[0])
    got = r.results[0]["out_t"]
    return np.ascontiguousarray(got.transpose(2, 1, 0).reshape(1, S, D))
```
